# Optimizing a Trainium2 kernel written in Bass

```python
import jax
import jax.numpy as jnp
from jax import lax
import numpy as np

D_MODEL = 1024
BATCH = 1
SEQ = 256
DEPTH = 2

GRID_W = 64
CTX_LEN = 256
HEAD_DIM = 64
RW_HEADS = 8
RW_DIM = RW_HEADS * HEAD_DIM
LORA_W = 64
LORA_A = 64
LORA_V = 32
LORA_G = 128
ATT_HEADS = 8
KV_HEADS = 2
GROUP = ATT_HEADS // KV_HEADS
ATT_DIM = ATT_HEADS * HEAD_DIM
KV_DIM = KV_HEADS * HEAD_DIM
WINDOW = 128
BLOCK_Q = 128
SPAN = BLOCK_Q + 2 * WINDOW
ATT_SCALE = HEAD_DIM ** -0.5
ROPE_THETA = 10000.0
RW_IN = 3 * RW_DIM + LORA_W + LORA_A + LORA_G
ATT_IN = ATT_DIM + 2 * KV_DIM
N_IN = RW_IN + ATT_IN + 2 * D_MODEL
RW_SPLITS = [RW_DIM, 2 * RW_DIM, 3 * RW_DIM, 3 * RW_DIM + LORA_W, 3 * RW_DIM + LORA_W + LORA_A]
D_FF = 2816
N_EXPERTS = 8
TOP_K = 2
D_FF_EXPERT = 3584
N_DENSE = (DEPTH + 1) // 2
N_MOE = DEPTH // 2
N_VRES = DEPTH - 1
RMS_EPS = 1e-6
GN_EPS = 64e-5
NEG_INF = -1e30

kernel_name = 'hybrid_rwkv7_swa_moe_dit_block'

def rms_norm(x, g, eps=RMS_EPS):
    xf = x.astype(jnp.float32)
    y = xf * lax.rsqrt(jnp.mean(xf * xf, axis=-1, keepdims=True) + eps)
    return (y * g.astype(jnp.float32)).astype(x.dtype)

def modulate(h, shift, scale):
    return h * (1 + scale) + shift

def token_shift(p, mu):
    prev = jnp.pad(p, ((0, 0), (1, 0), (0, 0)))[:, :-1]
    nxt = jnp.pad(p, ((0, 0), (0, 1), (0, 0)))[:, 1:]
    return p + mu[0] * (prev - p) + mu[1] * (nxt - p)

def axial_rope(n_tokens):
    rows = n_tokens // GRID_W
    row = jnp.repeat(jnp.arange(rows, dtype=jnp.float32), GRID_W)
    col = jnp.tile(jnp.arange(GRID_W, dtype=jnp.float32), rows)
    half = HEAD_DIM // 2
    inv_freq = ROPE_THETA ** (-jnp.arange(0, half, 2, dtype=jnp.float32) / half)
    ar = row[:, None] * inv_freq
    ac = col[:, None] * inv_freq
    ang = jnp.concatenate([ar, ar, ac, ac], axis=-1)
    return jnp.cos(ang)[:, None, :], jnp.sin(ang)[:, None, :]

def apply_rope(u, cos, sin):
    uf = u.astype(jnp.float32)
    r1, r2, c1, c2 = jnp.split(uf, 4, axis=-1)
    rot = jnp.concatenate([-r2, r1, -c2, c1], axis=-1)
    return (uf * cos + rot * sin).astype(u.dtype)

def orient(u):
    return jnp.stack([u[0], jnp.flip(u[1], axis=1)])

def rwkv_branch(p, h, v_first, state0, lp, vres, emit):
    f32 = jnp.float32
    B, T, _ = p.shape
    r, k, v, w_lo, a_lo, g_lo = jnp.split(p, RW_SPLITS, axis=-1)
    w_pre = lp['w0'][:, None, None, :] + jnp.einsum('btl,dlc->dbtc', jnp.tanh(w_lo), lp['w_decay_up'])
    decay = jnp.exp(-jnp.exp(-jax.nn.softplus(-w_pre.astype(f32)) - 0.5))
    iclr = jax.nn.sigmoid(lp['a0'][:, None, None, :] + jnp.einsum('btl,dlc->dbtc', a_lo, lp['w_iclr_up']))
    if vres is None:
        v_first = v
    else:
        v0, v_down, v_up = vres
        v = v + (v_first - v) * jax.nn.sigmoid(v0 + (h @ v_down) @ v_up)

    def heads(u):
        return u.reshape(u.shape[:-1] + (RW_HEADS, HEAD_DIM))

    kk = heads(k * lp['k_k']).astype(f32)
    kk = kk * lax.rsqrt(jnp.sum(kk * kk, axis=-1, keepdims=True) + 1e-12)
    k_h = heads(k[None] * (1 + (iclr - 1) * lp['k_a'])).astype(f32)
    r_h = heads(r).astype(f32)
    v_h = heads(v).astype(f32)

    def both(u):
        return jnp.broadcast_to(u[None], (2,) + u.shape)

    xs = (orient(both(r_h)), orient(heads(decay)), orient(k_h), orient(both(v_h)),
          orient(both(kk)), orient(heads(iclr).astype(f32)))
    xs = tuple(jnp.moveaxis(u, 2, 0) for u in xs)

    def step(S, inp):
        r_t, w_t, k_t, v_t, kk_t, a_t = inp
        s_kk = jnp.einsum('dbhij,dbhj->dbhi', S, kk_t)
        S = S * w_t[..., None, :] - s_kk[..., None] * (kk_t * a_t)[..., None, :] + v_t[..., None] * k_t[..., None, :]
        return S, (jnp.einsum('dbhij,dbhj->dbhi', S, r_t) if emit else None)

    state, ys = lax.scan(step, state0, xs)
    if not emit:
        return state, v_first, None
    ys = orient(jnp.moveaxis(ys, 0, 2))
    y = ys[0] + ys[1]
    mu = jnp.mean(y, axis=-1, keepdims=True)
    var = jnp.mean(jnp.square(y - mu), axis=-1, keepdims=True)
    yn = ((y - mu) * lax.rsqrt(var + GN_EPS)).reshape(B, T, RW_DIM)
    yn = yn * lp['lnx_g'].astype(f32) + lp['lnx_b'].astype(f32)
    coef = jnp.sum(r_h * (k_h[0] + k_h[1]) * lp['r_k'].astype(f32), axis=-1, keepdims=True)
    y = yn + (coef * v_h).reshape(B, T, RW_DIM)
    g = jax.nn.sigmoid(g_lo) @ lp['w_gate_up']
    return state, v_first, y.astype(p.dtype) * g

def window_attention(q, k, v, kc, vc, sink):
    B, T = q.shape[:2]
    n_blocks = T // BLOCK_Q
    kp = jnp.pad(k, ((0, 0), (WINDOW, WINDOW), (0, 0), (0, 0)))
    vp = jnp.pad(v, ((0, 0), (WINDOW, WINDOW), (0, 0), (0, 0)))
    qb = jnp.swapaxes(q.reshape(B, n_blocks, BLOCK_Q, KV_HEADS, GROUP, HEAD_DIM), 0, 1)
    rel = jnp.arange(SPAN)[None, :] - WINDOW - jnp.arange(BLOCK_Q)[:, None]
    in_window = jnp.abs(rel) <= WINDOW
    sink_col = jnp.broadcast_to(sink.reshape(1, KV_HEADS, GROUP, 1, 1).astype(jnp.float32),
                                (B, KV_HEADS, GROUP, BLOCK_Q, 1))

    def block(args):
        qblk, i = args
        start = i * BLOCK_Q
        kb = lax.dynamic_slice_in_dim(kp, start, SPAN, axis=1)
        vb = lax.dynamic_slice_in_dim(vp, start, SPAN, axis=1)
        kpos = start - WINDOW + jnp.arange(SPAN)
        ok = in_window & ((kpos >= 0) & (kpos < T))[None, :]
        s_loc = jnp.einsum('bqhgd,bkhd->bhgqk', qblk, kb).astype(jnp.float32) * ATT_SCALE
        s_loc = jnp.where(ok, s_loc, NEG_INF)
        s_ctx = jnp.einsum('bqhgd,bchd->bhgqc', qblk, kc).astype(jnp.float32) * ATT_SCALE
        pr = jax.nn.softmax(jnp.concatenate([s_loc, s_ctx, sink_col], axis=-1), axis=-1).astype(v.dtype)
        o = jnp.einsum('bhgqk,bkhd->bqhgd', pr[..., :SPAN], vb)
        return o + jnp.einsum('bhgqc,bchd->bqhgd', pr[..., SPAN:-1], vc)

    o = lax.map(block, (qb, jnp.arange(n_blocks)))
    return jnp.swapaxes(o, 0, 1).reshape(B, T, ATT_DIM)

def context_attention(qc, kc, vc, sink):
    B, C = qc.shape[:2]
    qg = qc.reshape(B, C, KV_HEADS, GROUP, HEAD_DIM)
    s = jnp.einsum('bqhgd,bkhd->bhgqk', qg, kc).astype(jnp.float32) * ATT_SCALE
    sink_col = jnp.broadcast_to(sink.reshape(1, KV_HEADS, GROUP, 1, 1).astype(jnp.float32), s.shape[:-1] + (1,))
    pr = jax.nn.softmax(jnp.concatenate([s, sink_col], axis=-1), axis=-1)[..., :C].astype(vc.dtype)
    return jnp.einsum('bhgqk,bkhd->bqhgd', pr, vc).reshape(B, C, ATT_DIM)

def merge(y_rw, y_att, gates, lp):
    g_rw, g_att = jnp.split(gates, 2, axis=-1)
    m = jax.nn.sigmoid(g_rw) * (y_rw @ lp['w_br_rwkv']) + jax.nn.sigmoid(g_att) * (y_att @ lp['w_br_attn'])
    return m @ lp['w_out']

def mixer(h, hc, vf_lat, vf_ctx, lp, vres, cos, sin, last):
    p = h @ lp['w_in']
    pc = hc @ lp['w_in']
    rw, att, gates = jnp.split(p, [RW_IN, RW_IN + ATT_IN], axis=-1)
    rwc, attc, gatesc = jnp.split(pc, [RW_IN, RW_IN + ATT_IN], axis=-1)
    rw = token_shift(rw, lp['tshift'])
    rwc = token_shift(rwc, lp['tshift'])
    state0 = jnp.zeros((2, hc.shape[0], RW_HEADS, HEAD_DIM, HEAD_DIM), jnp.float32)
    s_ctx, vf_ctx, y_rw_c = rwkv_branch(rwc, hc, vf_ctx, state0, lp, vres, emit=not last)
    _, vf_lat, y_rw = rwkv_branch(rw, h, vf_lat, s_ctx, lp, vres, emit=True)

    def split_qkv(a):
        B, T = a.shape[:2]
        q, k, v = jnp.split(a, [ATT_DIM, ATT_DIM + KV_DIM], axis=-1)
        return (q.reshape(B, T, ATT_HEADS, HEAD_DIM),
                rms_norm(k.reshape(B, T, KV_HEADS, HEAD_DIM), lp['k_norm']),
                v.reshape(B, T, KV_HEADS, HEAD_DIM))

    q, k, v = split_qkv(att)
    q = apply_rope(rms_norm(q, lp['q_norm']), cos, sin)
    k = apply_rope(k, cos, sin)
    qc, kc, vc = split_qkv(attc)
    y_att = window_attention(q, k, v, kc, vc, lp['sink'])
    y = merge(y_rw, y_att, gates, lp)
    if last:
        return y, None, vf_lat, vf_ctx
    y_att_c = context_attention(rms_norm(qc, lp['q_norm']), kc, vc, lp['sink'])
    yc = merge(y_rw_c, y_att_c, gatesc, lp)
    return y, yc, vf_lat, vf_ctx

def swiglu(h, wg, wu, wd):
    return (jax.nn.silu(h @ wg) * (h @ wu)) @ wd

def moe_swiglu(h, router, wg, wu, wd):
    logits = (h @ router).astype(jnp.float32)
    top_v, top_i = lax.top_k(logits, TOP_K)
    w = jax.nn.softmax(top_v, axis=-1).astype(h.dtype)
    out = jnp.zeros_like(h)
    for e in range(N_EXPERTS):
        we = jnp.sum(jnp.where(top_i == e, w, 0.0), axis=-1, keepdims=True)
        out = out + we * swiglu(h, wg[e], wu[e], wd[e])
    return out

def setup_inputs(seed: int = 0) -> dict:
    key = jax.random.key(seed)
    keys = iter(jax.random.split(key, 40))

    def nrm(shape, s):
        return jax.random.normal(next(keys), shape, jnp.float32) * s

    def uni(shape, lo, hi):
        return jax.random.uniform(next(keys), shape, jnp.float32, lo, hi)

    D = D_MODEL
    return {
        'x': nrm((BATCH, SEQ, D), 1.0),
        'c': nrm((BATCH, D), 1.0),
        'ctx': nrm((BATCH, CTX_LEN, D), 1.0),
        'c_ctx': nrm((D,), 1.0),
        'norm1': 1.0 + nrm((DEPTH, D), 0.02),
        'norm2': 1.0 + nrm((DEPTH, D), 0.02),
        'w_mod': nrm((DEPTH, D, 6 * D), 0.5 * D ** -0.5),
        'b_mod': nrm((DEPTH, 6 * D), 0.02),
        'w_in': nrm((DEPTH, D, N_IN), D ** -0.5),
        'tshift': uni((DEPTH, 2, RW_IN), 0.0, 0.5),
        'w0': uni((DEPTH, 2, RW_DIM), -6.0, -1.0),
        'w_decay_up': nrm((DEPTH, 2, LORA_W, RW_DIM), 0.1 * LORA_W ** -0.5),
        'a0': nrm((DEPTH, 2, RW_DIM), 0.1),
        'w_iclr_up': nrm((DEPTH, 2, LORA_A, RW_DIM), 0.3 * LORA_A ** -0.5),
        'v0': 1.0 + nrm((N_VRES, RW_DIM), 0.1),
        'w_vres_down': nrm((N_VRES, D, LORA_V), D ** -0.5),
        'w_vres_up': nrm((N_VRES, LORA_V, RW_DIM), 0.3 * LORA_V ** -0.5),
        'w_gate_up': nrm((DEPTH, LORA_G, RW_DIM), LORA_G ** -0.5),
        'k_k': 0.85 + nrm((DEPTH, RW_DIM), 0.02),
        'k_a': 1.0 + nrm((DEPTH, RW_DIM), 0.02),
        'r_k': nrm((DEPTH, RW_HEADS, HEAD_DIM), 0.1),
        'lnx_g': 1.0 + nrm((DEPTH, RW_DIM), 0.02),
        'lnx_b': nrm((DEPTH, RW_DIM), 0.02),
        'q_norm': 1.0 + nrm((DEPTH, HEAD_DIM), 0.02),
        'k_norm': 1.0 + nrm((DEPTH, HEAD_DIM), 0.02),
        'sink': nrm((DEPTH, ATT_HEADS), 0.5),
        'w_br_rwkv': nrm((DEPTH, RW_DIM, D), RW_DIM ** -0.5),
        'w_br_attn': nrm((DEPTH, ATT_DIM, D), ATT_DIM ** -0.5),
        'w_out': nrm((DEPTH, D, D), D ** -0.5),
        'ffn_gate': nrm((N_DENSE, D, D_FF), D ** -0.5),
        'ffn_up': nrm((N_DENSE, D, D_FF), D ** -0.5),
        'ffn_down': nrm((N_DENSE, D_FF, D), D_FF ** -0.5),
        'router': nrm((N_MOE, D, N_EXPERTS), D ** -0.5),
        'moe_gate': nrm((N_MOE, N_EXPERTS, D, D_FF_EXPERT), D ** -0.5),
        'moe_up': nrm((N_MOE, N_EXPERTS, D, D_FF_EXPERT), D ** -0.5),
        'moe_down': nrm((N_MOE, N_EXPERTS, D_FF_EXPERT, D), D_FF_EXPERT ** -0.5),
    }

def reference(x, c, ctx, c_ctx, norm1, norm2, w_mod, b_mod, w_in, tshift, w0, w_decay_up, a0, w_iclr_up,
              v0, w_vres_down, w_vres_up, w_gate_up, k_k, k_a, r_k, lnx_g, lnx_b, q_norm, k_norm, sink,
              w_br_rwkv, w_br_attn, w_out, ffn_gate, ffn_up, ffn_down, router, moe_gate, moe_up, moe_down):
    cos, sin = axial_rope(x.shape[1])
    xc = ctx
    vf_lat = None
    vf_ctx = None
    for layer in range(DEPTH):
        last = layer == DEPTH - 1
        mod_l = jax.nn.silu(c) @ w_mod[layer] + b_mod[layer]
        mod_c = jax.nn.silu(c_ctx) @ w_mod[layer] + b_mod[layer]
        sh1, sc1, g1, sh2, sc2, g2 = jnp.split(mod_l[:, None, :], 6, axis=-1)
        csh1, csc1, cg1, csh2, csc2, cg2 = jnp.split(mod_c, 6, axis=-1)
        lp = {
            'w_in': w_in[layer], 'tshift': tshift[layer], 'w0': w0[layer], 'w_decay_up': w_decay_up[layer],
            'a0': a0[layer], 'w_iclr_up': w_iclr_up[layer], 'w_gate_up': w_gate_up[layer],
            'k_k': k_k[layer], 'k_a': k_a[layer], 'r_k': r_k[layer], 'lnx_g': lnx_g[layer], 'lnx_b': lnx_b[layer],
            'q_norm': q_norm[layer], 'k_norm': k_norm[layer], 'sink': sink[layer],
            'w_br_rwkv': w_br_rwkv[layer], 'w_br_attn': w_br_attn[layer], 'w_out': w_out[layer],
        }
        vres = None if layer == 0 else (v0[layer - 1], w_vres_down[layer - 1], w_vres_up[layer - 1])
        h = modulate(rms_norm(x, norm1[layer]), sh1, sc1)
        hc = modulate(rms_norm(xc, norm1[layer]), csh1, csc1)
        y, yc, vf_lat, vf_ctx = mixer(h, hc, vf_lat, vf_ctx, lp, vres, cos, sin, last)
        x = x + g1 * y
        if not last:
            xc = xc + cg1 * yc
        if layer % 2 == 0:
            i = layer // 2
            ffn = lambda u, i=i: swiglu(u, ffn_gate[i], ffn_up[i], ffn_down[i])
        else:
            i = layer // 2
            ffn = lambda u, i=i: moe_swiglu(u, router[i], moe_gate[i], moe_up[i], moe_down[i])
        x = x + g2 * ffn(modulate(rms_norm(x, norm2[layer]), sh2, sc2))
        if not last:
            xc = xc + cg2 * ffn(modulate(rms_norm(xc, norm2[layer]), csh2, csc2))
    return x


_drawn_inputs = setup_inputs


def setup_inputs(seed=0):
    import zlib

    import numpy as np

    out = dict(_drawn_inputs(seed))
    spreads = {}
    factors = {'norm1': 8.0,
     'norm2': 34.272,
     'w_decay_up': 64.0,
     'a0': 6.367,
     'w_iclr_up': 2.981,
     'v0': 8.0,
     'w_vres_down': 5.545,
     'w_vres_up': 4.935,
     'k_k': 200.0,
     'k_a': 6.16,
     'lnx_g': 200.0,
     'lnx_b': 200.0,
     'q_norm': 50.199,
     'k_norm': 60.053,
     'sink': 8.0,
     'w0': 3.068}
    for name, (base, spread) in spreads.items():
        noise = np.random.default_rng([zlib.crc32(name.encode()), seed]).standard_normal(out[name].shape)
        drawn = base * np.exp(spread * noise) if base else spread * noise
        out[name] = jnp.asarray(drawn.astype(out[name].dtype))
    for name, factor in factors.items():
        out[name] = (out[name] * factor).astype(out[name].dtype)
    return out
```

```python
import numpy as np
import concourse.bass as bass
from concourse import mybir
from contextlib import ExitStack

P = 128
D = 1024
KT = D // P
CTX = LAT = 256
T = CTX + LAT
HD = 64
CH = 64
NCH = CTX // CH
RW = 512
NB = RW // P
FF = 2816
NFF = FF // P
FE = 3584
EC = FE // 512
NE = 8
NJ = NE + 3
SLOT = 4096
NS = 3
L = 2
EPS = 1e-6
GN_EPS = 64e-5
DECAY = -float(np.exp(-0.5))

PV = {}
_n = 0
for _name, _w in [("norm1", 8), ("norm2", 8), ("bmod", 48), ("mu0", 14), ("mu1", 14), ("w0", 8), ("a0", 8),
                  ("kk", 4), ("ka", 4), ("rk", 4), ("lg", 4), ("lb", 4), ("v0", 4), ("qn", 1), ("kn", 1), ("sink", 8)]:
    PV[_name] = (_n, _n + _w)
    _n += _w
NPV = _n

CO = {}
_n = 0
for _name, _w in [("ident", 128), ("strict", 256), ("incl", 256), ("level", 6 * 2 * 128), ("cos", 256), ("sin", 256), ("rot", 128),
                  ("bones", 128), ("bmean", 128), ("mean", 128), ("ones", 128), ("before", 128), ("amask", 512),
                  ("iota", 128), ("sel", 2), ("zero", 512)]:
    CO[_name] = (_n, _n + _w)
    _n += _w
NCO = _n


def constants():
    c = np.zeros((P, NCO), np.float32)

    def put(name, a):
        c[:, CO[name][0]:CO[name][1]] = np.asarray(a, np.float32).reshape(P, -1)

    i = np.arange(P)
    s, t = i[:, None], i[None, :]
    bd = (s // 64) == (t // 64)
    fwd = bd & (s < t)
    put("ident", np.eye(P))
    put("strict", np.stack([fwd, fwd.T], 1))
    put("incl", np.stack([fwd | (s == t), fwd.T | (s == t)], 1))
    lv = []
    for k in range(6):
        n = 1 << k
        m = (s // (2 * n) == t // (2 * n)) & ((s // n) % 2 == 0) & ((t // n) % 2 == 1)
        lv.append(np.stack([m, m.T], 1))
    put("level", np.stack(lv, 1))
    half = HD // 2
    inv = np.float32(10000.0) ** (-np.arange(0, half, 2, dtype=np.float32) / np.float32(half))
    tok = np.arange(LAT)
    ar = (tok // 64).astype(np.float32)[:, None] * inv
    ac = (tok % 64).astype(np.float32)[:, None] * inv
    ang = np.concatenate([ar, ar, ac, ac], -1).astype(np.float32)
    put("cos", np.tile(np.cos(ang).T, (2, 1)))
    put("sin", np.tile(np.sin(ang).T, (2, 1)))
    rot = np.zeros((P, P))
    for h in range(2):
        for q in range(2):
            for j in range(16):
                a = 64 * h + 32 * q + j
                rot[a + 16, a] = -1.0
                rot[a, a + 16] = 1.0
    put("rot", rot)
    put("bones", bd)
    put("bmean", bd / 64.0)
    put("mean", np.full((P, P), 1.0 / D))
    put("ones", np.ones((P, P)))
    put("before", s < t)
    q = np.arange(P)[:, None]
    am = [np.where(np.abs(np.arange(LAT)[None] - (q + P * b)) <= 128, 0.0, -1e30) for b in range(2)]
    put("amask", np.stack(am, 1))
    put("iota", np.tile(np.arange(P), (P, 1)))
    sel = np.zeros((P, 2))
    for g in range(4):
        for v in range(2):
            sel[32 * g + v, v] = 1.0
    put("sel", sel)
    return c


class Signal:

    def __init__(self, sem, name, book):
        self.sem, self.name, self.book, self.n = sem, name, book, 0

    def done(self, ins, *key):
        ins.then_inc(self.sem, 1)
        self.n += 1
        if key:
            self.book[(self.name,) + key] = self.n

    def count(self, *key):
        return self.book.get((self.name,) + key, 1)


def build(nc, a, out, x_mid, vf_mid, book, stop=None):
    f32 = mybir.dt.float32
    i32 = mybir.dt.int32
    u32 = mybir.dt.uint32
    ALU = mybir.AluOpType
    ACT = mybir.ActivationFunctionType
    AX = mybir.AxisListType
    ctx = ExitStack()
    with ctx:
        def sb(name, n, dt=f32):
            return ctx.enter_context(nc.sbuf_tensor(name, [P, n], dt))

        ring = sb("ring", NS * SLOT)
        hbuf = sb("hbuf", KT * T)
        proj = sb("proj", 14 * T)
        yatt = sb("yatt", NB * T)
        mw = sb("mw", 2304)
        co = sb("co", NCO)
        pv = sb("pv", NPV)
        modt = sb("modt", 96)
        nrm = sb("nrm", 32)
        rstd = sb("rstd", 512)
        csil = sb("csil", KT * 32)
        work = sb("work", 19200)
        ctrl = sb("ctrl", 16, i32)
        small = sb("small", 256)
        tidx = sb("tidx", 16, u32)
        bank = [ctx.enter_context(nc.psum_tensor(f"bank{i}", [P, 512], f32)) for i in range(8)]

        def sem(name):
            return ctx.enter_context(nc.semaphore(name))

        pe_done = Signal(sem("pe_done"), "pe", book)
        act_done = Signal(sem("act_done"), "act", book)
        dve_done = Signal(sem("dve_done"), "dve", book)
        pool_done = Signal(sem("pool_done"), "pool", book)
        ring_used = sem("ring_used")
        ring_full = [sem(f"ring_full{i}") for i in range(NS)]
        const_loaded, par_loaded, mw_loaded, x_loaded, c_loaded = (sem(n) for n in
                                                                   ("const_loaded", "par_loaded", "mw_loaded", "x_loaded", "c_loaded"))
        x_stored, vf_stored, vf_loaded, out_stored = (sem(n) for n in ("x_stored", "vf_stored", "vf_loaded", "out_stored"))
        X = {n: sem("moe_" + n) for n in ("key", "key2", "gat", "xg", "gt", "gtc", "silu", "act", "tr", "trc", "yc", "sc", "add")}

        def C(name, *dims):
            v = co[:, CO[name][0]:CO[name][1]]
            return v if not dims else v.rearrange("p (a b) -> p a b", a=dims[0])

        ident = C("ident")
        strict = C("strict", 2)
        incl = C("incl", 2)
        level = C("level", 12)
        amask = C("amask", 2)

        def V(name, i=0):
            o = PV[name][0] + i
            return pv[:, o:o + 1]

        def wk(off, n, *dims):
            v = work[:, off:off + n]
            if len(dims) == 1:
                return v.rearrange("p (a b) -> p a b", a=dims[0])
            if len(dims) == 2:
                return v.rearrange("p (a b c) -> p a b c", a=dims[0], b=dims[1])
            return v

        h3 = hbuf[:, :].rearrange("p (k t) -> p k t", k=KT)
        pr = proj[:, :].rearrange("p (k t) -> p k t", k=14)
        ya = yatt[:, :].rearrange("p (k t) -> p k t", k=NB)
        x3 = wk(0, 4096, KT)
        modv = modt[:, :].rearrange("p (m v) -> p m v", v=2)

        items = []
        for l in range(L):
            items += [(a["w_mod"][l, n], 4096) for n in range(12)]
            items += [(a["w_in"][l, n], 4096) for n in range(5)]
            items += [(a["w_mrg"][l, n], 3072) for n in range(8)]
            items += [(a["w_out"][l, n], 4096) for n in range(2)]
            if l == 0:
                items += [(a["w_gu"][n], 4096) for n in range(11)]
                items += [(a["w_dn"][n], 2816) for n in range(8)]
        items += [(a["router"], 64)]
        N_STATIC = len(items)
        order = [("g", 0), ("u", 0)]
        for c in range(1, EC):
            order += [("g", c), ("u", c), ("d", c - 1)]
        order += [("d", EC - 1)]
        place_of = {x: i for i, x in enumerate(order)}

        def used_count(kind, c, j):
            return j * (3 * EC) + (NS + place_of[kind, c] + 1)

        taken = [0]

        def slot(i):
            return ring[:, (i % NS) * SLOT:(i % NS + 1) * SLOT]

        QK = 3072
        att = wk(0, QK, 6)

        o = 0
        J = {}
        for n_, w_ in [("kr", 1024), ("kapbd", 1024), ("Kbd", 1024), ("Bbd", 1024), ("vbd", 512), ("LkT", 1024), ("QkT", 1024),
                       ("U", 1024), ("QbT", 1024), ("N", 1024), ("Um", 1024), ("Ktok", 1024), ("Btok", 1024), ("Vtok", 512),
                       ("lw", 512), ("Lc", 512), ("Pc", 512), ("Qc", 512), ("ic", 512), ("kh", 512), ("bb", 512),
                       ("kk", 256), ("kkt", 256), ("cv", 256), ("sq", 256), ("rs", 256), ("Y", 256), ("S", 256), ("Rs", 256), ("Un", 256)]:
            J[n_] = (o, w_)
            o += w_
        assert o <= 19200, o

        def j3(name, n):
            return wk(*J[name], n)

        j_kr = wk(*J["kr"], 8, 2)
        j_kap, j_K, j_B = j3("kapbd", 8), j3("Kbd", 8), j3("Bbd", 8)
        j_M, j_X = j_K, j_B
        j_v, j_Lk, j_Qk, j_U, j_Qb, j_N, j_Um = j3("vbd", 4), j3("LkT", 8), j3("QkT", 8), j3("U", 8), j3("QbT", 8), j3("N", 8), j3("Um", 8)
        j_Kt, j_Bt, j_Vt = j3("Ktok", 8), j3("Btok", 8), j3("Vtok", 4)
        j_lw, j_L, j_P, j_Q, j_ic, j_kh, j_bb = (j3(n, 2) for n in ("lw", "Lc", "Pc", "Qc", "ic", "kh", "bb"))
        j_kk, j_kkt, j_cv, j_sq, j_rs, j_Y = (wk(*J[n]) for n in ("kk", "kkt", "cv", "sq", "rs", "Y"))
        j_S, j_R, j_Un = (j3(n, 2) for n in ("S", "Rs", "Un"))
        mup = mw[:, 0:1024].rearrange("p (d c) -> p d c", d=2)
        mgate = mw[:, 1024:1536]
        mvd = mw[:, 1536:1792].rearrange("p (k c) -> p k c", k=KT)
        mvu = mw[:, 1792:2304]

        jobs = [(l, b, q) for l in range(L) for b in range(NB) for q in range(2)]

        def cols(l):
            return (0, T) if l == 0 else (CTX, LAT)

        o = 4096
        M = {}
        for n_, w_ in [("htok", 2048), ("xg", 1024), ("sil", 1024), ("hid", 1024), ("hT", 1024), ("G", 256), ("Gw", 256), ("GwT", 256),
                       ("y", 1024), ("rt", 512)]:
            M[n_] = (o, w_)
            o += w_
        m_htok = wk(*M["htok"], 2)
        m_xg = wk(*M["xg"], KT)
        m_sil = wk(*M["sil"], 2)
        m_hid = wk(*M["hid"], 2)
        m_hT = wk(*M["hT"], 2, 4)
        m_G = wk(*M["G"], 2)
        m_Gw = wk(*M["Gw"], 2)
        m_GwT = wk(*M["GwT"])
        m_y = wk(*M["y"])
        rt = wk(*M["rt"])

        block = ctx.enter_context(nc.Block())

        @block.sync
        def _(sp):
            for i, (src, n) in enumerate(items):
                if i >= NS:
                    sp.wait_ge(pe_done.sem, pe_done.count("item", i - NS))
                sp.dma_start(slot(i)[:, 0:n], src).then_inc(ring_full[i % NS], 16)

            def expert(e, j):
                for m in range(3 * EC):
                    sp.wait_ge(ring_used, j * (3 * EC) + (m + 1))
                    dst = slot(N_STATIC + m)
                    sp.dma_start(dst, a["w_exp"][bass.ds(e, 1), m, :, :].rearrange("e p n -> p (e n)"))\
                      .then_inc(ring_full[(N_STATIC + m) % NS], 16)

            with sp.Fori(0, NE) as j:
                expert(j, j)
            sp.wait_ge(dve_done.sem, dve_done.count("ctrl"))
            more = sp.value_load(ctrl[0:1, NJ:NJ + 1], min_val=0, max_val=3)
            with sp.If(more > 0):
                with sp.Fori(0, more) as j2:
                    r = sp.value_load(ctrl[0:1, bass.ds(j2 + NE, 1)], min_val=0, max_val=NE - 1)
                    expert(r, j2 + NE)
            sp.wait_ge(dve_done.sem, dve_done.count("final"))
            sp.dma_start(out, x3[:, :, CTX:T]).then_inc(out_stored, 16)
            sp.wait_ge(out_stored, 16)

        @block.tensor
        def _(pe):
            seen = {}

            def need(sig, *key):
                n = sig.count(*key)
                if seen.get(sig.name, 0) < n:
                    seen[sig.name] = n
                    pe.wait_ge(sig.sem, n)

            def mm(o_, lhsT, rhs, start=True, stop=True, **kw):
                return pe.matmul(o_, lhsT, rhs, start=start, stop=stop, **kw)

            def next_item():
                i = taken[0]
                taken[0] += 1
                pe.wait_ge(ring_full[i % NS], 16 * (i // NS + 1))
                return slot(i)

            def item_done():
                book[("pe", "item", taken[0] - 1)] = pe_done.n

            pe.wait_ge(const_loaded, 16)
            for l in range(L):
                need(act_done, "csil")
                for n in range(12):
                    w = next_item()[:, :].rearrange("p (k c) -> p k c", k=KT)
                    cs3 = csil[:, :].rearrange("p (k c) -> p k c", k=KT)
                    if n >= 2:
                        need(act_done, "modrow", l, n - 2)
                    elif l:
                        need(dve_done, "ffn", 0)
                    b_ = bank[n % 2]
                    for k in range(KT):
                        g = k % 4
                        ins = mm(b_[32 * g:32 * g + 32, :], cs3[:, k, :], w[:, k, :], start=(k < 4), stop=(k >= 4),
                                 tile_position=(0, 32 * g), skip_group_check=True)
                        if k == KT - 1:
                            pe_done.done(ins, "modrow", l, n)
                            item_done()
                    need(act_done, "modrow", l, n)
                    for j in range(4):
                        ins = mm(bank[2][:, 2 * (4 * n + j):2 * (4 * n + j) + 2], wk(0, 6144)[:, 512 * n + 128 * j:512 * n + 128 * j + 128],
                                 C("sel"))
                    pe_done.done(ins, "modt", l, n)
                for k in range(KT):
                    need(act_done, "sq1", l, k)
                    if k == 0:
                        need(act_done, "modrow", l, 11)
                    ins = mm(bank[0][:, :], C("mean"), wk(4096 + 512 * k, 512), start=(k == 0), stop=(k == KT - 1))
                pe_done.done(ins, "ms1", l)
                need(act_done, "h1", l)
                need(dve_done, "h1", l)
                for n in range(5):
                    w = next_item()[:, :].rearrange("p (j k c) -> p j k c", j=4, k=KT)
                    for j in range(4):
                        bi = 4 * n + j
                        if bi >= 4:
                            need(act_done, "proj", l, bi - 4)
                        else:
                            need(act_done, "rms1", l)
                            need(dve_done, "modt", l)
                        for k in range(KT):
                            ins = mm(bank[bi % 4][:, :], w[:, j, k, :], h3[:, k, :], start=(k == 0), stop=(k == KT - 1))
                        pe_done.done(ins, "proj", l, bi)
                    item_done()
                for i in range(5):
                    need(act_done, "qsq", l, i)
                    if i >= 2:
                        need(act_done, "qrms", l, i - 2)
                    pe_done.done(mm(bank[i % 2][:, :], C("bmean"), wk(3072 + 512 * (i % 2), 512)), "qms", l, i)
                    need(dve_done, "qn", l, i)
                    if i >= 2:
                        need(dve_done, "qrot", l, i - 2)
                    pe_done.done(mm(bank[2 + i % 2][:, 0:256], C("rot"), att[:, i, CTX:T]), "qrot", l, i)
                for tb in range(4):
                    if tb == 0:
                        need(act_done, "proj", l, 19)
                        need(dve_done, "qrot", l, 4)
                    ins = pe.transpose(bank[4][:, 128 * tb:128 * tb + 128], att[:, 5, 128 * tb:128 * tb + 128], ident)
                pe_done.done(ins, "vtok", l)
                need(act_done, "vtok", l)
                vt = wk(4096, 512, 4)
                units = [(b, hh, qb) for b in range(NB) for hh in range(2) for qb in ((0, 1, 2, 3) if l == 0 else (2, 3))]

                def pv_unit(u):
                    b, hh, qb = units[u]
                    nk = 2 if qb < 2 else 4
                    need(dve_done, "prob", l, u)
                    if u >= 2:
                        need(act_done, "pT", l, u - 2)
                    for kb in range(nk):
                        ins = pe.transpose(bank[2 + u % 2][:, 128 * kb:128 * kb + 128], wk(5632 + 512 * (u % 2), 512)[:, 128 * kb:128 * kb + 128], ident)
                    pe_done.done(ins, "pT", l, u)
                    need(act_done, "pT", l, u)
                    if (hh, qb) == units[0][1:] and b >= 2:
                        need(act_done, "yatt", l, b - 2)
                    for kb in range(nk):
                        ins = mm(bank[4 + b % 2][64 * hh:64 * hh + 64, 128 * qb:128 * qb + 128], vt[:, kb, 64 * hh:64 * hh + 64],
                                 wk(6656 + 512 * (u % 2), 512)[:, 128 * kb:128 * kb + 128], start=(kb == 0), stop=(kb == nk - 1))
                    pe_done.done(ins, "pv", l, u)

                for u, (b, hh, qb) in enumerate(units):
                    nk = 2 if qb < 2 else 4
                    if u >= 2:
                        need(dve_done, "scored", l, u - 2)
                    pe_done.done(mm(bank[u % 2][:, 0:128 * nk], att[64 * hh:64 * hh + 64, b, 128 * qb:128 * qb + 128],
                                    att[64 * hh:64 * hh + 64, 4, 0:128 * nk]), "score", l, u)
                    if u >= 1:
                        pv_unit(u - 1)
                pv_unit(len(units) - 1)
                if l == 1:
                    pe.wait_ge(mw_loaded, 32)
                    need(act_done, "yatt", 1, NB - 1)
                    for k in range(KT):
                        ins = mm(bank[7][0:32, :], mvd[:, k, :], h3[:, k, :], start=(k == 0), stop=(k == KT - 1))
                    pe_done.done(ins, "vdown")
                    need(act_done, "vdown")
                    for b in range(NB):
                        if b >= 1:
                            need(act_done, "vsig", b - 1)
                        pe_done.done(mm(bank[7][:, :], mvu[0:32, P * b:P * b + P], rstd[0:32, :]), "vup", b)
                pe.wait_ge(mw_loaded, 16 * (l + 1))
                for jl, b, q in [x for x in jobs if x[0] == l]:
                    jn = (l, b, q)
                    q0 = 256 * q
                    emit = not (l == 1 and q == 0)
                    for d in range(2):
                        if d == 0:
                            need(dve_done, "jobready", *jn)
                        mm(bank[0][:, 256 * d:256 * d + 256], mup[0:64, d, P * b:P * b + P], pr[0:64, 0, q0:q0 + 256])
                    for d in range(2):
                        ins = mm(bank[1][:, 256 * d:256 * d + 256], mup[64:128, d, P * b:P * b + P], pr[64:128, 0, q0:q0 + 256])
                    pe_done.done(ins, "lora", *jn)
                    need(act_done, "kksq", *jn)
                    pe_done.done(mm(bank[2][:, 0:256], C("bones"), j_sq), "kkss", *jn)
                    need(dve_done, "coef", *jn)
                    pe_done.done(mm(bank[2][:, 256:512], C("bones"), j_rs), "coef", *jn)
                    need(dve_done, "cv", *jn)
                    need(dve_done, "bd", *jn)
                    need(act_done, "bd", *jn)
                    for w_, src in enumerate((j_K, j_B)):
                        for s in range(8):
                            rhs = j_kr[:, s, :, :].rearrange("p a b -> p (a b)").unsqueeze(1).to_broadcast([P, 2, 128])
                            ins = mm(bank[4 * w_ + s // 2][:, 256 * (s % 2):256 * (s % 2) + 256], src[:, s, :], rhs)
                            if s % 2:
                                pe_done.done(ins, "gram", *jn, w_, s // 2)
                    n = 0
                    for src, m_ in ((j_K, 8), (j_B, 8), (j_v, 4)):
                        for g in range(m_ // 4):
                            if n < 2:
                                need(dve_done, "gram", *jn, 1, 2 + n)
                            else:
                                need(act_done, "tok", *jn, n - 2)
                            for s in range(4):
                                ins = pe.transpose(bank[6 + n % 2][:, 128 * s:128 * s + 128], src[:, 4 * g + s, :], ident)
                            pe_done.done(ins, "tok", *jn, n)
                            n += 1
                    for lv in range(6):
                        for d in range(2):
                            need(pool_done, "um", *jn, lv, d)
                            if lv == 0:
                                for c in range(4):
                                    ins = pe.transpose(bank[3 * d][:, 128 * c:128 * c + 128], j_Um[:, 4 * d + c, :], ident)
                                pe_done.done(ins, "x", *jn, lv, d)
                                continue
                            need(dve_done, "mn", *jn, lv - 1, d)
                            for c in range(4):
                                s = 4 * d + c
                                ins = mm(bank[3 * d][:, 128 * c:128 * c + 128], j_Um[:, s, :], j_M[:, s, :])
                            pe_done.done(ins, "x", *jn, lv, d)
                        if lv == 0:
                            continue
                        for d in range(2):
                            need(act_done, "x", *jn, lv, d)
                            for c in range(4):
                                s = 4 * d + c
                                if lv < 5:
                                    mm(bank[3 * d + 1][:, 128 * c:128 * c + 128], j_N[:, s, :], j_X[:, s, :])
                            for c in range(4):
                                s = 4 * d + c
                                ins = mm(bank[3 * d + 2][:, 128 * c:128 * c + 128], j_X[:, s, :], j_N[:, s, :])
                            pe_done.done(ins, "mn", *jn, lv, d)
                    for c in range(NCH):
                        for d in range(2):
                            ch = c if d == 0 else NCH - 1 - c
                            s = 4 * d + ch
                            if c == 0:
                                need(dve_done, "mn", *jn, 5, d)
                                need(act_done, "tok", *jn, 4)
                            else:
                                need(dve_done, "state", *jn, c - 1, d)
                            mm(bank[3 * d][:, 0:128], j_Lk[:, s, :], j_Vt[:, ch, :], stop=False)
                            pe_done.done(mm(bank[3 * d][:, 0:128], j_kap[:, s, :], j_S[:, d, :], start=False), "R", *jn, c, d)
                            if emit:
                                r_dup = j_kr[:, s, 1, :].unsqueeze(1).to_broadcast([P, 2, CH])
                                yb = bank[6][:, 128 * ch:128 * ch + 128]
                                mm(yb, j_S[:, d, :], r_dup, start=(c == 0 and d == 0), stop=False, skip_group_check=True)
                                mm(yb, j_Vt[:, ch, :], j_Qk[:, s, :], start=False, stop=False, skip_group_check=True)
                        for d in range(2):
                            ch = c if d == 0 else NCH - 1 - c
                            s = 4 * d + ch
                            need(act_done, "R", *jn, c, d)
                            pe_done.done(mm(bank[3 * d][:, 128:256], j_N[:, s, :], j_R[:, d, :]), "U", *jn, c, d)
                        for d in range(2):
                            ch = c if d == 0 else NCH - 1 - c
                            s = 4 * d + ch
                            need(dve_done, "U", *jn, c, d)
                            mm(bank[3 * d][:, 256:384], j_Kt[:, s, :], j_Vt[:, ch, :], stop=False)
                            pe_done.done(mm(bank[3 * d][:, 256:384], j_Bt[:, s, :], j_Un[:, d, :], start=False), "state", *jn, c, d)
                            if emit:
                                ins = mm(bank[6][:, 128 * ch:128 * ch + 128], j_Un[:, d, :], j_Qb[:, s, :], start=False,
                                         stop=(c == NCH - 1 and d == 1), skip_group_check=True)
                                pe_done.done(ins, "y", *jn, c, d)
                    if emit:
                        need(act_done, "y", *jn)
                        pe_done.done(mm(bank[7][:, 0:256], C("bmean"), j_Y), "ymean", *jn)
                        need(act_done, "ysq", *jn)
                        pe_done.done(mm(bank[7][:, 256:512], C("bmean"), j_sq), "yvar", *jn)
                        pe_done.done(mm(bank[5][:, 0:256], mgate[:, P * b:P * b + P], pr[:, 1, q0:q0 + 256]), "gate", *jn)
                c0, nt = cols(l)
                for n in range(KT):
                    w = next_item()
                    wg = w[:, 0:2048].rearrange("p (g k c) -> p g k c", g=2, k=KT)
                    wb = w[:, 2048:3072].rearrange("p (g k c) -> p g k c", g=2, k=NB)
                    st = 4 * (n % 2)
                    if n == 0:
                        need(dve_done, "yrw", l)
                        need(act_done, "yatt", l, NB - 1)
                    if n >= 2:
                        need(dve_done, "merge", l, n - 2)
                    for g in range(2):
                        for k in range(KT):
                            ins = mm(bank[st + g][:, 0:nt], wg[:, g, k, :], h3[:, k, c0:c0 + nt], start=(k == 0), stop=(k == KT - 1))
                        pe_done.done(ins, "mg", l, n, g)
                    for g in range(2):
                        for k in range(NB):
                            rhs = pr[:, 2 + 3 * k, c0:c0 + nt] if g == 0 else ya[:, k, c0:c0 + nt]
                            ins = mm(bank[st + 2 + g][:, 0:nt], wb[:, g, k, :], rhs, start=(k == 0), stop=(k == NB - 1))
                        pe_done.done(ins, "mb", l, n, g)
                    item_done()
                for n in range(2):
                    w = next_item()[:, :].rearrange("p (j k c) -> p j k c", j=4, k=KT)
                    for j in range(4):
                        di = 4 * n + j
                        if di == 0:
                            need(dve_done, "merge", l, KT - 1)
                        if di >= 2:
                            need(dve_done, "res1", l, di - 2)
                        for k in range(KT):
                            ins = mm(bank[di % 2][:, 0:nt], w[:, j, k, :], wk(4096 + 512 * k, nt), start=(k == 0), stop=(k == KT - 1))
                            if l == 1 and di == 4 and k == 0:
                                ins.then_inc(ring_used, 1)
                        pe_done.done(ins, "wo", l, di)
                    item_done()
                for k in range(KT):
                    need(act_done, "sq2", l, k)
                    if k == 0:
                        need(dve_done, "res1", l, KT - 1)
                    ins = mm(bank[0][:, 0:nt], C("mean"), wk(8192 + 512 * k, nt), start=(k == 0), stop=(k == KT - 1))
                    if l == 1 and k == 0:
                        ins.then_inc(ring_used, 1)
                pe_done.done(ins, "ms2", l)
                need(act_done, "h2", l)
                need(dve_done, "h2", l)
                if l == 0:
                    for n in range(11):
                        w = next_item()[:, :].rearrange("p (j k c) -> p j k c", j=4, k=KT)
                        for j in range(4):
                            f, g = 2 * n + j // 2, j % 2
                            if f >= 2 and g == 0:
                                need(dve_done, "hff", f - 2)
                            for k in range(KT):
                                ins = mm(bank[2 * (f % 2) + g][:, :], w[:, j, k, :], h3[:, k, :], start=(k == 0), stop=(k == KT - 1))
                            pe_done.done(ins, "gu", f, g)
                        item_done()
                    for n in range(KT):
                        w = next_item()[:, 0:2816].rearrange("p (k c) -> p k c", k=NFF)
                        if n == 0:
                            need(dve_done, "hff", NFF - 1)
                        if n >= 2:
                            need(dve_done, "res2", n - 2)
                        for k in range(NFF):
                            ins = mm(bank[n % 2][:, :], w[:, k, :], wk(4096 + 512 * k, 512), start=(k == 0), stop=(k == NFF - 1))
                        pe_done.done(ins, "dn", n)
                        item_done()
                else:
                    w = next_item()[:, 0:64].rearrange("p (k e) -> p k e", k=KT)
                    for tb in range(2):
                        for k in range(KT):
                            ins = mm(bank[1][:, 8 * tb:8 * tb + 8], h3[:, k, CTX + P * tb:CTX + P * tb + P], w[:, k, :],
                                     start=(k == 0), stop=(k == KT - 1))
                    pe_done.done(ins, "logits")
                    for tb in range(2):
                        for g in range(2):
                            for k in range(4):
                                ins = pe.transpose(bank[4 + 2 * tb + g][:, 128 * k:128 * k + 128],
                                                   h3[:, 4 * g + k, CTX + P * tb:CTX + P * tb + P], ident)
                                if (tb, g, k) == (0, 0, 0):
                                    ins.then_inc(ring_used, 1)
                            pe_done.done(ins, "htok", tb, g)
                    need(dve_done, "mask")
                    rmask = rt[:, 0:16].rearrange("p (t e) -> p t e", t=2)
                    mm(bank[0][:, 0:8], C("before"), rmask[:, 0, :])
                    mm(bank[0][:, 8:16], C("before"), rmask[:, 1, :], stop=False)
                    mm(bank[0][:, 8:16], C("ones"), rmask[:, 0, :], start=False)
                    mm(bank[0][:, 16:24], C("ones"), rmask[:, 0, :], stop=False)
                    pe_done.done(mm(bank[0][:, 16:24], C("ones"), rmask[:, 1, :], start=False), "rank")
                    need(dve_done, "ctrl")
                    need(act_done, "htok", 1, 1)
                    jobs_here = pe.value_load(ctrl[0:1, NJ + 1:NJ + 2], min_val=NE, max_val=NJ)
                    with pe.Fori(0, jobs_here) as j:
                        pe.wait_ge(X["key"], j + 1)
                        for g in range(2):
                            for k in range(4):
                                for tb in range(2):
                                    ins = mm(bank[6 + g][:, 128 * k:128 * k + 128], m_htok[:, tb, P * (4 * g + k):P * (4 * g + k) + P],
                                             m_G[:, tb, :], start=(tb == 0), stop=(tb == 1))
                            ins.then_inc(X["gat"], 1)
                        for tb in range(2):
                            ins = pe.transpose(bank[4][:, 128 * tb:128 * tb + 128], m_Gw[:, tb, :], ident)
                        ins.then_inc(X["gt"], 1)
                        pe.wait_ge(X["xg"], j * 2 + 2)
                        pe.wait_ge(X["gtc"], j + 1)

                        def item(kind, c):
                            m = N_STATIC + place_of[kind, c]
                            before = len(range(m % NS, m, NS))
                            pe.wait_ge(ring_full[m % NS], j * (16 * EC) + 16 * (before + 1))
                            return slot(m)

                        def down(c):
                            pe.wait_ge(X["act"], j * EC + (c + 1))
                            if c >= 1:
                                pe.wait_ge(X["trc"], j * EC + c)
                            for k in range(4):
                                ins = pe.transpose(bank[4][:, 128 * k:128 * k + 128], m_hid[:, c % 2, 128 * k:128 * k + 128], ident)
                            ins.then_inc(X["tr"], 1)
                            w = item("d", c)
                            pe.wait_ge(X["trc"], j * EC + (c + 1))
                            for k in range(4):
                                for g in range(2):
                                    ins = mm([bank[5], bank[7]][g][:, :], m_hT[:, c % 2, k, :], w[:, 1024 * k + 512 * g:1024 * k + 512 * g + 512],
                                             start=(c == 0 and k == 0), stop=(c == EC - 1 and k == 3))
                            ins.then_inc(ring_used, 1)

                        for c in range(EC):
                            for g in range(2):
                                w = item("gu"[g], c)
                                if c >= 2:
                                    pe.wait_ge(X["act"], j * EC + (c - 1))
                                for k in range(KT):
                                    ins = mm(bank[2 * (c % 2) + g][:, :], m_xg[:, k, :], w[:, 512 * k:512 * k + 512], start=(k == 0), stop=(k == KT - 1))
                                ins.then_inc(ring_used, 1)
                            if c >= 1:
                                down(c - 1)
                        down(EC - 1)
                        pe.wait_ge(X["yc"], j * 2 + 2)
                        for g in range(4):
                            for k in range(2):
                                kk_ = 2 * g + k
                                ins = mm(bank[g][:, 256 * k:256 * k + 256], m_y[:, P * kk_:P * kk_ + P], m_GwT)
                            ins.then_inc(X["sc"], 1)
                        pe.wait_ge(X["add"], j * 4 + 4)

        @block.scalar
        def _(act):
            seen = {}

            def need(sig, *key):
                n = sig.count(*key)
                if seen.get(sig.name, 0) < n:
                    seen[sig.name] = n
                    act.wait_ge(sig.sem, n)

            def af(o_, i_, f, *key, **kw):
                act_done.done(act.activation(o_, i_, f, **kw), *key)

            def own():
                act.wait_ge(act_done.sem, act_done.n)

            act.dma_start(co[:, :], a["consts"]).then_inc(const_loaded, 16)
            act.dma_start(rstd[:, 0:16], a["c"]).then_inc(c_loaded, 16)
            need(dve_done, "eps")
            act.wait_ge(c_loaded, 16)
            cs3 = csil[:, :].rearrange("p (k c) -> p k c", k=KT)
            af(cs3[:, :, 0:2], rstd[:, 0:16].rearrange("p (k c) -> p k c", k=KT), ACT.Silu, "csil")
            for l in range(L):
                if l:
                    need(dve_done, "ffn", 0)
                    need(pe_done, "vup", 3) if False else None
                act.dma_start(pv[:, :], a["pv"][l]).then_inc(par_loaded, 16)
                act.dma_start(mw[:, :], a["mw"][l]).then_inc(mw_loaded, 16)
                for n in range(12):
                    need(pe_done, "modrow", l, n)
                    af(wk(512 * n, 512), bank[n % 2][:, :], ACT.Copy, "modrow", l, n)
                need(pe_done, "modt", l, 11)
                act.dma_start(x3, a["x"] if l == 0 else x_mid).then_inc(x_loaded, 16)
                act.wait_ge(x_loaded, 16 * (2 * l + 1))
                for k in range(KT):
                    af(wk(4096 + 512 * k, 512), x3[:, k, :], ACT.Square, "sq1", l, k)
                need(pe_done, "ms1", l)
                af(rstd[:, :], bank[0][:, :], ACT.Sqrt, "rms1", l, bias=small[:, 240:241])
                need(dve_done, "xr1", l)
                for k in range(KT):
                    af(h3[:, k, 0:CTX], h3[:, k, 0:CTX], ACT.Identity, *(("h1", l) if k == KT - 1 else ()),
                       scale=nrm[:, 2 * k + 1:2 * k + 2], bias=modv[:, k, 1:2])
                need(dve_done, "h1", l)
                for bi in range(20):
                    need(pe_done, "proj", l, bi)
                    if 2 <= bi < 8:
                        src = [4, 5, 0, 1, 2, 3][bi - 2]
                        af(att[:, src, :], bank[bi % 4][:, :], ACT.Copy, "proj", l, bi)
                    else:
                        m = bi if bi < 2 else bi - 6
                        if m >= 2:
                            need(dve_done, "shift", l, m - 2)
                        pad = wk(8192 + 516 * (m % 2), 516, 2)
                        af(pad[:, :, 1:257], bank[bi % 4][:, :].rearrange("p (a b) -> p a b", a=2), ACT.Copy, "proj", l, bi)
                need(dve_done, "shift", l, 1)
                own()
                af(pr[0:64, 0, :], pr[0:64, 0, :], ACT.Tanh, "tanh", l)
                af(pr[:, 1, :], pr[:, 1, :], ACT.Sigmoid, "glo", l)
                def q_rms(i):
                    need(pe_done, "qms", l, i)
                    if i >= 1:
                        need(dve_done, "qn", l, i - 1)
                    af(rstd[:, :], bank[i % 2][:, :], ACT.Sqrt, "qrms", l, i, bias=small[:, 240:241])

                for i in range(5):
                    own()
                    if i >= 2:
                        need(pe_done, "qms", l, i - 2)
                    if i >= 1:
                        q_rms(i - 1)
                    af(wk(3072 + 512 * (i % 2), 512), att[:, i, :], ACT.Square, "qsq", l, i)
                q_rms(4)
                need(pe_done, "vtok", l)
                af(wk(4096, 512), bank[4][:, :], ACT.Copy, "vtok", l)
                units = [(b, hh, qb) for b in range(NB) for hh in range(2) for qb in ((0, 1, 2, 3) if l == 0 else (2, 3))]

                def after(u):
                    b, hh, qb = units[u]
                    nk = 2 if qb < 2 else 4
                    need(pe_done, "pT", l, u)
                    if u >= 2:
                        need(pe_done, "pv", l, u - 2)
                    af(wk(6656 + 512 * (u % 2), 512)[:, 0:128 * nk], bank[2 + u % 2][:, 0:128 * nk], ACT.Copy, "pT", l, u)
                    if u + 1 == len(units) or units[u + 1][0] != b:
                        need(pe_done, "pv", l, u)
                        c0_, n_ = cols(l)
                        af(ya[:, b, c0_:c0_ + n_], bank[4 + b % 2][:, c0_:c0_ + n_], ACT.Copy, "yatt", l, b)

                for u, (b, hh, qb) in enumerate(units):
                    nk = 2 if qb < 2 else 4
                    need(dve_done, "max", l, u)
                    sm = small[:, 8 * (u % 2):8 * (u % 2) + 8]
                    if u >= 2:
                        need(pe_done, "pT", l, u - 2)
                    p_ = wk(5632 + 512 * (u % 2), 512)[:, 0:128 * nk]
                    s_ = wk(4608 + 512 * (u % 2), 512)[:, 0:128 * nk]
                    af(p_, s_, ACT.Exp, bias=sm[:, 1:2], accum_out=sm[:, 2:3])
                    hq = b + 4 * hh
                    af(sm[:, 3:4], V("sink", hq), ACT.Exp, "exp", l, u, bias=sm[:, 1:2])
                    if u >= 1:
                        after(u - 1)
                after(len(units) - 1)
                if l == 1:
                    need(pe_done, "vdown")
                    af(rstd[0:32, :], bank[7][0:32, :], ACT.Copy, "vdown")
                    for b in range(NB):
                        need(pe_done, "vup", b)
                        if b >= 2:
                            need(dve_done, "vres", b - 2)
                        af(wk(512 * (b % 2), 512), bank[7][:, :], ACT.Sigmoid, "vsig", b, bias=V("v0", b))
                for jl, b, q in [x for x in jobs if x[0] == l]:
                    jn = (l, b, q)
                    emit = not (l == 1 and q == 0)
                    need(dve_done, "kkt", *jn)
                    af(j_sq, j_kkt, ACT.Square, "kksq", *jn)
                    need(pe_done, "kkss", *jn)
                    af(j_rs, bank[2][:, 0:256], ACT.Sqrt, "kkrms", *jn, bias=small[:, 241:242])
                    need(pe_done, "lora", *jn)
                    for d in range(2):
                        af(j_lw[:, d, :], bank[0][:, 256 * d:256 * d + 256], ACT.Sigmoid, bias=V("w0", 4 * d + b))
                    for d in range(2):
                        af(j_ic[:, d, :], bank[1][:, 256 * d:256 * d + 256], ACT.Sigmoid, "sig", *jn, bias=V("a0", 4 * d + b))
                    need(dve_done, "cum", *jn)
                    af(wk(*J["Pc"]), wk(*J["Lc"]), ACT.Exp)
                    af(wk(*J["Qc"]), wk(*J["Lc"]), ACT.Exp, "decay", *jn, scale=-1.0)
                    need(dve_done, "kr", *jn)
                    for h in range(2):
                        af(j_kap[64 * h:64 * h + 64, :, 64 * h:64 * h + 64], j_kr[64 * h:64 * h + 64, :, 0, :], ACT.Copy)
                    for h in range(2):
                        af(j_v[64 * h:64 * h + 64, :, 64 * h:64 * h + 64],
                           pr[64 * h:64 * h + 64, 4 + 3 * b, 256 * q:256 * q + 256].rearrange("p (c t) -> p c t", c=4), ACT.Copy, "bd", *jn)
                    for n in range(5):
                        need(pe_done, "tok", *jn, n)
                        dst = [j_Kt[:, 0:4, :], j_Kt[:, 4:8, :], j_Bt[:, 0:4, :], j_Bt[:, 4:8, :], j_Vt[:, :, :]][n]
                        af(dst, bank[6 + n % 2][:, :].rearrange("p (a b) -> p a b", a=4), ACT.Copy, "tok", *jn, n)
                    for lv in range(1, 6):
                        for d in range(2):
                            need(pe_done, "x", *jn, lv, d)
                            af(j_X[:, 4 * d:4 * d + 4, :], bank[3 * d][:, :].rearrange("p (a b) -> p a b", a=4), ACT.Copy, "x", *jn, lv, d)
                    for c in range(NCH):
                        for d in range(2):
                            need(pe_done, "R", *jn, c, d)
                            af(j_R[:, d, :], bank[3 * d][:, 0:128], ACT.Copy, "R", *jn, c, d)
                    if emit:
                        need(pe_done, "y", *jn, NCH - 1, 1)
                        for h in range(2):
                            af(j_Y[64 * h:64 * h + 64, :].rearrange("p (c t) -> p c t", c=4),
                               bank[6][64 * h:64 * h + 64, :].rearrange("p (c h t) -> p c h t", c=4, h=2)[:, :, h, :], ACT.Copy, "y", *jn)
                        need(dve_done, "yc", *jn)
                        af(j_sq, j_Y, ACT.Square, "ysq", *jn)
                        need(pe_done, "yvar", *jn)
                        af(j_rs, bank[7][:, 256:512], ACT.Sqrt, "yrms", *jn, bias=small[:, 242:243])
                c0, nt = cols(l)
                for n in range(KT):
                    st = 4 * (n % 2)
                    if n == 0:
                        need(dve_done, "yrw", l)
                    if n >= 2:
                        need(dve_done, "merge", l, n - 2)
                    for g in range(2):
                        need(pe_done, "mg", l, n, g)
                        af(wk(8192 + 512 * (2 * (n % 2) + g), nt), bank[st + g][:, 0:nt], ACT.Sigmoid, "mg", l, n, g)
                    if n == 0:
                        act.dma_start(x3, a["x"] if l == 0 else x_mid).then_inc(x_loaded, 16)
                need(dve_done, "merge", l, KT - 1)
                for k in range(KT):
                    need(dve_done, "res1", l, k)
                    af(wk(8192 + 512 * k, nt), x3[:, k, c0:c0 + nt], ACT.Square, "sq2", l, k)
                need(pe_done, "ms2", l)
                af(rstd[:, 0:nt], bank[0][:, 0:nt], ACT.Sqrt, "rms2", l, bias=small[:, 240:241])
                need(dve_done, "xr2", l)
                for k in range(KT):
                    v = 1 if l == 0 else 0
                    c_ = 0 if l == 0 else CTX
                    n_ = CTX if l == 0 else 128
                    af(h3[:, k, c_:c_ + n_], h3[:, k, c_:c_ + n_], ACT.Identity, *(("h2", l) if k == KT - 1 else ()),
                       scale=nrm[:, 16 + 2 * k + v:17 + 2 * k + v], bias=modv[:, 24 + k, v:v + 1])
                if l == 0:
                    for f in range(NFF):
                        need(pe_done, "gu", f, 0)
                        if f >= 2:
                            need(dve_done, "hff", f - 2)
                        af(wk(15360 + 512 * (f % 2), 512), bank[2 * (f % 2)][:, :], ACT.Silu, "silu", f)
                    need(dve_done, "ffn", 0)
                    act.dma_start(x_mid, x3).then_inc(x_stored, 16)
                    act.wait_ge(x_stored, 16)
                else:
                    for tb in range(2):
                        for g in range(2):
                            need(pe_done, "htok", tb, g)
                            af(m_htok[:, tb, 512 * g:512 * g + 512], bank[4 + 2 * tb + g][:, :], ACT.Copy, "htok", tb, g)
                    need(dve_done, "gap")
                    af(small[:, 32:34], small[:, 34:36], ACT.Exp, "gap")
                    need(dve_done, "ctrl")
                    jobs_here = act.value_load(ctrl[0:1, NJ + 1:NJ + 2], min_val=NE, max_val=NJ)
                    with act.Fori(0, jobs_here) as j:
                        for g in range(2):
                            act.wait_ge(X["gat"], j * 2 + (g + 1))
                            act.activation(m_xg[:, 4 * g:4 * g + 4, :], bank[6 + g][:, :].rearrange("p (a b) -> p a b", a=4),
                                           ACT.Copy).then_inc(X["xg"], 1)
                        act.wait_ge(X["gt"], j + 1)
                        act.activation(m_GwT, bank[4][:, 0:256], ACT.Copy).then_inc(X["gtc"], 1)

                        def tr(c):
                            act.wait_ge(X["tr"], j * EC + (c + 1))
                            act.activation(m_hT[:, c % 2, :, :], bank[4][:, :].rearrange("p (a b) -> p a b", a=4), ACT.Copy)\
                               .then_inc(X["trc"], 1)

                        for c in range(EC):
                            act.wait_ge(ring_used, used_count("g", c, j))
                            if c >= 2:
                                act.wait_ge(X["act"], j * EC + (c - 1))
                            act.activation(m_sil[:, c % 2, :], bank[2 * (c % 2)][:, :], ACT.Silu).then_inc(X["silu"], 1)
                            if c >= 1:
                                tr(c - 1)
                        tr(EC - 1)
                        act.wait_ge(ring_used, used_count("d", EC - 1, j))
                        for g in range(2):
                            act.activation(m_y[:, 512 * g:512 * g + 512], [bank[5], bank[7]][g][:, :], ACT.Copy).then_inc(X["yc"], 1)

        @block.vector
        def _(dve):
            seen = {}

            def need(sig, *key):
                n = sig.count(*key)
                if seen.get(sig.name, 0) < n:
                    seen[sig.name] = n
                    dve.wait_ge(sig.sem, n)

            def dv(ins, *key, hold=True):
                dve_done.done(ins, *key)
                if hold:
                    dve.wait_ge(dve_done.sem, dve_done.n)

            tt = dve.tensor_tensor
            ts = dve.tensor_scalar
            stt = dve.scalar_tensor_tensor
            dv(dve.memset(csil[:, :], 0.0), "czero")
            for i, e_ in enumerate((EPS, 1e-12, GN_EPS)):
                dv(dve.memset(small[:, 240 + i:241 + i], e_), "eps")
            dve.wait_ge(const_loaded, 16)
            for l in range(L):
                dve.wait_ge(par_loaded, 16 * (l + 1))
                need(pe_done, "modt", l, 11)
                bm = pv[:, PV["bmod"][0]:PV["bmod"][1]].unsqueeze(2).to_broadcast([P, 48, 2])
                dv(tt(modv, bank[2][:, 0:96].rearrange("p (m v) -> p m v", v=2), bm, ALU.add), "modt", l)
                for i, nn in enumerate(("norm1", "norm2")):
                    g_ = pv[:, PV[nn][0]:PV[nn][1]].unsqueeze(2).to_broadcast([P, KT, 2])
                    n3 = nrm[:, 16 * i:16 * i + 16].rearrange("p (k v) -> p k v", v=2)
                    sc_ = modv[:, 24 * i + 8:24 * i + 16, :]
                    dv(tt(n3, sc_, g_, ALU.mult))
                    dv(tt(n3, n3, g_, ALU.add))
                c0m = small[:, 64:78]
                mu0 = pv[:, PV["mu0"][0]:PV["mu0"][1]]
                mu1 = pv[:, PV["mu1"][0]:PV["mu1"][1]]
                dv(tt(c0m, mu0, mu1, ALU.add))
                dv(ts(c0m, c0m, -1.0, 1.0, ALU.mult, ALU.add))
                need(act_done, "rms1", l)
                dv(dve.reciprocal(rstd[:, :], rstd[:, :]))
                dve.wait_ge(x_loaded, 16 * (2 * l + 1))
                dv(tt(h3, x3, rstd[:, :].unsqueeze(1).to_broadcast([P, KT, T]), ALU.mult), "xr1", l)
                for k in range(KT):
                    dv(ts(h3[:, k, CTX:T], h3[:, k, CTX:T], nrm[:, 2 * k:2 * k + 1], modv[:, k, 0:1], ALU.mult, ALU.add),
                       *(("h1", l) if k == KT - 1 else ()), hold=False)
                for i in range(2):
                    pad = wk(8192 + 516 * i, 516, 2)
                    dv(dve.memset(pad[:, :, 0:1], 0.0), hold=False)
                    dv(dve.memset(pad[:, :, 257:258], 0.0))
                for m in range(14):
                    need(act_done, "proj", l, m if m < 2 else m + 6)
                    pad = wk(8192 + 516 * (m % 2), 516, 2)
                    o_ = pr[:, m, :].rearrange("p (a b) -> p a b", a=2)
                    dv(ts(o_, pad[:, :, 1:257], c0m[:, m:m + 1], None, ALU.mult))
                    dv(stt(o_, pad[:, :, 0:256], V("mu0", m), o_, ALU.mult, ALU.add))
                    dv(stt(o_, pad[:, :, 2:258], V("mu1", m), o_, ALU.mult, ALU.add), "shift", l, m)
                for i in range(5):
                    need(act_done, "qrms", l, i)
                    dv(dve.reciprocal(rstd[:, :], rstd[:, :]))
                    dv(stt(att[:, i, :], att[:, i, :], V("qn") if i < 4 else V("kn"), rstd[:, :], ALU.mult, ALU.mult), "qn", l, i)
                    need(pe_done, "qrot", l, i)
                    t_ = wk(9728, 256)
                    dv(tt(t_, bank[2 + i % 2][:, 0:256], C("sin"), ALU.mult))
                    dv(tt(att[:, i, CTX:T], att[:, i, CTX:T], C("cos"), ALU.mult))
                    dv(tt(att[:, i, CTX:T], att[:, i, CTX:T], t_, ALU.add), "qrot", l, i)
                units = [(b, hh, qb) for b in range(NB) for hh in range(2) for qb in ((0, 1, 2, 3) if l == 0 else (2, 3))]

                def finish(u):
                    b, hh, qb = units[u]
                    nk = 2 if qb < 2 else 4
                    sm = small[:, 8 * (u % 2):8 * (u % 2) + 8]
                    need(act_done, "exp", l, u)
                    dv(tt(sm[:, 4:5], sm[:, 2:3], sm[:, 3:4], ALU.add))
                    dv(dve.reciprocal(sm[:, 5:6], sm[:, 4:5]))
                    p_ = wk(5632 + 512 * (u % 2), 512)[:, 0:128 * nk]
                    dv(ts(p_, p_, sm[:, 5:6], None, ALU.mult), "prob", l, u)

                for u, (b, hh, qb) in enumerate(units):
                    nk = 2 if qb < 2 else 4
                    need(pe_done, "score", l, u)
                    sm = small[:, 8 * (u % 2):8 * (u % 2) + 8]
                    s_ = wk(4608 + 512 * (u % 2), 512)
                    dv(ts(s_[:, 0:256], bank[u % 2][:, 0:256], HD ** -0.5, None, ALU.mult), *(("scored", l, u) if nk == 2 else ()))
                    if nk == 4:
                        dv(stt(s_[:, 256:512], bank[u % 2][:, 256:512], HD ** -0.5, amask[:, qb - 2, :], ALU.mult, ALU.add), "scored", l, u)
                    dv(dve.tensor_reduce(sm[:, 0:1], s_[:, 0:128 * nk], AX.X, ALU.max))
                    dv(ts(sm[:, 1:2], sm[:, 0:1], V("sink", b + 4 * hh), -1.0, ALU.max, ALU.mult), "max", l, u)
                    if u >= 1:
                        finish(u - 1)
                finish(len(units) - 1)
                if l == 1:
                    for b in range(NB):
                        need(act_done, "vsig", b)
                        dve.wait_ge(vf_loaded, 16)
                        v_ = pr[:, 4 + 3 * b, :]
                        t_ = wk(1024, 512)
                        dv(tt(t_, wk(2048 + 512 * b, 512), v_, ALU.subtract))
                        dv(tt(t_, t_, wk(512 * (b % 2), 512), ALU.mult))
                        dv(tt(v_, v_, t_, ALU.add), "vres", b)
                need(act_done, "glo", l)
                need(act_done, "yatt", l, NB - 1)
                need(pool_done, "zeroed", l)
                for jl, b, q in [x for x in jobs if x[0] == l]:
                    jn = (l, b, q)
                    emit = not (l == 1 and q == 0)
                    q0 = 256 * q
                    r_, k_, v_ = (pr[:, 2 + 3 * b + i, q0:q0 + 256] for i in range(3))
                    if q == 0:
                        dv(dve.memset(wk(*J["S"]), 0.0))
                    dv(ts(j_kkt, k_, V("kk", b), None, ALU.mult), "jobready", *jn)
                    dve_done.book[("dve", "kkt") + jn] = dve_done.n
                    need(act_done, "sig", *jn)
                    dv(ts(wk(*J["lw"]), wk(*J["lw"]), DECAY, None, ALU.mult))
                    for d in range(2):
                        for c in range(4):
                            o_, i_ = j_L[:, d, CH * c:CH * c + CH], j_lw[:, d, CH * c:CH * c + CH]
                            if d:
                                o_, i_ = o_[:, ::-1], i_[:, ::-1]
                            dv(dve.tensor_tensor_scan(out=o_, data0=i_, data1=i_, initial=0.0, op0=ALU.add, op1=ALU.bypass),
                               *(("cum",) + jn if (d, c) == (1, 3) else ()), hold=(d, c) == (1, 3))
                    need(act_done, "kkrms", *jn)
                    dv(dve.reciprocal(j_rs, j_rs))
                    dv(tt(j_kk, j_kkt, j_rs, ALU.mult))
                    dv(ts(wk(*J["kh"]), wk(*J["ic"]), 1.0, V("ka", b), ALU.subtract, ALU.mult))
                    k2 = k_.unsqueeze(1).to_broadcast([P, 2, 256])
                    dv(stt(j_kh, j_kh, 1.0, k2, ALU.add, ALU.mult))
                    dv(tt(j_rs, j_kh[:, 0, :], j_kh[:, 1, :], ALU.add))
                    dv(stt(j_rs, j_rs, V("rk", b), r_, ALU.mult, ALU.mult), "coef", *jn)
                    dv(tt(j_bb, j_ic, j_kk.unsqueeze(1).to_broadcast([P, 2, 256]), ALU.mult))
                    need(act_done, "decay", *jn)
                    c4 = lambda ap: ap.rearrange("p (c t) -> p c t", c=4)
                    kkc = c4(j_kk)
                    for d in range(2):
                        Pd = c4(j_P[:, d, :])
                        dv(tt(j_kr[:, 4 * d:4 * d + 4, 1, :], c4(r_), Pd, ALU.mult), hold=False)
                        if d == 0:
                            dv(tt(j_kr[:, 0:4, 0, 1:64], kkc[:, :, 1:64], Pd[:, :, 0:63], ALU.mult), hold=False)
                            dv(dve.tensor_copy(j_kr[:, 0:4, 0, 0:1], kkc[:, :, 0:1]), hold=False)
                        else:
                            dv(tt(j_kr[:, 4:8, 0, 0:63], kkc[:, :, 0:63], Pd[:, :, 1:64], ALU.mult), hold=False)
                            dv(dve.tensor_copy(j_kr[:, 4:8, 0, 63:64], kkc[:, :, 63:64]), "kr", *jn)
                    s8 = lambda n_, h: wk(*J[n_])[64 * h:64 * h + 64, :].rearrange("p (s t) -> p s t", s=8)
                    for h in range(2):
                        hs = slice(64 * h, 64 * h + 64)
                        dv(tt(j_K[hs, :, hs], s8("kh", h), s8("Qc", h), ALU.mult), hold=False)
                        dv(tt(j_B[hs, :, hs], s8("bb", h), s8("Qc", h), ALU.mult), *(("bd",) + jn if h else ()))
                    need(pe_done, "coef", *jn)
                    dv(tt(j_cv, bank[2][:, 256:512], v_, ALU.mult), "cv", *jn)
                    for w_ in range(2):
                        for sp_ in range(4):
                            need(pe_done, "gram", *jn, w_, sp_)
                            d = sp_ // 2
                            g5 = bank[4 * w_ + sp_][:, :].rearrange("p (s h r t) -> p s h r t", s=2, h=2, r=2)
                            for r2, (dst, msk) in enumerate(((j_Lk, strict), (j_Qk, incl)) if w_ == 0 else ((j_U, strict), (j_Qb, incl))):
                                if r2 == 1 and not emit:
                                    continue
                                dv(tt(dst[:, 2 * sp_:2 * sp_ + 2, :].rearrange("p s (h t) -> p s h t", h=2), g5[:, :, :, r2, :],
                                      msk[:, d, :].rearrange("p (h t) -> p h t", h=2).unsqueeze(1).to_broadcast([P, 2, 2, 64]), ALU.mult),
                                   "gram", *jn, w_, sp_, hold=False)
                    idb = ident.unsqueeze(1).to_broadcast([P, 4, 128])
                    for lv in range(6):
                        for d in range(2):
                            N_, M_ = j_N[:, 4 * d:4 * d + 4, :], j_M[:, 4 * d:4 * d + 4, :]
                            if lv == 0:
                                need(pool_done, "um", *jn, lv, d)
                                dv(stt(N_, j_Um[:, 4 * d:4 * d + 4, :], -1.0, idb, ALU.mult, ALU.add), hold=False)
                                need(pe_done, "x", *jn, lv, d)
                                need(pe_done, "tok", *jn, 1)
                                dv(stt(M_, bank[3 * d][:, :].rearrange("p (a b) -> p a b", a=4), -1.0, idb, ALU.mult, ALU.add), "mn", *jn, lv, d)
                            else:
                                need(pe_done, "mn", *jn, lv, d)
                                if lv < 5:
                                    dv(tt(M_, M_, bank[3 * d + 1][:, :].rearrange("p (a b) -> p a b", a=4), ALU.subtract), hold=False)
                                dv(tt(N_, N_, bank[3 * d + 2][:, :].rearrange("p (a b) -> p a b", a=4), ALU.subtract), "mn", *jn, lv, d)
                    for c in range(NCH):
                        for d in range(2):
                            need(pe_done, "U", *jn, c, d)
                            dv(ts(j_Un[:, d, :], bank[3 * d][:, 128:256], -1.0, None, ALU.mult), "U", *jn, c, d, hold=False)
                        for d in range(2):
                            need(pe_done, "state", *jn, c, d)
                            ch = c if d == 0 else NCH - 1 - c
                            last = CH * ch + (CH - 1 if d == 0 else 0)
                            dv(tt(j_S[:, d, :], j_S[:, d, :], bank[3 * d][:, 256:384], ALU.add))
                            dv(ts(j_S[:, d, :], j_S[:, d, :], j_P[:, d, last:last + 1], None, ALU.mult), "state", *jn, c, d)
                    if emit:
                        need(pe_done, "ymean", *jn)
                        dv(tt(j_Y, j_Y, bank[7][:, 0:256], ALU.subtract), "yc", *jn)
                        need(act_done, "yrms", *jn)
                        dv(dve.reciprocal(j_rs, j_rs))
                        dv(tt(j_Y, j_Y, j_rs, ALU.mult))
                        dv(ts(j_Y, j_Y, V("lg", b), V("lb", b), ALU.mult, ALU.add))
                        dv(tt(j_Y, j_Y, j_cv, ALU.add))
                        need(pe_done, "gate", *jn)
                        dv(tt(r_, j_Y, bank[5][:, 0:256], ALU.mult), *(("yrw", l) if (b, q) == (NB - 1, 1) else ()))
                c0, nt = cols(l)
                for n in range(KT):
                    st = 4 * (n % 2)
                    s0, s1 = (wk(8192 + 512 * (2 * (n % 2) + g), nt) for g in range(2))
                    m_ = wk(4096 + 512 * n, nt)
                    need(act_done, "mg", l, n, 1)
                    need(pe_done, "mb", l, n, 1)
                    dv(tt(m_, bank[st + 2][:, 0:nt], s0, ALU.mult), hold=False)
                    dv(tt(s1, bank[st + 3][:, 0:nt], s1, ALU.mult))
                    dv(tt(m_, m_, s1, ALU.add), "merge", l, n)
                dve.wait_ge(x_loaded, 16 * (2 * l + 2))
                spans = [(0, CTX, 1), (CTX, LAT, 0)] if l == 0 else [(CTX, LAT, 0)]
                for n in range(KT):
                    need(pe_done, "wo", l, n)
                    for s0_, n_, v in spans:
                        dv(stt(x3[:, n, s0_:s0_ + n_], bank[n % 2][:, s0_ - c0:s0_ - c0 + n_], modv[:, 16 + n, v:v + 1],
                               x3[:, n, s0_:s0_ + n_], ALU.mult, ALU.add), "res1", l, n, hold=False)
                need(act_done, "rms2", l)
                dv(dve.reciprocal(rstd[:, 0:nt], rstd[:, 0:nt]))
                dv(tt(h3[:, :, c0:c0 + nt], x3[:, :, c0:c0 + nt], rstd[:, 0:nt].unsqueeze(1).to_broadcast([P, KT, nt]), ALU.mult), "xr2", l)
                for k in range(KT):
                    a0_, n_ = (CTX, LAT) if l == 0 else (CTX + 128, 128)
                    dv(ts(h3[:, k, a0_:a0_ + n_], h3[:, k, a0_:a0_ + n_], nrm[:, 16 + 2 * k:17 + 2 * k], modv[:, 24 + k, 0:1], ALU.mult, ALU.add),
                       *(("h2", l) if k == KT - 1 else ()), hold=False)
                if l == 0:
                    for f in range(NFF):
                        need(act_done, "silu", f)
                        need(pe_done, "gu", f, 1)
                        dv(tt(wk(4096 + 512 * f, 512), bank[2 * (f % 2) + 1][:, :], wk(15360 + 512 * (f % 2), 512), ALU.mult), "hff", f, hold=False)
                    for n in range(KT):
                        need(pe_done, "dn", n)
                        for s0_, n_, v in spans:
                            dv(stt(x3[:, n, s0_:s0_ + n_], bank[n % 2][:, s0_:s0_ + n_], modv[:, 40 + n, v:v + 1],
                                   x3[:, n, s0_:s0_ + n_], ALU.mult, ALU.add), "res2", n)
                    dve_done.book[("dve", "ffn", 0)] = dve_done.n
                    continue
                need(pe_done, "logits")
                lg = small[:, 96:112].rearrange("p (t e) -> p t e", t=2)
                top = small[:, 112:128].rearrange("p (t e) -> p t e", t=2)
                dv(dve.tensor_copy(lg, bank[1][:, 0:16].rearrange("p (t e) -> p t e", t=2)))
                ti = tidx[:, :].rearrange("p (t e) -> p t e", t=2)
                for tb in range(2):
                    dv(dve.max(top[:, tb, :], lg[:, tb, :]))
                    dv(dve.max_index(ti[:, tb, :], top[:, tb, :], lg[:, tb, :]))
                tf = small[:, 128:144].rearrange("p (t e) -> p t e", t=2)
                dv(dve.tensor_copy(tf, ti))
                dv(tt(small[:, 34:36].unsqueeze(2), top[:, :, 1:2], top[:, :, 0:1], ALU.subtract), "gap")
                mask = rt[:, 0:16].rearrange("p (t e) -> p t e", t=2)
                w8 = rt[:, 16:32].rearrange("p (t e) -> p t e", t=2)
                one1 = rt[:, 32:48].rearrange("p (t e) -> p t e", t=2)
                iota = C("iota")
                for tb in range(2):
                    dv(ts(one1[:, tb, :], iota[:, 0:8], tf[:, tb, 0:1], None, ALU.is_equal))
                    dv(ts(w8[:, tb, :], iota[:, 0:8], tf[:, tb, 1:2], None, ALU.is_equal))
                dv(tt(mask, one1, w8, ALU.add), "mask")
                need(act_done, "gap")
                dv(ts(small[:, 36:38], small[:, 32:34], 1.0, None, ALU.add))
                dv(dve.reciprocal(small[:, 38:40], small[:, 36:38]))
                dv(tt(small[:, 40:42], small[:, 32:34], small[:, 38:40], ALU.mult))
                for tb in range(2):
                    dv(ts(w8[:, tb, :], w8[:, tb, :], small[:, 40 + tb:41 + tb], None, ALU.mult))
                    dv(stt(w8[:, tb, :], one1[:, tb, :], small[:, 38 + tb:39 + tb], w8[:, tb, :], ALU.mult, ALU.add))
                need(pe_done, "rank")
                keys = rt[:, 48:80].rearrange("p (t e) -> p t e", t=2)
                wts = rt[:, 80:112].rearrange("p (t e) -> p t e", t=2)
                dv(dve.memset(rt[:, 48:112], 0.0))
                rank = bank[0][:, 0:16].rearrange("p (t e) -> p t e", t=2)
                dv(tt(keys[:, :, 0:8], rank, mask, ALU.mult))
                dv(ts(one1, mask, 1.0, 1e4, ALU.subtract, ALU.mult))
                dv(tt(keys[:, :, 0:8], keys[:, :, 0:8], one1, ALU.add))
                dv(dve.tensor_copy(wts[:, :, 0:8], w8))
                over = rt[:, 112:120]
                place = rt[:, 120:128]
                dv(ts(over, bank[0][:, 16:24], 128.5, None, ALU.is_gt))
                dv(dve.tensor_tensor_scan(out=place, data0=over, data1=over, initial=0.0, op0=ALU.add, op1=ALU.bypass))
                for i in range(3):
                    sel = rt[:, 128:136]
                    dv(ts(sel, place, float(i + 1), None, ALU.is_equal))
                    dv(tt(sel, sel, over, ALU.mult))
                    dv(tt(rt[:, 136:144], sel, iota[:, 0:8], ALU.mult))
                    dv(dve.tensor_reduce(rt[:, 144 + i:145 + i], rt[:, 136:144], AX.X, ALU.add))
                    for tb in range(2):
                        dv(stt(rt[:, 136:144], keys[:, tb, 0:8], -128.0, sel, ALU.add, ALU.mult))
                        dv(dve.tensor_reduce(keys[:, tb, 8 + i:9 + i], rt[:, 136:144], AX.X, ALU.add))
                        dv(tt(rt[:, 136:144], w8[:, tb, :], sel, ALU.mult))
                        dv(dve.tensor_reduce(wts[:, tb, 8 + i:9 + i], rt[:, 136:144], AX.X, ALU.add))
                dv(dve.memset(ctrl[0:1, :], 0))
                dv(dve.tensor_copy(ctrl[0:1, 8:11], rt[0:1, 144:147]))
                dv(dve.tensor_copy(ctrl[0:1, NJ:NJ + 1], place[0:1, 7:8]))
                dv(ts(rt[0:1, 150:151], place[0:1, 7:8], float(NE), None, ALU.add))
                dv(dve.tensor_copy(ctrl[0:1, NJ + 1:NJ + 2], rt[0:1, 150:151]), "ctrl")
                jobs_here = dve.value_load(ctrl[0:1, NJ + 1:NJ + 2], min_val=NE, max_val=NJ)
                with dve.Fori(0, jobs_here) as j:
                    for tb in range(2):
                        dve.tensor_scalar(m_G[:, tb, :], iota, keys[:, tb, bass.ds(j, 1)], None, ALU.is_equal).then_inc(X["key2"], 1)
                    dve.wait_ge(X["key2"], j * 2 + 2)
                    for tb in range(2):
                        ins = dve.tensor_scalar(m_Gw[:, tb, :], m_G[:, tb, :], wts[:, tb, bass.ds(j, 1)], None, ALU.mult)
                    ins.then_inc(X["key"], 1)
                    for c in range(EC):
                        dve.wait_ge(X["silu"], j * EC + (c + 1))
                        dve.wait_ge(ring_used, used_count("u", c, j))
                        if c >= 2:
                            dve.wait_ge(X["tr"], j * EC + (c - 1))
                        dve.tensor_tensor(m_hid[:, c % 2, :], bank[2 * (c % 2) + 1][:, :], m_sil[:, c % 2, :], ALU.mult).then_inc(X["act"], 1)
                    for g in range(4):
                        dve.wait_ge(X["sc"], j * 4 + (g + 1))
                        for k in range(2):
                            kk_ = 2 * g + k
                            ins = dve.scalar_tensor_tensor(x3[:, kk_, CTX:T], bank[g][:, 256 * k:256 * k + 256], modv[:, 40 + kk_, 0:1],
                                                           x3[:, kk_, CTX:T], ALU.mult, ALU.add)
                        ins.then_inc(X["add"], 1)
                dve.wait_ge(X["add"], NE * 4)
                dv(dve.tensor_copy(small[:, 200:201], small[:, 34:35]), "final")

        @block.gpsimd
        def _(pool):
            seen = {}

            def need(sig, *key):
                n = sig.count(*key)
                if seen.get(sig.name, 0) < n:
                    seen[sig.name] = n
                    pool.wait_ge(sig.sem, n)

            for l in range(L):
                if l == 0:
                    need(dve_done, "shift", 0, 13)
                    for b in range(NB):
                        pool.dma_start(vf_mid[:, b, :], pr[:, 4 + 3 * b, :]).then_inc(vf_stored, 16)
                    pool.wait_ge(vf_stored, 16 * NB)
                    need(act_done, "yatt", 0, NB - 1)
                else:
                    need(act_done, "yatt", 1, NB - 1)
                    pool.dma_start(wk(2048, 2048, NB), vf_mid).then_inc(vf_loaded, 16)
                    need(dve_done, "vres", NB - 1)
                for n_ in ("kapbd", "Kbd", "Bbd", "vbd"):
                    pool_done.done(pool.memset(wk(*J[n_]), 0.0), "zeroed", l)
                for jl, b, q in [x for x in jobs if x[0] == l]:
                    jn = (l, b, q)
                    for lv in range(6):
                        for d in range(2):
                            if lv == 0:
                                need(dve_done, "gram", *jn, 1, 2 * d + 1)
                            else:
                                need(pe_done, "x", *jn, lv - 1, d)
                                if lv == 1:
                                    need(dve_done, "mn", *jn, 0, d)
                            pool_done.done(pool.tensor_tensor(j_Um[:, 4 * d:4 * d + 4, :], j_U[:, 4 * d:4 * d + 4, :],
                                                              level[:, 2 * lv + d, :].unsqueeze(1).to_broadcast([P, 4, 128]), ALU.mult),
                                           "um", *jn, lv, d)
    return book


_OUT = (P, KT, LAT)


def kernel(**inputs):
    import numpy as _np
    import concourse.bacc as _bacc
    from concourse import mybir as _mybir
    from concourse.bass_utils import run_bass_kernel_spmd as _run

    arrays = lay_out({k: _np.asarray(v) for k, v in inputs.items()})
    book = {}
    for _ in range(2):
        nc = _bacc.Bacc("TRN2", target_bir_lowering=False, num_devices=1)
        f32 = _mybir.dt.float32
        aps = {n: nc.dram_tensor("in_" + n, v.shape, f32, kind="ExternalInput").ap() for n, v in arrays.items()}
        out = nc.dram_tensor("out_0", _OUT, f32, kind="ExternalOutput").ap()
        x_mid = nc.dram_tensor("x_mid", (P, KT, T), f32, kind="Internal").ap()
        vf_mid = nc.dram_tensor("vf_mid", (P, NB, T), f32, kind="Internal").ap()
        build(nc, aps, out, x_mid, vf_mid, book)
    r = _run(nc, [{"in_" + n: v for n, v in arrays.items()}], core_ids=[0])
    y = r.results[0]["out_0"]
    return _np.ascontiguousarray(y.transpose(2, 1, 0).reshape(1, LAT, D))


def lay_out(i):
    c32 = np.ascontiguousarray

    def kp(w):
        s = w.shape
        w = w.reshape(s[:-2] + (s[-2] // P, P, s[-1]))
        return np.swapaxes(w, -3, -2)

    def blocks(w, n):
        w = kp(w)
        return w.reshape(P, w.shape[1], n, P).transpose(0, 2, 1, 3)

    o = {}
    x = np.concatenate([i["ctx"][0], i["x"][0]], 0)
    o["x"] = c32(x.T.reshape(KT, P, T).transpose(1, 0, 2))
    c = np.stack([i["c"][0], i["c_ctx"]], -1)
    o["c"] = c32(c.reshape(KT, P, 2).transpose(1, 0, 2).reshape(P, 16))
    o["consts"] = constants()
    o["w_mod"] = c32(kp(i["w_mod"]).reshape(L, P, KT, 12, 512).transpose(0, 3, 1, 2, 4).reshape(L, 12, P, 4096))
    rw, at = 3 * RW + 256, 768
    hp = np.concatenate([np.r_[64 * h:64 * h + 64, 64 * (h + 4):64 * (h + 4) + 64] for h in range(4)])
    blk = np.arange(P)
    colsets = [3 * RW + blk, 3 * RW + 128 + blk, rw + 512 + blk, rw + 640 + blk] + [rw + hp[P * b:P * b + P] for b in range(4)]
    rwcols = [3 * RW + blk, 3 * RW + 128 + blk]
    for b in range(NB):
        for part in range(3):
            colsets.append(part * RW + P * b + blk)
            rwcols.append(part * RW + P * b + blk)
    win, wmrg, wout, pvs, mws = [], [], [], [], []
    for l in range(L):
        w = i["w_in"][l]
        bl = blocks(w[:, np.concatenate(colsets)], 20)
        win.append(bl.reshape(P, 5, 4096).transpose(1, 0, 2))
        g = w[:, rw + at:]
        g0, g1 = blocks(g[:, :D], KT), blocks(g[:, D:], KT)
        b0, b1 = blocks(i["w_br_rwkv"][l], KT), blocks(i["w_br_attn"][l][hp], KT)
        m = np.concatenate([v.reshape(P, KT, -1) for v in (g0, g1, b0, b1)], -1)
        wmrg.append(m.transpose(1, 0, 2))
        wout.append(blocks(i["w_out"][l], KT).reshape(P, 2, 4096).transpose(1, 0, 2))
        pv = np.zeros((P, NPV), np.float32)

        def put(name, v):
            pv[:, PV[name][0]:PV[name][1]] = v

        put("norm1", i["norm1"][l].reshape(KT, P).T)
        put("norm2", i["norm2"][l].reshape(KT, P).T)
        put("bmod", i["b_mod"][l].reshape(48, P).T)
        for q in range(2):
            put(f"mu{q}", np.stack([i["tshift"][l, q][cs] for cs in rwcols], 1))
        put("w0", i["w0"][l].reshape(8, P).T)
        put("a0", i["a0"][l].reshape(8, P).T)
        for n, s in (("kk", "k_k"), ("ka", "k_a"), ("lg", "lnx_g"), ("lb", "lnx_b")):
            put(n, i[s][l].reshape(NB, P).T)
        put("rk", i["r_k"][l].reshape(NB, P).T)
        if l:
            put("v0", i["v0"][l - 1].reshape(NB, P).T)
        put("qn", np.concatenate([i["q_norm"][l]] * 2)[:, None])
        put("kn", np.concatenate([i["k_norm"][l]] * 2)[:, None])
        put("sink", np.broadcast_to(i["sink"][l][None], (P, 8)))
        pvs.append(pv)
        mw = np.zeros((P, 2304), np.float32)
        mw[0:64, 0:1024] = i["w_decay_up"][l].transpose(1, 0, 2).reshape(64, 1024)
        mw[64:128, 0:1024] = i["w_iclr_up"][l].transpose(1, 0, 2).reshape(64, 1024)
        mw[:, 1024:1536] = i["w_gate_up"][l]
        if l:
            mw[:, 1536:1792] = kp(i["w_vres_down"][l - 1]).reshape(P, 256)
            mw[0:32, 1792:2304] = i["w_vres_up"][l - 1]
        mws.append(mw)
    o["w_in"], o["w_mrg"], o["w_out"] = c32(np.stack(win)), c32(np.stack(wmrg)), c32(np.stack(wout))
    o["pv"], o["mw"] = np.stack(pvs), np.stack(mws)
    g, u = blocks(i["ffn_gate"][0], NFF), blocks(i["ffn_up"][0], NFF)
    gu = np.stack([g, u], 2)
    o["w_gu"] = c32(gu.reshape(P, 11, 4096).transpose(1, 0, 2))
    o["w_dn"] = c32(blocks(i["ffn_down"][0], KT).reshape(P, KT, FF).transpose(1, 0, 2))
    o["router"] = c32(kp(i["router"][0]).reshape(P, 64))
    g = kp(i["moe_gate"][0]).reshape(NE, P, KT, EC, 512)
    u = kp(i["moe_up"][0]).reshape(NE, P, KT, EC, 512)
    d = kp(i["moe_down"][0]).reshape(NE, P, EC, 4, D)
    gu = lambda w, c: w[:, :, :, c, :].reshape(NE, P, 4096)
    parts = [gu(g, 0), gu(u, 0)]
    for c in range(1, EC):
        parts += [gu(g, c), gu(u, c), d[:, :, c - 1].reshape(NE, P, 4096)]
    parts.append(d[:, :, EC - 1].reshape(NE, P, 4096))
    w_exp = np.empty((NE, 3 * EC, P, 4096), np.float32)
    for m, p_ in enumerate(parts):
        w_exp[:, m] = p_
    o["w_exp"] = w_exp
    return o
```

```python
import numpy as np
import concourse.bass as bass
from concourse import mybir
from contextlib import ExitStack

P = 128
D = 1024
KT = D // P
CTX = LAT = 256
T = CTX + LAT
HD = 64
CH = 64
NCH = CTX // CH
RW = 512
NB = RW // P
FF = 2816
NFF = FF // P
FE = 3584
EC = FE // 512
NE = 8
NJ = NE + 3
SLOT = 4096
NS = 3
UNIT = SLOT // 2
WB = 3
WORK = 19456
MOE_F32 = 10496
L = 2
EPS = 1e-6
GN_EPS = 64e-5
DECAY = -float(np.exp(-0.5))

PV = {}
_n = 0
for _name, _w in [("norm1", 8), ("norm2", 8), ("bmod", 48), ("mu0", 14), ("mu1", 14), ("w0", 8), ("a0", 8),
                  ("kk", 4), ("ka", 4), ("rk", 4), ("lg", 4), ("lb", 4), ("v0", 4), ("qn", 1), ("kn", 1), ("sink", 8)]:
    PV[_name] = (_n, _n + _w)
    _n += _w
NPV = _n

CO = {}
_n = 0
for _name, _w in [("ident", 128), ("strict", 256), ("incl", 256), ("level", 6 * 2 * 128), ("cos", 256), ("sin", 256), ("rot", 128),
                  ("bones", 128), ("bmean", 128), ("mean", 128), ("ones", 128), ("before", 128), ("amask", 512),
                  ("iota", 128), ("sel", 2)]:
    CO[_name] = (_n, _n + _w)
    _n += _w
NCO = _n


def constants():
    c = np.zeros((P, NCO), np.float32)

    def put(name, a):
        c[:, CO[name][0]:CO[name][1]] = np.asarray(a, np.float32).reshape(P, -1)

    i = np.arange(P)
    s, t = i[:, None], i[None, :]
    bd = (s // 64) == (t // 64)
    fwd = bd & (s < t)
    put("ident", np.eye(P))
    put("strict", np.stack([fwd, fwd.T], 1))
    put("incl", np.stack([fwd | (s == t), fwd.T | (s == t)], 1))
    lv = []
    for k in range(6):
        n = 1 << k
        m = (s // (2 * n) == t // (2 * n)) & ((s // n) % 2 == 0) & ((t // n) % 2 == 1)
        lv.append(np.stack([m, m.T], 1))
    put("level", np.stack(lv, 1))
    half = HD // 2
    inv = np.float32(10000.0) ** (-np.arange(0, half, 2, dtype=np.float32) / np.float32(half))
    tok = np.arange(LAT)
    ar = (tok // 64).astype(np.float32)[:, None] * inv
    ac = (tok % 64).astype(np.float32)[:, None] * inv
    ang = np.concatenate([ar, ar, ac, ac], -1).astype(np.float32)
    put("cos", np.tile(np.cos(ang).T, (2, 1)))
    put("sin", np.tile(np.sin(ang).T, (2, 1)))
    rot = np.zeros((P, P))
    for h in range(2):
        for q in range(2):
            for j in range(16):
                a = 64 * h + 32 * q + j
                rot[a + 16, a] = -1.0
                rot[a, a + 16] = 1.0
    put("rot", rot)
    put("bones", bd)
    put("bmean", bd / 64.0)
    put("mean", np.full((P, P), 1.0 / D))
    put("ones", np.ones((P, P)))
    put("before", s < t)
    q = np.arange(P)[:, None]
    am = [np.where(np.abs(np.arange(LAT)[None] - (q + P * b)) <= 128, 0.0, -1e30) for b in range(2)]
    put("amask", np.stack(am, 1))
    put("iota", np.tile(np.arange(P), (P, 1)))
    sel = np.zeros((P, 2))
    for g in range(4):
        for v in range(2):
            sel[32 * g + v, v] = 1.0
    put("sel", sel)
    return c


class Signal:

    def __init__(self, sem, name, book):
        self.sem, self.name, self.book, self.n = sem, name, book, 0

    def done(self, ins, *key):
        ins.then_inc(self.sem, 1)
        self.n += 1
        if key:
            self.book[(self.name,) + key] = self.n

    def count(self, *key):
        return self.book.get((self.name,) + key, 1)


def build(nc, a, out, x_mid, vf_mid, h_mid, book):
    f32 = mybir.dt.float32
    i32 = mybir.dt.int32
    u32 = mybir.dt.uint32
    ALU = mybir.AluOpType
    ACT = mybir.ActivationFunctionType
    AX = mybir.AxisListType
    ctx = ExitStack()
    with ctx:
        def sb(name, n, dt=f32):
            return ctx.enter_context(nc.sbuf_tensor(name, [P, n], dt))

        ring = sb("ring", NS * SLOT)
        hbuf = sb("hbuf", KT * T)
        co = sb("co", NCO)
        pv = sb("pv", NPV)
        modt = sb("modt", 96)
        nrm = sb("nrm", 32)
        rstd = sb("rstd", 512)
        csil = sb("csil", KT * 32)
        ctrl = sb("ctrl", 16, i32)
        small = sb("small", 256)
        tidx = sb("tidx", 16, u32)
        with ExitStack() as layers:
            work, proj, yatt, mw = (layers.enter_context(nc.sbuf_tensor(n_, [P, w_], f32))
                                    for n_, w_ in (("work", WORK), ("proj", 14 * T), ("yatt", NB * T), ("mw", 2304)))
        sb("work_kept", MOE_F32)
        f32r = mybir.dt.float32r
        w_hi, w_lo = (ctx.enter_context(nc.sbuf_tensor(n_, [P, WB, UNIT], f32r)) for n_ in ("w_hi", "w_lo"))
        xg_hi, xg_lo = (ctx.enter_context(nc.sbuf_tensor(n_, [P, KT, P], f32r)) for n_ in ("xg_hi", "xg_lo"))
        hT_hi, hT_lo = (ctx.enter_context(nc.sbuf_tensor(n_, [P, 2, 4, P], f32r)) for n_ in ("hT_hi", "hT_lo"))
        bank = [ctx.enter_context(nc.psum_tensor(f"bank{i}", [P, 512], f32)) for i in range(8)]

        def sem(name):
            return ctx.enter_context(nc.semaphore(name))

        pe_done = Signal(sem("pe_done"), "pe", book)
        act_done = Signal(sem("act_done"), "act", book)
        dve_done = Signal(sem("dve_done"), "dve", book)
        pool_done = Signal(sem("pool_done"), "pool", book)
        ring_full = [sem(f"ring_full{i}") for i in range(NS)]
        const_loaded, par_loaded, mw_loaded, x_loaded, c_loaded = (sem(n) for n in
                                                                   ("const_loaded", "par_loaded", "mw_loaded", "x_loaded", "c_loaded"))
        x_stored, vf_stored, vf_loaded, out_stored = (sem(n) for n in ("x_stored", "vf_stored", "vf_loaded", "out_stored"))
        h_stored, h_free, h_loaded = (sem(n) for n in ("h_stored", "h_free", "h_loaded"))
        X = {n: sem("moe_" + n) for n in ("key", "key2", "gat", "xg", "gt", "gtc", "silu", "act", "tr", "trc", "trl", "yc", "xl", "hi", "lo", "wused", "sc", "add", "zero")}

        def C(name, *dims):
            v = co[:, CO[name][0]:CO[name][1]]
            return v if not dims else v.rearrange("p (a b) -> p a b", a=dims[0])

        ident = C("ident")
        strict = C("strict", 2)
        incl = C("incl", 2)
        level = C("level", 12)
        amask = C("amask", 2)

        def V(name, i=0):
            o = PV[name][0] + i
            return pv[:, o:o + 1]

        def wk(off, n, *dims):
            v = work[:, off:off + n]
            if len(dims) == 1:
                return v.rearrange("p (a b) -> p a b", a=dims[0])
            if len(dims) == 2:
                return v.rearrange("p (a b c) -> p a b c", a=dims[0], b=dims[1])
            return v

        h3 = hbuf[:, :].rearrange("p (k t) -> p k t", k=KT)
        pr = proj[:, :].rearrange("p (k t) -> p k t", k=14)
        ya = yatt[:, :].rearrange("p (k t) -> p k t", k=NB)
        x3 = wk(0, 4096, KT)
        modv = modt[:, :].rearrange("p (m v) -> p m v", v=2)

        items = []
        for l in range(L):
            items += [(a["w_mod"][l, n], 4096) for n in range(12)]
            items += [(a["w_in"][l, n], 4096) for n in range(5)]
            items += [(a["w_mrg"][l, n], 3072) for n in range(8)]
            items += [(a["w_out"][l, n], 4096) for n in range(2)]
            if l == 0:
                items += [(a["w_gu"][n], 4096) for n in range(11)]
                items += [(a["w_dn"][n], 2816) for n in range(8)]
        items += [(a["router"], 64)]
        N_STATIC = len(items)
        order = [("g", 0), ("u", 0)]
        for c in range(1, EC):
            order += [("g", c), ("u", c), ("d", c - 1)]
        order += [("d", EC - 1)]
        place_of = {x: i for i, x in enumerate(order)}

        NU = 6 * EC

        def unit(kind, c, half):
            return 2 * place_of[kind, c] + half

        def count(j, u):
            return j * NU + (u + 1)

        taken = [0]

        def slot(i):
            return ring[:, (i % NS) * SLOT:(i % NS + 1) * SLOT]

        QK = 3072
        att = wk(0, QK, 6)

        def attention_units(l):
            return [(b, hh, qb) for b in range(NB) for hh in range(2) for qb in ((0, 1, 2, 3) if l == 0 else (2, 3))]

        def key_blocks(qb):
            return 2 if qb < 2 else 4

        score_bank = lambda u: bank[(0, 1, 6)[u % 3]]
        soft = lambda u: small[:, 8 * (u % 3):8 * (u % 3) + 8]
        probs = lambda u, nk: wk(4608 + 512 * (u % 3), 128 * nk)
        probs_T = lambda u: wk(6656 + 512 * (u % 2), 512)

        o = 0
        J = {}
        for n_, w_ in [("kr", 1024), ("kapbd", 1024), ("Kbd", 1024), ("Bbd", 1024), ("vbd", 512), ("LkT", 1024), ("QkT", 1024),
                       ("U", 1024), ("QbT", 1024), ("N", 1024), ("Um", 1024), ("Ktok", 1024), ("Btok", 1024), ("Vtok", 512),
                       ("lw", 512), ("Lc", 512), ("Pc", 512), ("Qc", 512), ("ic", 512), ("kh", 512), ("bb", 512),
                       ("kk", 256), ("kkt", 256), ("cv", 256), ("sq", 256), ("rs", 256), ("Y", 256), ("S", 256), ("Rs", 256), ("Un", 256)]:
            J[n_] = (o, w_)
            o += w_
        assert o <= 19200, o

        def j3(name, n):
            return wk(*J[name], n)

        def hb(off, n, *dims):
            v = hbuf[:, off:off + n]
            if len(dims) == 1:
                return v.rearrange("p (a b) -> p a b", a=dims[0])
            if len(dims) == 2:
                return v.rearrange("p (a b c) -> p a b c", a=dims[0], b=dims[1])
            return v

        jj_kr = [wk(*J["kr"], 8, 2), hb(0, 1024, 8, 2)]
        jj_kap = [j3("kapbd", 8), hb(1024, 1024, 8)]
        jj_P = [j3("Pc", 2), hb(2048, 512, 2)]
        jj_cv = [wk(*J["cv"]), hb(2560, 256)]
        j_sqp, j_rsp = hb(2816, 256), hb(3072, 256)
        j_K, j_B = j3("Kbd", 8), j3("Bbd", 8)
        j_M, j_X = j_K, j_B
        j_v, j_Lk, j_Qk, j_U, j_Qb, j_N, j_Um = j3("vbd", 4), j3("LkT", 8), j3("QkT", 8), j3("U", 8), j3("QbT", 8), j3("N", 8), j3("Um", 8)
        j_Kt, j_Bt, j_Vt = j3("Ktok", 8), j3("Btok", 8), j3("Vtok", 4)
        j_lw, j_L, j_Q, j_ic, j_kh, j_bb = (j3(n, 2) for n in ("lw", "Lc", "Qc", "ic", "kh", "bb"))
        j_kk, j_kkt, j_sq, j_rs, j_Y = (wk(*J[n]) for n in ("kk", "kkt", "sq", "rs", "Y"))
        j_S, j_R, j_Un = (j3(n, 2) for n in ("S", "Rs", "Un"))
        mup = mw[:, 0:1024].rearrange("p (d c) -> p d c", d=2)
        mgate = mw[:, 1024:1536]
        mvd = mw[:, 1536:1792].rearrange("p (k c) -> p k c", k=KT)
        mvu = mw[:, 1792:2304]

        def layer_jobs(l):
            js = [(l, b, q) for b in range(NB) for q in range(2)]
            return list(zip(js, [None] + js[:-1], js[1:] + [None]))

        def turn(jn):
            return jn[2]

        def emits(jn):
            return jn[0] == 0 or jn[2] == 1

        def cols(l):
            return (0, T) if l == 0 else (CTX, LAT)

        o = 4096
        M = {}
        for n_, w_ in [("htok", 2048), ("sil", 1024), ("hid", 1024), ("G", 256), ("Gw", 256), ("GwT", 256),
                       ("y", 1024), ("rt", 512)]:
            M[n_] = (o, w_)
            o += w_
        assert o == MOE_F32, o
        m_htok = wk(*M["htok"], 2)
        m_sil = wk(*M["sil"], 2)
        m_hid = wk(*M["hid"], 2)
        m_G = wk(*M["G"], 2)
        m_Gw = wk(*M["Gw"], 2)
        m_GwT = wk(*M["GwT"])
        m_y = wk(*M["y"])
        rt = wk(*M["rt"])

        block = ctx.enter_context(nc.Block())

        @block.sync
        def _(sp):
            for i, (src, n) in enumerate(items):
                if i >= NS:
                    sp.wait_ge(pe_done.sem, pe_done.count("item", i - NS))
                sp.dma_start(slot(i)[:, 0:n], src).then_inc(ring_full[i % NS], 16)

            def expert(e, j):
                for m in range(3 * EC):
                    if isinstance(j, int) and m < NS:
                        sp.wait_ge(pe_done.sem, pe_done.count("item", N_STATIC + m - NS))
                    else:
                        sp.wait_ge(X["lo"], j * NU + (2 * (m - NS) + 2))
                    src = a["w_exp"][e, m] if isinstance(e, int) else a["w_exp"][bass.ds(e, 1), m, :, :].rearrange("e p n -> p (e n)")
                    sp.dma_start(slot(N_STATIC + m), src).then_inc(ring_full[(N_STATIC + m) % NS], 16)

            expert(0, 0)
            with sp.Fori(1, NE) as j:
                expert(j, j)
            sp.wait_ge(dve_done.sem, dve_done.count("ctrl"))
            more = sp.value_load(ctrl[0:1, NJ:NJ + 1], min_val=0, max_val=3)
            with sp.If(more > 0):
                with sp.Fori(0, more) as j2:
                    r = sp.value_load(ctrl[0:1, bass.ds(j2 + NE, 1)], min_val=0, max_val=NE - 1)
                    expert(r, j2 + NE)
            sp.wait_ge(dve_done.sem, dve_done.count("final"))
            sp.dma_start(out, x3[:, :, CTX:T]).then_inc(out_stored, 16)
            sp.wait_ge(out_stored, 16)

        @block.tensor
        def _(pe):
            seen = {}

            def need(sig, *key):
                n = sig.count(*key)
                if seen.get(sig.name, 0) < n:
                    seen[sig.name] = n
                    pe.wait_ge(sig.sem, n)

            def mm(o_, lhsT, rhs, start=True, stop=True, **kw):
                return pe.matmul(o_, lhsT, rhs, start=start, stop=stop, **kw)

            def next_item():
                i = taken[0]
                taken[0] += 1
                pe.wait_ge(ring_full[i % NS], 16 * (i // NS + 1))
                return slot(i)

            def item_done():
                book[("pe", "item", taken[0] - 1)] = pe_done.n

            pe.wait_ge(const_loaded, 16)
            for l in range(L):
                need(act_done, "csil")
                for n in range(12):
                    w = next_item()[:, :].rearrange("p (k c) -> p k c", k=KT)
                    cs3 = csil[:, :].rearrange("p (k c) -> p k c", k=KT)
                    if n >= 2:
                        need(act_done, "modrow", l, n - 2)
                    elif l:
                        need(dve_done, "ffn", 0)
                    b_ = bank[n % 2]
                    for k in range(KT):
                        g = k % 4
                        ins = mm(b_[32 * g:32 * g + 32, :], cs3[:, k, :], w[:, k, :], start=(k < 4), stop=(k >= 4),
                                 tile_position=(0, 32 * g), skip_group_check=True)
                        if k == KT - 1:
                            pe_done.done(ins, "modrow", l, n)
                            item_done()
                    need(act_done, "modrow", l, n)
                    for j in range(4):
                        ins = mm(bank[2][:, 2 * (4 * n + j):2 * (4 * n + j) + 2], wk(0, 6144)[:, 512 * n + 128 * j:512 * n + 128 * j + 128],
                                 C("sel"))
                    pe_done.done(ins, "modt", l, n)
                for k in range(KT):
                    need(act_done, "sq1", l, k)
                    if k == 0:
                        need(act_done, "modrow", l, 11)
                    ins = mm(bank[0][:, :], C("mean"), wk(4096 + 512 * k, 512), start=(k == 0), stop=(k == KT - 1))
                pe_done.done(ins, "ms1", l)
                need(act_done, "h1", l)
                need(dve_done, "h1", l)
                for n in range(5):
                    w = next_item()[:, :].rearrange("p (j k c) -> p j k c", j=4, k=KT)
                    for j in range(4):
                        bi = 4 * n + j
                        if bi >= 4:
                            need(act_done, "proj", l, bi - 4)
                        else:
                            need(act_done, "rms1", l)
                            need(dve_done, "modt", l)
                        for k in range(KT):
                            ins = mm(bank[bi % 4][:, :], w[:, j, k, :], h3[:, k, :], start=(k == 0), stop=(k == KT - 1))
                        pe_done.done(ins, "proj", l, bi)
                    item_done()
                for i in range(5):
                    need(act_done, "qsq", l, i)
                    if i >= 2:
                        need(act_done, "qrms", l, i - 2)
                    pe_done.done(mm(bank[i % 2][:, :], C("bmean"), wk(3072 + 512 * (i % 2), 512)), "qms", l, i)
                    need(dve_done, "qn", l, i)
                    if i >= 2:
                        need(dve_done, "qrot", l, i - 2)
                    pe_done.done(mm(bank[2 + i % 2][:, 0:256], C("rot"), att[:, i, CTX:T]), "qrot", l, i)
                for tb in range(4):
                    if tb == 0:
                        need(act_done, "proj", l, 19)
                        need(dve_done, "qrot", l, 4)
                    ins = pe.transpose(bank[4][:, 128 * tb:128 * tb + 128], att[:, 5, 128 * tb:128 * tb + 128], ident)
                pe_done.done(ins, "vtok", l)
                need(act_done, "vtok", l)
                vt = wk(4096, 512, 4)
                units = attention_units(l)

                def score(u):
                    b, hh, qb = units[u]
                    if u >= 3:
                        need(act_done, "exp", l, u - 3)
                    q_ = att[64 * hh:64 * hh + 64, b, 128 * qb:128 * qb + 128]
                    k_ = att[64 * hh:64 * hh + 64, 4, :]
                    ins = mm(score_bank(u)[:, 0:256], q_, k_[:, 0:256])
                    if key_blocks(qb) == 4:
                        mm(score_bank(u)[:, 256:512], q_, k_[:, 256:512], stop=False)
                        ins = mm(score_bank(u)[:, 256:512], ident, amask[:, qb - 2, :], start=False)
                    pe_done.done(ins, "score", l, u)

                def turn_probs(u):
                    nk = key_blocks(units[u][2])
                    need(dve_done, "prob", l, u)
                    if u >= 2:
                        need(act_done, "pT", l, u - 2)
                    for kb in range(nk):
                        ins = pe.transpose(bank[2 + u % 2][:, 128 * kb:128 * kb + 128], probs(u, nk)[:, 128 * kb:128 * kb + 128], ident)
                    pe_done.done(ins, "pT", l, u)

                def times_values(u):
                    b, hh, qb = units[u]
                    nk = key_blocks(qb)
                    need(act_done, "pT", l, u)
                    if (hh, qb) == units[0][1:] and b >= 2:
                        need(act_done, "yatt", l, b - 2)
                    for kb in range(nk):
                        ins = mm(bank[4 + b % 2][64 * hh:64 * hh + 64, 128 * qb:128 * qb + 128], vt[:, kb, 64 * hh:64 * hh + 64],
                                 probs_T(u)[:, 128 * kb:128 * kb + 128], start=(kb == 0), stop=(kb == nk - 1))
                    pe_done.done(ins, "pv", l, u)

                for u in range(len(units) + 3):
                    if u < len(units):
                        score(u)
                    if 2 <= u < len(units) + 2:
                        turn_probs(u - 2)
                    if u >= 3:
                        times_values(u - 3)
                if l == 1:
                    pe.wait_ge(mw_loaded, 32)
                    need(act_done, "yatt", 1, NB - 1)
                    for k in range(KT):
                        ins = mm(bank[7][0:32, :], mvd[:, k, :], h3[:, k, :], start=(k == 0), stop=(k == KT - 1))
                    pe_done.done(ins, "vdown")
                    need(act_done, "vdown")
                    for b in range(NB):
                        if b >= 1:
                            need(act_done, "vsig", b - 1)
                        pe_done.done(mm(bank[7][:, :], mvu[0:32, P * b:P * b + P], rstd[0:32, :]), "vup", b)
                pe.wait_ge(mw_loaded, 16 * (l + 1))
                def head(jn, i):
                    _, b, q = jn
                    q0 = 256 * q
                    if i == 1:
                        need(act_done, "kksq", *jn)
                        pe_done.done(mm(bank[6][:, 256:512], C("bones"), j_sq), "kkss", *jn)
                    if i == 2:
                        need(act_done, "kkrms", *jn)
                        for d in range(2):
                            mm(bank[7][:, 256 * d:256 * d + 256], mup[0:64, d, P * b:P * b + P], pr[0:64, 0, q0:q0 + 256])
                        for d in range(2):
                            ins = mm(bank[6][:, 256 * d:256 * d + 256], mup[64:128, d, P * b:P * b + P], pr[64:128, 0, q0:q0 + 256])
                        pe_done.done(ins, "lora", *jn)
                    if i == 4:
                        need(dve_done, "coef", *jn)
                        need(act_done, "sig", *jn)
                        pe_done.done(mm(bank[7][:, 0:256], C("bones"), j_rs), "coef", *jn)

                def post(jn, i):
                    _, b, q = jn
                    if not emits(jn):
                        return
                    if i == 0:
                        need(act_done, "y", *jn)
                        pe_done.done(mm(bank[7][:, 0:256], C("bmean"), j_Y), "ymean", *jn)
                    if i == 1:
                        need(act_done, "ysq", *jn)
                        pe_done.done(mm(bank[7][:, 256:512], C("bmean"), j_sqp), "yvar", *jn)
                        pe_done.done(mm(bank[6][:, 0:256], mgate[:, P * b:P * b + P], pr[:, 1, 256 * q:256 * q + 256]), "gate", *jn)
                    if i == 2:
                        need(act_done, "yrms", *jn)
                        need(dve_done, "post", *jn)

                first = layer_jobs(l)[0][0]
                need(dve_done, "ready", l)
                for i in range(5):
                    head(first, i)
                for jn, prev, nxt in layer_jobs(l):
                    b, q = jn[1:]
                    emit = emits(jn)
                    j_kr, j_kap = jj_kr[turn(jn)], jj_kap[turn(jn)]
                    need(dve_done, "kr", *jn)
                    need(dve_done, "bd", *jn)
                    need(pool_done, "bd", *jn)
                    need(act_done, "bd", *jn)
                    need(dve_done, "cv", *jn)
                    if prev is not None:
                        need(dve_done, "state", *prev, NCH - 1, 1)
                    for w_, src in enumerate((j_K, j_B)):
                        for s in range(8):
                            if w_ == 1 and s == 4 and prev is not None and emits(prev):
                                need(act_done, "y", *prev)
                            rhs = j_kr[:, s, :, :].rearrange("p a b -> p (a b)").unsqueeze(1).to_broadcast([P, 2, 128])
                            ins = mm(bank[4 * w_ + s // 2][:, 256 * (s % 2):256 * (s % 2) + 256], src[:, s, :], rhs)
                            if s % 2:
                                pe_done.done(ins, "gram", *jn, w_, s // 2)
                    n = 0
                    for src, m_ in ((j_K, 8), (j_B, 8), (j_v, 4)):
                        for g in range(m_ // 4):
                            if n < 2:
                                need(dve_done, "gram", *jn, 1, 2 + n)
                            else:
                                need(act_done, "tok", *jn, n - 2)
                            for s in range(4):
                                ins = pe.transpose(bank[6 + n % 2][:, 128 * s:128 * s + 128], src[:, 4 * g + s, :], ident)
                            pe_done.done(ins, "tok", *jn, n)
                            n += 1
                    for lv in range(6):
                        for d in range(2):
                            need(pool_done, "um", *jn, lv, d)
                            if lv == 0:
                                for c in range(4):
                                    ins = pe.transpose(bank[3 * d][:, 128 * c:128 * c + 128], j_Um[:, 4 * d + c, :], ident)
                                pe_done.done(ins, "x", *jn, lv, d)
                                continue
                            need(dve_done, "mn", *jn, lv - 1, d)
                            for c in range(4):
                                s = 4 * d + c
                                ins = mm(bank[3 * d][:, 128 * c:128 * c + 128], j_Um[:, s, :], j_M[:, s, :])
                            pe_done.done(ins, "x", *jn, lv, d)
                        if lv == 0:
                            continue
                        for d in range(2):
                            need(act_done, "x", *jn, lv, d)
                            for c in range(4):
                                s = 4 * d + c
                                if lv < 5:
                                    mm(bank[3 * d + 1][:, 128 * c:128 * c + 128], j_N[:, s, :], j_X[:, s, :])
                            for c in range(4):
                                s = 4 * d + c
                                ins = mm(bank[3 * d + 2][:, 128 * c:128 * c + 128], j_X[:, s, :], j_N[:, s, :])
                            pe_done.done(ins, "mn", *jn, lv, d)
                        if lv == 1:
                            need(act_done, "tok", *jn, 4)
                            need(act_done, "tok", *jn, 3)
                        if prev is not None:
                            post(prev, lv - 1)
                        if nxt is not None:
                            head(nxt, lv - 1)
                    for c in range(NCH):
                        for d in range(2):
                            ch = c if d == 0 else NCH - 1 - c
                            s = 4 * d + ch
                            if c == 0:
                                need(dve_done, "mn", *jn, 5, d)
                                need(act_done, "tok", *jn, 4)
                            else:
                                need(dve_done, "state", *jn, c - 1, d)
                            mm(bank[3 * d][:, 0:128], j_Lk[:, s, :], j_Vt[:, ch, :], stop=False)
                            pe_done.done(mm(bank[3 * d][:, 0:128], j_kap[:, s, :], j_S[:, d, :], start=False), "R", *jn, c, d)
                            if emit:
                                r_dup = j_kr[:, s, 1, :].unsqueeze(1).to_broadcast([P, 2, CH])
                                yb = bank[6][:, 128 * ch:128 * ch + 128]
                                if c == 0 and d == 0 and nxt is not None:
                                    need(act_done, "sig", *nxt)
                                mm(yb, j_S[:, d, :], r_dup, start=(c == 0 and d == 0), stop=False, skip_group_check=True)
                                mm(yb, j_Vt[:, ch, :], j_Qk[:, s, :], start=False, stop=False, skip_group_check=True)
                        for d in range(2):
                            ch = c if d == 0 else NCH - 1 - c
                            s = 4 * d + ch
                            need(act_done, "R", *jn, c, d)
                            pe_done.done(mm(bank[3 * d][:, 128:256], j_N[:, s, :], j_R[:, d, :]), "U", *jn, c, d)
                        for d in range(2):
                            ch = c if d == 0 else NCH - 1 - c
                            s = 4 * d + ch
                            need(dve_done, "U", *jn, c, d)
                            mm(bank[3 * d][:, 256:384], j_Kt[:, s, :], j_Vt[:, ch, :], stop=False)
                            pe_done.done(mm(bank[3 * d][:, 256:384], j_Bt[:, s, :], j_Un[:, d, :], start=False), "state", *jn, c, d)
                            if emit:
                                ins = mm(bank[6][:, 128 * ch:128 * ch + 128], j_Un[:, d, :], j_Qb[:, s, :], start=False,
                                         stop=(c == NCH - 1 and d == 1), skip_group_check=True)
                                pe_done.done(ins, "y", *jn, c, d)
                for i in range(3):
                    post(jn, i)
                c0, nt = cols(l)
                for n in range(KT):
                    w = next_item()
                    wg = w[:, 0:2048].rearrange("p (g k c) -> p g k c", g=2, k=KT)
                    wb = w[:, 2048:3072].rearrange("p (g k c) -> p g k c", g=2, k=NB)
                    st = 4 * (n % 2)
                    if n == 0:
                        need(dve_done, "yrw", l)
                        need(act_done, "yatt", l, NB - 1)
                        pe.wait_ge(h_loaded, 16 * (l + 1))
                    if n >= 2:
                        need(dve_done, "merge", l, n - 2)
                    for g in range(2):
                        for k in range(KT):
                            ins = mm(bank[st + g][:, 0:nt], wg[:, g, k, :], h3[:, k, c0:c0 + nt], start=(k == 0), stop=(k == KT - 1))
                        pe_done.done(ins, "mg", l, n, g)
                    for g in range(2):
                        for k in range(NB):
                            rhs = pr[:, 2 + 3 * k, c0:c0 + nt] if g == 0 else ya[:, k, c0:c0 + nt]
                            ins = mm(bank[st + 2 + g][:, 0:nt], wb[:, g, k, :], rhs, start=(k == 0), stop=(k == NB - 1))
                        pe_done.done(ins, "mb", l, n, g)
                    item_done()
                for n in range(2):
                    w = next_item()[:, :].rearrange("p (j k c) -> p j k c", j=4, k=KT)
                    for j in range(4):
                        di = 4 * n + j
                        if di == 0:
                            need(dve_done, "merge", l, KT - 1)
                        if di >= 2:
                            need(dve_done, "res1", l, di - 2)
                        for k in range(KT):
                            ins = mm(bank[di % 2][:, 0:nt], w[:, j, k, :], wk(4096 + 512 * k, nt), start=(k == 0), stop=(k == KT - 1))
                        pe_done.done(ins, "wo", l, di)
                    item_done()
                for k in range(KT):
                    need(act_done, "sq2", l, k)
                    if k == 0:
                        need(dve_done, "res1", l, KT - 1)
                    ins = mm(bank[0][:, 0:nt], C("mean"), wk(8192 + 512 * k, nt), start=(k == 0), stop=(k == KT - 1))
                pe_done.done(ins, "ms2", l)
                need(act_done, "h2", l)
                need(dve_done, "h2", l)
                if l == 0:
                    for n in range(11):
                        w = next_item()[:, :].rearrange("p (j k c) -> p j k c", j=4, k=KT)
                        for j in range(4):
                            f, g = 2 * n + j // 2, j % 2
                            if f >= 2 and g == 0:
                                need(dve_done, "hff", f - 2)
                            for k in range(KT):
                                ins = mm(bank[2 * (f % 2) + g][:, :], w[:, j, k, :], h3[:, k, :], start=(k == 0), stop=(k == KT - 1))
                            pe_done.done(ins, "gu", f, g)
                        item_done()
                    for n in range(KT):
                        w = next_item()[:, 0:2816].rearrange("p (k c) -> p k c", k=NFF)
                        if n == 0:
                            need(dve_done, "hff", NFF - 1)
                        if n >= 2:
                            need(dve_done, "res2", n - 2)
                        for k in range(NFF):
                            ins = mm(bank[n % 2][:, :], w[:, k, :], wk(4096 + 512 * k, 512), start=(k == 0), stop=(k == NFF - 1))
                        pe_done.done(ins, "dn", n)
                        item_done()
                else:
                    w = next_item()[:, 0:64].rearrange("p (k e) -> p k e", k=KT)
                    for tb in range(2):
                        for k in range(KT):
                            ins = mm(bank[1][:, 8 * tb:8 * tb + 8], h3[:, k, CTX + P * tb:CTX + P * tb + P], w[:, k, :],
                                     start=(k == 0), stop=(k == KT - 1))
                    pe_done.done(ins, "logits")
                    item_done()
                    for tb in range(2):
                        for g in range(2):
                            for k in range(4):
                                ins = pe.transpose(bank[4 + 2 * tb + g][:, 128 * k:128 * k + 128],
                                                   h3[:, 4 * g + k, CTX + P * tb:CTX + P * tb + P], ident)
                            pe_done.done(ins, "htok", tb, g)
                    need(dve_done, "mask")
                    rmask = rt[:, 0:16].rearrange("p (t e) -> p t e", t=2)
                    mm(bank[0][:, 0:8], C("before"), rmask[:, 0, :]).then_inc(X["wused"], 1)
                    mm(bank[0][:, 8:16], C("before"), rmask[:, 1, :], stop=False).then_inc(X["wused"], 1)
                    mm(bank[0][:, 8:16], C("ones"), rmask[:, 0, :], start=False).then_inc(X["wused"], 1)
                    mm(bank[0][:, 16:24], C("ones"), rmask[:, 0, :], stop=False)
                    pe_done.done(mm(bank[0][:, 16:24], C("ones"), rmask[:, 1, :], start=False), "rank")
                    need(dve_done, "ctrl")
                    need(act_done, "htok", 1, 1)
                    need(dve_done, "gwt0")
                    jobs_here = pe.value_load(ctrl[0:1, NJ + 1:NJ + 2], min_val=NE, max_val=NJ)

                    def gather(j, g):
                        if g == 0:
                            pe.wait_ge(X["key"], j + 1)
                            if not isinstance(j, int):
                                pe.wait_ge(X["gtc"], j)
                        else:
                            pe.wait_ge(X["xl"], j * 2 + 1)
                        for k in range(4):
                            for tb in range(2):
                                ins = mm(bank[6][:, 128 * k:128 * k + 128], m_htok[:, tb, P * (4 * g + k):P * (4 * g + k) + P],
                                         m_G[:, tb, :], start=(tb == 0), stop=(tb == 1))
                        ins.then_inc(X["gat"], 1)

                    def scatter(j):
                        pe.wait_ge(X["yc"], j * 2 + 2)
                        pe.wait_ge(X["xl"], j * 2 + 2)
                        for g in range(4):
                            for k in range(2):
                                kk_ = 2 * g + k
                                ins = mm(bank[4 + g][:, 256 * k:256 * k + 256], m_y[:, P * kk_:P * kk_ + P], m_GwT)
                            ins.then_inc(X["sc"], 1)

                    for g in range(2):
                        gather(0, g)
                    for i in range(2):
                        ins = mm(bank[[5, 7][i]][:, :], m_GwT[:, 0:P], m_htok[:, 0, 0:512])
                    ins.then_inc(X["zero"], 1)
                    with pe.Fori(0, jobs_here) as j:
                        pe.wait_ge(X["xl"], j * 2 + 2)

                        def transposes(c):
                            pe.wait_ge(X["act"], j * EC + (c + 1))
                            if c >= 1:
                                pe.wait_ge(X["trl"], j * EC + c)
                            else:
                                pe.wait_ge(X["add"], j * 4 + 1)
                            for k in range(4):
                                ins = pe.transpose(bank[4][:, 128 * k:128 * k + 128], m_hid[:, c % 2, 128 * k:128 * k + 128], ident)
                            ins.then_inc(X["tr"], 1)

                        def parts(o_, x_hi, x_lo, wh, wl, first, last):
                            mm(o_, x_hi, wh, start=first, stop=False)
                            mm(o_, x_hi, wl, start=False, stop=False)
                            return mm(o_, x_lo, wh, start=False, stop=last)

                        for kind, c in order:
                            for half in range(2):
                                u = unit(kind, c, half)
                                if kind == "d" and half == 0:
                                    pe.wait_ge(X["trl"], j * EC + (c + 1))
                                    if c == 0:
                                        pe.wait_ge(X["add"], j * 4 + 4)
                                if kind == "g" and half == 0 and c >= 2:
                                    pe.wait_ge(X["act"], j * EC + (c - 1))
                                pe.wait_ge(X["lo"], count(j, u))
                                wh, wl = w_hi[:, u % WB, :], w_lo[:, u % WB, :]
                                if kind == "d":
                                    for k in range(2):
                                        kk_ = 2 * half + k
                                        for g in range(2):
                                            cs = slice(1024 * k + 512 * g, 1024 * k + 512 * g + 512)
                                            ins = parts([bank[5], bank[7]][g][:, :], hT_hi[:, c % 2, kk_, :], hT_lo[:, c % 2, kk_, :],
                                                        wh[:, cs], wl[:, cs], c == 0 and kk_ == 0, c == EC - 1 and kk_ == 3)
                                else:
                                    for k in range(4):
                                        kk_ = 4 * half + k
                                        cs = slice(512 * k, 512 * k + 512)
                                        ins = parts(bank[2 * (c % 2) + (kind == "u")][:, :], xg_hi[:, kk_, :], xg_lo[:, kk_, :],
                                                    wh[:, cs], wl[:, cs], kk_ == 0, kk_ == KT - 1)
                                ins.then_inc(X["wused"], 1)
                            if kind == "g" and c >= 1:
                                transposes(c - 1)
                            if (kind, c) == ("u", 0):
                                scatter(j)
                            if (kind, c) == ("d", 0):
                                for tb in range(2):
                                    ins = pe.transpose(bank[6][:, 128 * tb:128 * tb + 128], m_Gw[:, tb, :], ident)
                                ins.then_inc(X["gt"], 1)
                            if (kind, c) == ("u", EC - 1):
                                gather(j + 1, 0)
                            if (kind, c) == ("d", EC - 2):
                                transposes(EC - 1)
                                gather(j + 1, 1)
                    scatter(jobs_here)

        @block.scalar
        def _(act):
            seen = {}

            def need(sig, *key):
                n = sig.count(*key)
                if seen.get(sig.name, 0) < n:
                    seen[sig.name] = n
                    act.wait_ge(sig.sem, n)

            def af(o_, i_, f, *key, **kw):
                act_done.done(act.activation(o_, i_, f, **kw), *key)

            def own():
                act.wait_ge(act_done.sem, act_done.n)

            act.dma_start(co[:, :], a["consts"]).then_inc(const_loaded, 16)
            act.dma_start(rstd[:, 0:16], a["c"]).then_inc(c_loaded, 16)
            need(dve_done, "eps")
            act.wait_ge(c_loaded, 16)
            cs3 = csil[:, :].rearrange("p (k c) -> p k c", k=KT)
            af(cs3[:, :, 0:2], rstd[:, 0:16].rearrange("p (k c) -> p k c", k=KT), ACT.Silu, "csil")
            for l in range(L):
                if l:
                    need(dve_done, "ffn", 0)
                act.dma_start(pv[:, :], a["pv"][l]).then_inc(par_loaded, 16)
                act.dma_start(mw[:, :], a["mw"][l]).then_inc(mw_loaded, 16)
                for n in range(12):
                    need(pe_done, "modrow", l, n)
                    af(wk(512 * n, 512), bank[n % 2][:, :], ACT.Copy, "modrow", l, n)
                need(pe_done, "modt", l, 11)
                act.dma_start(x3, a["x"] if l == 0 else x_mid).then_inc(x_loaded, 16)
                act.wait_ge(x_loaded, 16 * (2 * l + 1))
                for k in range(KT):
                    af(wk(4096 + 512 * k, 512), x3[:, k, :], ACT.Square, "sq1", l, k)
                need(pe_done, "ms1", l)
                af(rstd[:, :], bank[0][:, :], ACT.Sqrt, "rms1", l, bias=small[:, 240:241])
                need(dve_done, "xr1", l)
                for k in range(KT):
                    af(h3[:, k, 0:CTX], h3[:, k, 0:CTX], ACT.Identity, *(("h1", l) if k == KT - 1 else ()),
                       scale=nrm[:, 2 * k + 1:2 * k + 2], bias=modv[:, k, 1:2])
                need(dve_done, "h1", l)
                for bi in range(20):
                    need(pe_done, "proj", l, bi)
                    if 2 <= bi < 8:
                        src = [4, 5, 0, 1, 2, 3][bi - 2]
                        af(att[:, src, :], bank[bi % 4][:, :], ACT.Copy, "proj", l, bi)
                    else:
                        m = bi if bi < 2 else bi - 6
                        if m >= 2:
                            need(dve_done, "shift", l, m - 2)
                        pad = wk(8192 + 516 * (m % 2), 516, 2)
                        af(pad[:, :, 1:257], bank[bi % 4][:, :].rearrange("p (a b) -> p a b", a=2), ACT.Copy, "proj", l, bi)
                need(dve_done, "shift", l, 1)
                own()
                af(pr[0:64, 0, :], pr[0:64, 0, :], ACT.Tanh, "tanh", l)
                af(pr[:, 1, :], pr[:, 1, :], ACT.Sigmoid, "glo", l)
                def q_rms(i):
                    need(pe_done, "qms", l, i)
                    if i >= 1:
                        need(dve_done, "qn", l, i - 1)
                    if i < 4:
                        af(rstd[:, :], bank[i % 2][:, :], ACT.Sqrt, "qrms", l, i, scale=float(HD), bias=small[:, 243:244])
                    else:
                        af(rstd[:, :], bank[i % 2][:, :], ACT.Sqrt, "qrms", l, i, bias=small[:, 240:241])

                for i in range(5):
                    own()
                    if i >= 2:
                        need(pe_done, "qms", l, i - 2)
                    if i >= 1:
                        q_rms(i - 1)
                    af(wk(3072 + 512 * (i % 2), 512), att[:, i, :], ACT.Square, "qsq", l, i)
                q_rms(4)
                need(pe_done, "vtok", l)
                af(wk(4096, 512), bank[4][:, :], ACT.Copy, "vtok", l)
                units = attention_units(l)
                for u in range(len(units) + 3):
                    if u < len(units):
                        b, hh, qb = units[u]
                        nk = key_blocks(qb)
                        need(dve_done, "max", l, u)
                        if u >= 3:
                            need(pe_done, "pT", l, u - 3)
                        af(probs(u, nk), score_bank(u)[:, 0:128 * nk], ACT.Exp, bias=soft(u)[:, 1:2], accum_out=soft(u)[:, 2:3])
                        af(soft(u)[:, 3:4], V("sink", b + 4 * hh), ACT.Exp, "exp", l, u, bias=soft(u)[:, 1:2])
                    if 2 <= u < len(units) + 2:
                        v = u - 2
                        nk = key_blocks(units[v][2])
                        need(pe_done, "pT", l, v)
                        if v >= 2:
                            need(pe_done, "pv", l, v - 2)
                        af(probs_T(v)[:, 0:128 * nk], bank[2 + v % 2][:, 0:128 * nk], ACT.Copy, "pT", l, v)
                    if u >= 3:
                        v = u - 3
                        b = units[v][0]
                        if v + 1 == len(units) or units[v + 1][0] != b:
                            need(pe_done, "pv", l, v)
                            c0_, n_ = cols(l)
                            af(ya[:, b, c0_:c0_ + n_], bank[4 + b % 2][:, c0_:c0_ + n_], ACT.Copy, "yatt", l, b)
                if l == 1:
                    need(pe_done, "vdown")
                    af(rstd[0:32, :], bank[7][0:32, :], ACT.Copy, "vdown")
                    for b in range(NB):
                        need(pe_done, "vup", b)
                        if b >= 2:
                            need(dve_done, "vres", b - 2)
                        af(wk(512 * (b % 2), 512), bank[7][:, :], ACT.Sigmoid, "vsig", b, bias=V("v0", b))
                def head(jn, i):
                    _, b, q = jn
                    if i == 0:
                        need(dve_done, "kkt", *jn)
                        af(j_sq, j_kkt, ACT.Square, "kksq", *jn)
                    if i == 1:
                        need(pe_done, "kkss", *jn)
                        af(j_rs, bank[6][:, 256:512], ACT.Sqrt, "kkrms", *jn, bias=small[:, 241:242])
                    if i == 2:
                        need(pe_done, "lora", *jn)
                        for d in range(2):
                            af(j_lw[:, d, :], bank[7][:, 256 * d:256 * d + 256], ACT.Sigmoid, bias=V("w0", 4 * d + b))
                        for d in range(2):
                            af(j_ic[:, d, :], bank[6][:, 256 * d:256 * d + 256], ACT.Sigmoid, "sig", *jn, bias=V("a0", 4 * d + b))
                    if i == 3:
                        need(dve_done, "cum", *jn)
                        af(jj_P[turn(jn)], j_L, ACT.Exp)
                        af(j_Q, j_L, ACT.Exp, "decay", *jn, scale=-1.0)

                def spread(jn, c):
                    _, b, q = jn
                    if c == 2:
                        for h in range(2):
                            af(j_v[64 * h:64 * h + 64, :, 64 * h:64 * h + 64],
                               pr[64 * h:64 * h + 64, 4 + 3 * b, 256 * q:256 * q + 256].rearrange("p (c t) -> p c t", c=4), ACT.Copy)
                    if c == 3:
                        need(dve_done, "kr", *jn)
                        for h in range(2):
                            af(jj_kap[turn(jn)][64 * h:64 * h + 64, :, 64 * h:64 * h + 64], jj_kr[turn(jn)][64 * h:64 * h + 64, :, 0, :],
                               ACT.Copy, "bd", *jn)

                def post(jn, i):
                    if not emits(jn):
                        return
                    if i == 0:
                        need(dve_done, "yc", *jn)
                        af(j_sqp, j_Y, ACT.Square, "ysq", *jn)
                    if i == 1:
                        need(pe_done, "yvar", *jn)
                        af(j_rsp, bank[7][:, 256:512], ACT.Sqrt, "yrms", *jn, bias=small[:, 242:243])

                first = layer_jobs(l)[0][0]
                need(pe_done, "proj", l, 19)
                if l == 1:
                    need(pe_done, "vdown")
                act.dma_start(h_mid, hbuf[:, :]).then_inc(h_stored, 16)
                act.wait_ge(h_stored, 16 * (l + 1))
                act.sem_inc(h_free, 1)
                need(dve_done, "ready", l)
                need(pool_done, "zeroed", l)
                for i in range(4):
                    head(first, i)
                for c in range(4):
                    spread(first, c)
                for jn, prev, nxt in layer_jobs(l):
                    b, q = jn[1:]
                    for n in range(5):
                        need(pe_done, "tok", *jn, n)
                        dst = [j_Kt[:, 0:4, :], j_Kt[:, 4:8, :], j_Bt[:, 0:4, :], j_Bt[:, 4:8, :], j_Vt[:, :, :]][n]
                        af(dst, bank[6 + n % 2][:, :].rearrange("p (a b) -> p a b", a=4), ACT.Copy, "tok", *jn, n)
                    for lv in range(1, 6):
                        for d in range(2):
                            need(pe_done, "x", *jn, lv, d)
                            af(j_X[:, 4 * d:4 * d + 4, :], bank[3 * d][:, :].rearrange("p (a b) -> p a b", a=4), ACT.Copy, "x", *jn, lv, d)
                        if prev is not None:
                            post(prev, lv - 1)
                        if nxt is not None:
                            head(nxt, lv - 1)
                    for c in range(NCH):
                        for d in range(2):
                            need(pe_done, "R", *jn, c, d)
                            af(j_R[:, d, :], bank[3 * d][:, 0:128], ACT.Copy, "R", *jn, c, d)
                        if nxt is not None:
                            spread(nxt, c)
                    if emits(jn):
                        need(pe_done, "y", *jn, NCH - 1, 1)
                        for h in range(2):
                            af(j_Y[64 * h:64 * h + 64, :].rearrange("p (c t) -> p c t", c=4),
                               bank[6][64 * h:64 * h + 64, :].rearrange("p (c h t) -> p c h t", c=4, h=2)[:, :, h, :], ACT.Copy, "y", *jn)
                for i in range(3):
                    post(jn, i)
                need(dve_done, "yrw", l)
                own()
                act.dma_start(hbuf[:, :], h_mid).then_inc(h_loaded, 16)
                c0, nt = cols(l)
                for n in range(KT):
                    st = 4 * (n % 2)
                    if n == 0:
                        need(dve_done, "yrw", l)
                    if n >= 2:
                        need(dve_done, "merge", l, n - 2)
                    for g in range(2):
                        need(pe_done, "mg", l, n, g)
                        af(wk(8192 + 512 * (2 * (n % 2) + g), nt), bank[st + g][:, 0:nt], ACT.Sigmoid, "mg", l, n, g)
                    if n == 0:
                        act.dma_start(x3, a["x"] if l == 0 else x_mid).then_inc(x_loaded, 16)
                need(dve_done, "merge", l, KT - 1)
                for k in range(KT):
                    need(dve_done, "res1", l, k)
                    af(wk(8192 + 512 * k, nt), x3[:, k, c0:c0 + nt], ACT.Square, "sq2", l, k)
                need(pe_done, "ms2", l)
                af(rstd[:, 0:nt], bank[0][:, 0:nt], ACT.Sqrt, "rms2", l, bias=small[:, 240:241])
                need(dve_done, "xr2", l)
                for k in range(KT):
                    v = 1 if l == 0 else 0
                    c_ = 0 if l == 0 else CTX
                    n_ = CTX if l == 0 else 128
                    af(h3[:, k, c_:c_ + n_], h3[:, k, c_:c_ + n_], ACT.Identity, *(("h2", l) if k == KT - 1 else ()),
                       scale=nrm[:, 16 + 2 * k + v:17 + 2 * k + v], bias=modv[:, 24 + k, v:v + 1])
                if l == 0:
                    for f in range(NFF):
                        need(pe_done, "gu", f, 0)
                        if f >= 2:
                            need(dve_done, "hff", f - 2)
                        af(wk(15360 + 512 * (f % 2), 512), bank[2 * (f % 2)][:, :], ACT.Silu, "silu", f)
                    need(dve_done, "ffn", 0)
                    act.dma_start(x_mid, x3).then_inc(x_stored, 16)
                    act.wait_ge(x_stored, 16)
                else:
                    for tb in range(2):
                        for g in range(2):
                            need(pe_done, "htok", tb, g)
                            af(m_htok[:, tb, 512 * g:512 * g + 512], bank[4 + 2 * tb + g][:, :], ACT.Copy, "htok", tb, g)
                    need(dve_done, "gap")
                    af(small[:, 32:34], small[:, 34:36], ACT.Exp, "gap")
                    need(dve_done, "ctrl")
                    jobs_here = act.value_load(ctrl[0:1, NJ + 1:NJ + 2], min_val=NE, max_val=NJ)

                    def gathered(j, g):
                        act.wait_ge(X["gat"], j * 2 + (g + 1))
                        act.activation(xg_hi[:, 4 * g:4 * g + 4, :], bank[6][:, :].rearrange("p (a b) -> p a b", a=4),
                                       ACT.Copy).then_inc(X["xg"], 1)

                    def outputs(j):
                        act.wait_ge(X["wused"], j * NU + WB)
                        for g in range(2):
                            act.activation(m_y[:, 512 * g:512 * g + 512], [bank[5], bank[7]][g][:, :], ACT.Copy).then_inc(X["yc"], 1)

                    for g in range(2):
                        gathered(0, g)
                    act.wait_ge(X["zero"], 1)
                    with act.Fori(0, jobs_here) as j:
                        def silu(c):
                            act.wait_ge(X["wused"], j * NU + (WB + unit("g", c, 1) + 1))
                            if c >= 2:
                                act.wait_ge(X["act"], j * EC + (c - 1))
                            act.activation(m_sil[:, c % 2, :], bank[2 * (c % 2)][:, :], ACT.Silu).then_inc(X["silu"], 1)

                        def tr(c):
                            act.wait_ge(X["tr"], j * EC + (c + 1))
                            act.activation(hT_hi[:, c % 2, :, :], bank[4][:, :].rearrange("p (a b) -> p a b", a=4), ACT.Copy)\
                               .then_inc(X["trc"], 1)

                        for m, (kind, c) in enumerate(order):
                            i = N_STATIC + m
                            act.wait_ge(ring_full[i % NS], j * (16 * EC) + 16 * (len(range(i % NS, i, NS)) + 1))
                            for half in range(2):
                                u = unit(kind, c, half)
                                act.wait_ge(X["wused"], count(j, u))
                                act.activation(w_hi[:, u % WB, :], slot(i)[:, UNIT * half:UNIT * half + UNIT], ACT.Copy).then_inc(X["hi"], 1)
                                if (kind, c, half) == ("g", 1, 0):
                                    silu(0)
                                if kind == "d" and half == 0:
                                    if c < EC - 1:
                                        silu(c + 1)
                            if kind == "u" and c >= 1:
                                tr(c - 1)
                            if (kind, c) == ("g", 0):
                                outputs(j)
                            if (kind, c) == ("u", 2):
                                act.wait_ge(X["gt"], j + 1)
                                act.activation(m_GwT, bank[6][:, 0:256], ACT.Copy).then_inc(X["gtc"], 1)
                            if (kind, c) == ("d", EC - 2):
                                gathered(j + 1, 0)
                        tr(EC - 1)
                        gathered(j + 1, 1)
                    outputs(jobs_here)

        @block.vector
        def _(dve):
            seen = {}

            def need(sig, *key):
                n = sig.count(*key)
                if seen.get(sig.name, 0) < n:
                    seen[sig.name] = n
                    dve.wait_ge(sig.sem, n)

            def dv(ins, *key, hold=True):
                dve_done.done(ins, *key)
                if hold:
                    dve.wait_ge(dve_done.sem, dve_done.n)

            tt = dve.tensor_tensor
            ts = dve.tensor_scalar
            stt = dve.scalar_tensor_tensor
            dv(dve.memset(csil[:, :], 0.0), "czero")
            for i, e_ in enumerate((EPS, 1e-12, GN_EPS, HD * EPS)):
                dv(dve.memset(small[:, 240 + i:241 + i], e_), "eps")
            dve.wait_ge(const_loaded, 16)
            for l in range(L):
                dve.wait_ge(par_loaded, 16 * (l + 1))
                need(pe_done, "modt", l, 11)
                bm = pv[:, PV["bmod"][0]:PV["bmod"][1]].unsqueeze(2).to_broadcast([P, 48, 2])
                dv(tt(modv, bank[2][:, 0:96].rearrange("p (m v) -> p m v", v=2), bm, ALU.add), "modt", l)
                for i, nn in enumerate(("norm1", "norm2")):
                    g_ = pv[:, PV[nn][0]:PV[nn][1]].unsqueeze(2).to_broadcast([P, KT, 2])
                    n3 = nrm[:, 16 * i:16 * i + 16].rearrange("p (k v) -> p k v", v=2)
                    sc_ = modv[:, 24 * i + 8:24 * i + 16, :]
                    dv(tt(n3, sc_, g_, ALU.mult))
                    dv(tt(n3, n3, g_, ALU.add))
                c0m = small[:, 64:78]
                mu0 = pv[:, PV["mu0"][0]:PV["mu0"][1]]
                mu1 = pv[:, PV["mu1"][0]:PV["mu1"][1]]
                dv(tt(c0m, mu0, mu1, ALU.add))
                dv(ts(c0m, c0m, -1.0, 1.0, ALU.mult, ALU.add))
                need(act_done, "rms1", l)
                dv(dve.reciprocal(rstd[:, :], rstd[:, :]))
                dve.wait_ge(x_loaded, 16 * (2 * l + 1))
                dv(tt(h3, x3, rstd[:, :].unsqueeze(1).to_broadcast([P, KT, T]), ALU.mult), "xr1", l)
                for k in range(KT):
                    dv(ts(h3[:, k, CTX:T], h3[:, k, CTX:T], nrm[:, 2 * k:2 * k + 1], modv[:, k, 0:1], ALU.mult, ALU.add),
                       *(("h1", l) if k == KT - 1 else ()), hold=False)
                for i in range(2):
                    pad = wk(8192 + 516 * i, 516, 2)
                    dv(dve.memset(pad[:, :, 0:1], 0.0), hold=False)
                    dv(dve.memset(pad[:, :, 257:258], 0.0))
                for m in range(14):
                    need(act_done, "proj", l, m if m < 2 else m + 6)
                    pad = wk(8192 + 516 * (m % 2), 516, 2)
                    o_ = pr[:, m, :].rearrange("p (a b) -> p a b", a=2)
                    dv(ts(o_, pad[:, :, 1:257], c0m[:, m:m + 1], None, ALU.mult))
                    dv(stt(o_, pad[:, :, 0:256], V("mu0", m), o_, ALU.mult, ALU.add))
                    dv(stt(o_, pad[:, :, 2:258], V("mu1", m), o_, ALU.mult, ALU.add), "shift", l, m)
                for i in range(5):
                    need(act_done, "qrms", l, i)
                    dv(dve.reciprocal(rstd[:, :], rstd[:, :]))
                    dv(stt(att[:, i, :], att[:, i, :], V("qn") if i < 4 else V("kn"), rstd[:, :], ALU.mult, ALU.mult), "qn", l, i)
                    need(pe_done, "qrot", l, i)
                    t_ = wk(9728, 256)
                    dv(tt(t_, bank[2 + i % 2][:, 0:256], C("sin"), ALU.mult))
                    dv(tt(att[:, i, CTX:T], att[:, i, CTX:T], C("cos"), ALU.mult))
                    dv(tt(att[:, i, CTX:T], att[:, i, CTX:T], t_, ALU.add), "qrot", l, i)
                units = attention_units(l)
                for u in range(len(units) + 1):
                    if u < len(units):
                        b, hh, qb = units[u]
                        need(pe_done, "score", l, u)
                        dv(dve.tensor_reduce(soft(u)[:, 0:1], score_bank(u)[:, 0:128 * key_blocks(qb)], AX.X, ALU.max))
                        dv(ts(soft(u)[:, 1:2], soft(u)[:, 0:1], V("sink", b + 4 * hh), -1.0, ALU.max, ALU.mult), "max", l, u)
                    if u >= 1:
                        v = u - 1
                        need(act_done, "exp", l, v)
                        dv(tt(soft(v)[:, 4:5], soft(v)[:, 2:3], soft(v)[:, 3:4], ALU.add))
                        dv(dve.reciprocal(soft(v)[:, 5:6], soft(v)[:, 4:5]))
                        p_ = probs(v, key_blocks(units[v][2]))
                        dv(ts(p_, p_, soft(v)[:, 5:6], None, ALU.mult), "prob", l, v)
                if l == 1:
                    for b in range(NB):
                        need(act_done, "vsig", b)
                        dve.wait_ge(vf_loaded, 16)
                        v_ = pr[:, 4 + 3 * b, :]
                        t_ = wk(1024, 512)
                        dv(tt(t_, wk(2048 + 512 * b, 512), v_, ALU.subtract))
                        dv(tt(t_, t_, wk(512 * (b % 2), 512), ALU.mult))
                        dv(tt(v_, v_, t_, ALU.add), "vres", b)
                need(act_done, "glo", l)
                need(act_done, "yatt", l, NB - 1)
                need(pool_done, "zeroed", l)
                dve.wait_ge(h_free, l + 1)
                dv(dve.memset(wk(*J["S"]), 0.0), "ready", l)
                c4 = lambda ap: ap.rearrange("p (c t) -> p c t", c=4)

                def rkv(jn):
                    _, b, q = jn
                    return (pr[:, 2 + 3 * b + i, 256 * q:256 * q + 256] for i in range(3))

                def head(jn, i):
                    _, b, q = jn
                    r_, k_, v_ = rkv(jn)
                    j_cv = jj_cv[turn(jn)]
                    if i == 0:
                        dv(ts(j_kkt, k_, V("kk", b), None, ALU.mult), "kkt", *jn)
                    if i == 1:
                        need(act_done, "kkrms", *jn)
                        dv(dve.reciprocal(j_rs, j_rs))
                        dv(tt(j_kk, j_kkt, j_rs, ALU.mult))
                    if i == 2:
                        need(act_done, "sig", *jn)
                        dv(ts(j_lw, j_lw, DECAY, None, ALU.mult))
                        for d in range(2):
                            for c in range(4):
                                o_, i_ = j_L[:, d, CH * c:CH * c + CH], j_lw[:, d, CH * c:CH * c + CH]
                                if d:
                                    o_, i_ = o_[:, ::-1], i_[:, ::-1]
                                dv(dve.tensor_tensor_scan(out=o_, data0=i_, data1=i_, initial=0.0, op0=ALU.add, op1=ALU.bypass),
                                   *(("cum",) + jn if (d, c) == (1, 3) else ()), hold=(d, c) == (1, 3))
                    if i == 3:
                        dv(ts(j_kh, j_ic, 1.0, V("ka", b), ALU.subtract, ALU.mult))
                        k2 = k_.unsqueeze(1).to_broadcast([P, 2, 256])
                        dv(stt(j_kh, j_kh, 1.0, k2, ALU.add, ALU.mult))
                        dv(tt(j_rs, j_kh[:, 0, :], j_kh[:, 1, :], ALU.add))
                        dv(stt(j_rs, j_rs, V("rk", b), r_, ALU.mult, ALU.mult), "coef", *jn)
                        dv(tt(j_bb, j_ic, j_kk.unsqueeze(1).to_broadcast([P, 2, 256]), ALU.mult), "bb", *jn)
                    if i == 4:
                        need(pe_done, "coef", *jn)
                        dv(tt(j_cv, bank[7][:, 0:256], v_, ALU.mult), "cv", *jn)

                def spread(jn, c):
                    r_, k_, v_ = rkv(jn)
                    if c == 0:
                        need(act_done, "decay", *jn)
                        for h in range(2):
                            hs = slice(64 * h, 64 * h + 64)
                            s8 = lambda ap: ap.rearrange("p d (c t) -> p (d c) t", c=4)
                            dv(tt(j_K[hs, :, hs], s8(j_kh[hs, :, :]), s8(j_Q[hs, :, :]), ALU.mult), *(("bd",) + jn if h else ()), hold=False)
                    if c in (1, 2):
                        d = c - 1
                        kkc = c4(j_kk)
                        Pd = c4(jj_P[turn(jn)][:, d, :])
                        kr = jj_kr[turn(jn)]
                        dv(tt(kr[:, 4 * d:4 * d + 4, 1, :], c4(r_), Pd, ALU.mult), hold=False)
                        if d == 0:
                            dv(tt(kr[:, 0:4, 0, 1:64], kkc[:, :, 1:64], Pd[:, :, 0:63], ALU.mult), hold=False)
                            dv(dve.tensor_copy(kr[:, 0:4, 0, 0:1], kkc[:, :, 0:1]), hold=False)
                        else:
                            dv(tt(kr[:, 4:8, 0, 0:63], kkc[:, :, 0:63], Pd[:, :, 1:64], ALU.mult), hold=False)
                            dv(dve.tensor_copy(kr[:, 4:8, 0, 63:64], kkc[:, :, 63:64]), "kr", *jn, hold=False)

                def post(jn, i):
                    _, b, q = jn
                    if not emits(jn):
                        return
                    if i == 0:
                        need(pe_done, "ymean", *jn)
                        dv(tt(j_Y, j_Y, bank[7][:, 0:256], ALU.subtract), "yc", *jn)
                    if i == 2:
                        need(act_done, "yrms", *jn)
                        dv(dve.reciprocal(j_rsp, j_rsp))
                        dv(tt(j_Y, j_Y, j_rsp, ALU.mult))
                        dv(ts(j_Y, j_Y, V("lg", b), V("lb", b), ALU.mult, ALU.add))
                        dv(tt(j_Y, j_Y, jj_cv[turn(jn)], ALU.add))
                        need(pe_done, "gate", *jn)
                        r_, _, _ = rkv(jn)
                        dv(tt(r_, j_Y, bank[6][:, 0:256], ALU.mult), "post", *jn)

                first = layer_jobs(l)[0][0]
                for i in range(5):
                    head(first, i)
                for c in range(4):
                    spread(first, c)
                for jn, prev, nxt in layer_jobs(l):
                    b, q = jn[1:]
                    emit = emits(jn)
                    j_P = jj_P[turn(jn)]
                    if q == 0 and b:
                        dv(dve.memset(wk(*J["S"]), 0.0), hold=False)
                    for w_ in range(2):
                        for sp_ in range(4):
                            need(pe_done, "gram", *jn, w_, sp_)
                            d = sp_ // 2
                            g5 = bank[4 * w_ + sp_][:, :].rearrange("p (s h r t) -> p s h r t", s=2, h=2, r=2)
                            for r2, (dst, msk) in enumerate(((j_Lk, strict), (j_Qk, incl)) if w_ == 0 else ((j_U, strict), (j_Qb, incl))):
                                if r2 == 1 and not emit:
                                    continue
                                dv(tt(dst[:, 2 * sp_:2 * sp_ + 2, :].rearrange("p s (h t) -> p s h t", h=2), g5[:, :, :, r2, :],
                                      msk[:, d, :].rearrange("p (h t) -> p h t", h=2).unsqueeze(1).to_broadcast([P, 2, 2, 64]), ALU.mult),
                                   "gram", *jn, w_, sp_, hold=False)
                    idb = ident.unsqueeze(1).to_broadcast([P, 4, 128])
                    for lv in range(6):
                        for d in range(2):
                            N_, M_ = j_N[:, 4 * d:4 * d + 4, :], j_M[:, 4 * d:4 * d + 4, :]
                            if lv == 0:
                                need(pool_done, "um", *jn, lv, d)
                                dv(stt(N_, j_Um[:, 4 * d:4 * d + 4, :], -1.0, idb, ALU.mult, ALU.add), hold=False)
                                need(pe_done, "x", *jn, lv, d)
                                need(pe_done, "tok", *jn, 1)
                                dv(stt(M_, bank[3 * d][:, :].rearrange("p (a b) -> p a b", a=4), -1.0, idb, ALU.mult, ALU.add),
                                   "mn", *jn, lv, d, hold=d == 1)
                            else:
                                need(pe_done, "mn", *jn, lv, d)
                                if lv < 5:
                                    dv(tt(M_, M_, bank[3 * d + 1][:, :].rearrange("p (a b) -> p a b", a=4), ALU.subtract), hold=False)
                                dv(tt(N_, N_, bank[3 * d + 2][:, :].rearrange("p (a b) -> p a b", a=4), ALU.subtract), "mn", *jn, lv, d,
                                   hold=d == 1)
                        if lv and prev is not None:
                            post(prev, lv - 1)
                        if lv and nxt is not None:
                            head(nxt, lv - 1)
                    for c in range(NCH):
                        for d in range(2):
                            need(pe_done, "U", *jn, c, d)
                            dv(ts(j_Un[:, d, :], bank[3 * d][:, 128:256], -1.0, None, ALU.mult), "U", *jn, c, d, hold=False)
                        for d in range(2):
                            need(pe_done, "state", *jn, c, d)
                            ch = c if d == 0 else NCH - 1 - c
                            last = CH * ch + (CH - 1 if d == 0 else 0)
                            dv(tt(j_S[:, d, :], j_S[:, d, :], bank[3 * d][:, 256:384], ALU.add))
                            dv(ts(j_S[:, d, :], j_S[:, d, :], j_P[:, d, last:last + 1], None, ALU.mult), "state", *jn, c, d)
                        if nxt is not None:
                            spread(nxt, c)
                for i in range(3):
                    post(jn, i)
                dve_done.book[("dve", "yrw", l)] = dve_done.n
                c0, nt = cols(l)
                for n in range(KT):
                    st = 4 * (n % 2)
                    s0, s1 = (wk(8192 + 512 * (2 * (n % 2) + g), nt) for g in range(2))
                    m_ = wk(4096 + 512 * n, nt)
                    need(act_done, "mg", l, n, 1)
                    need(pe_done, "mb", l, n, 1)
                    dv(tt(m_, bank[st + 2][:, 0:nt], s0, ALU.mult), hold=False)
                    dv(tt(s1, bank[st + 3][:, 0:nt], s1, ALU.mult))
                    dv(tt(m_, m_, s1, ALU.add), "merge", l, n)
                dve.wait_ge(x_loaded, 16 * (2 * l + 2))
                spans = [(0, CTX, 1), (CTX, LAT, 0)] if l == 0 else [(CTX, LAT, 0)]
                for n in range(KT):
                    need(pe_done, "wo", l, n)
                    for s0_, n_, v in spans:
                        dv(stt(x3[:, n, s0_:s0_ + n_], bank[n % 2][:, s0_ - c0:s0_ - c0 + n_], modv[:, 16 + n, v:v + 1],
                               x3[:, n, s0_:s0_ + n_], ALU.mult, ALU.add), "res1", l, n, hold=False)
                need(act_done, "rms2", l)
                dv(dve.reciprocal(rstd[:, 0:nt], rstd[:, 0:nt]))
                dv(tt(h3[:, :, c0:c0 + nt], x3[:, :, c0:c0 + nt], rstd[:, 0:nt].unsqueeze(1).to_broadcast([P, KT, nt]), ALU.mult), "xr2", l)
                for k in range(KT):
                    a0_, n_ = (CTX, LAT) if l == 0 else (CTX + 128, 128)
                    dv(ts(h3[:, k, a0_:a0_ + n_], h3[:, k, a0_:a0_ + n_], nrm[:, 16 + 2 * k:17 + 2 * k], modv[:, 24 + k, 0:1], ALU.mult, ALU.add),
                       *(("h2", l) if k == KT - 1 else ()), hold=False)
                if l == 0:
                    for f in range(NFF):
                        need(act_done, "silu", f)
                        need(pe_done, "gu", f, 1)
                        dv(tt(wk(4096 + 512 * f, 512), bank[2 * (f % 2) + 1][:, :], wk(15360 + 512 * (f % 2), 512), ALU.mult), "hff", f, hold=False)
                    for n in range(KT):
                        need(pe_done, "dn", n)
                        for s0_, n_, v in spans:
                            dv(stt(x3[:, n, s0_:s0_ + n_], bank[n % 2][:, s0_:s0_ + n_], modv[:, 40 + n, v:v + 1],
                                   x3[:, n, s0_:s0_ + n_], ALU.mult, ALU.add), "res2", n)
                    dve_done.book[("dve", "ffn", 0)] = dve_done.n
                    continue
                need(pe_done, "logits")
                lg = small[:, 96:112].rearrange("p (t e) -> p t e", t=2)
                top = small[:, 112:128].rearrange("p (t e) -> p t e", t=2)
                dv(dve.tensor_copy(lg, bank[1][:, 0:16].rearrange("p (t e) -> p t e", t=2)))
                ti = tidx[:, :].rearrange("p (t e) -> p t e", t=2)
                for tb in range(2):
                    dv(dve.max(top[:, tb, :], lg[:, tb, :]))
                    dv(dve.max_index(ti[:, tb, :], top[:, tb, :], lg[:, tb, :]))
                tf = small[:, 128:144].rearrange("p (t e) -> p t e", t=2)
                dv(dve.tensor_copy(tf, ti))
                dv(tt(small[:, 34:36].unsqueeze(2), top[:, :, 1:2], top[:, :, 0:1], ALU.subtract), "gap")
                mask = rt[:, 0:16].rearrange("p (t e) -> p t e", t=2)
                w8 = rt[:, 16:32].rearrange("p (t e) -> p t e", t=2)
                one1 = rt[:, 32:48].rearrange("p (t e) -> p t e", t=2)
                iota = C("iota")
                for tb in range(2):
                    dv(ts(one1[:, tb, :], iota[:, 0:8], tf[:, tb, 0:1], None, ALU.is_equal))
                    dv(ts(w8[:, tb, :], iota[:, 0:8], tf[:, tb, 1:2], None, ALU.is_equal))
                dv(tt(mask, one1, w8, ALU.add), "mask")
                need(act_done, "gap")
                dv(ts(small[:, 36:38], small[:, 32:34], 1.0, None, ALU.add))
                dv(dve.reciprocal(small[:, 38:40], small[:, 36:38]))
                dv(tt(small[:, 40:42], small[:, 32:34], small[:, 38:40], ALU.mult))
                for tb in range(2):
                    dv(ts(w8[:, tb, :], w8[:, tb, :], small[:, 40 + tb:41 + tb], None, ALU.mult))
                    dv(stt(w8[:, tb, :], one1[:, tb, :], small[:, 38 + tb:39 + tb], w8[:, tb, :], ALU.mult, ALU.add))
                need(pe_done, "rank")
                keys = rt[:, 48:80].rearrange("p (t e) -> p t e", t=2)
                wts = rt[:, 80:112].rearrange("p (t e) -> p t e", t=2)
                dv(dve.memset(rt[:, 48:112], 0.0))
                rank = bank[0][:, 0:16].rearrange("p (t e) -> p t e", t=2)
                dv(tt(keys[:, :, 0:8], rank, mask, ALU.mult))
                dv(ts(one1, mask, 1.0, 1e4, ALU.subtract, ALU.mult))
                dv(tt(keys[:, :, 0:8], keys[:, :, 0:8], one1, ALU.add))
                dv(dve.tensor_copy(wts[:, :, 0:8], w8))
                over = rt[:, 112:120]
                place = rt[:, 120:128]
                dv(ts(over, bank[0][:, 16:24], 128.5, None, ALU.is_gt))
                dv(dve.tensor_tensor_scan(out=place, data0=over, data1=over, initial=0.0, op0=ALU.add, op1=ALU.bypass))
                for i in range(3):
                    sel = rt[:, 128:136]
                    dv(ts(sel, place, float(i + 1), None, ALU.is_equal))
                    dv(tt(sel, sel, over, ALU.mult))
                    dv(tt(rt[:, 136:144], sel, iota[:, 0:8], ALU.mult))
                    dv(dve.tensor_reduce(rt[:, 144 + i:145 + i], rt[:, 136:144], AX.X, ALU.add))
                    for tb in range(2):
                        dv(stt(rt[:, 136:144], keys[:, tb, 0:8], -128.0, sel, ALU.add, ALU.mult))
                        dv(dve.tensor_reduce(keys[:, tb, 8 + i:9 + i], rt[:, 136:144], AX.X, ALU.add))
                        dv(tt(rt[:, 136:144], w8[:, tb, :], sel, ALU.mult))
                        dv(dve.tensor_reduce(wts[:, tb, 8 + i:9 + i], rt[:, 136:144], AX.X, ALU.add))
                dv(dve.memset(ctrl[0:1, :], 0))
                dv(dve.tensor_copy(ctrl[0:1, 8:11], rt[0:1, 144:147]))
                dv(dve.tensor_copy(ctrl[0:1, NJ:NJ + 1], place[0:1, 7:8]))
                dv(ts(rt[0:1, 150:151], place[0:1, 7:8], float(NE), None, ALU.add))
                dv(dve.tensor_copy(ctrl[0:1, NJ + 1:NJ + 2], rt[0:1, 150:151]), "ctrl")
                dv(dve.memset(m_GwT, 0.0), "gwt0")
                jobs_here = dve.value_load(ctrl[0:1, NJ + 1:NJ + 2], min_val=NE, max_val=NJ)

                def one_hot(j):
                    for tb in range(2):
                        dve.tensor_scalar(m_G[:, tb, :], iota, keys[:, tb, bass.ds(j, 1)], None, ALU.is_equal).then_inc(X["key2"], 1)
                    dve.wait_ge(X["key2"], j * 2 + 2)
                    for tb in range(2):
                        ins = dve.tensor_scalar(m_Gw[:, tb, :], m_G[:, tb, :], wts[:, tb, bass.ds(j, 1)], None, ALU.mult)
                    ins.then_inc(X["key"], 1)

                def gathered(j, g):
                    dve.wait_ge(X["xg"], j * 2 + (g + 1))
                    dve.tensor_tensor(xg_lo[:, 4 * g:4 * g + 4, :], bank[6][:, :].rearrange("p (a b) -> p a b", a=4),
                                      xg_hi[:, 4 * g:4 * g + 4, :].bitcast(f32), ALU.subtract).then_inc(X["xl"], 1)

                def scattered(j):
                    for g in range(4):
                        dve.wait_ge(X["sc"], j * 4 + (g + 1))
                        if g == 0:
                            dve.wait_ge(X["add"], j * 4)
                        for k in range(2):
                            kk_ = 2 * g + k
                            ins = dve.scalar_tensor_tensor(x3[:, kk_, CTX:T], bank[4 + g][:, 256 * k:256 * k + 256], modv[:, 40 + kk_, 0:1],
                                                           x3[:, kk_, CTX:T], ALU.mult, ALU.add)
                        ins.then_inc(X["add"], 1)

                one_hot(0)
                for g in range(2):
                    gathered(0, g)
                with dve.Fori(0, jobs_here) as j:
                    def hidden(c):
                        dve.wait_ge(X["silu"], j * EC + (c + 1))
                        dve.wait_ge(X["wused"], j * NU + (WB + unit("u", c, 1) + 1))
                        if c >= 2:
                            dve.wait_ge(X["tr"], j * EC + (c - 1))
                        dve.tensor_tensor(m_hid[:, c % 2, :], bank[2 * (c % 2) + 1][:, :], m_sil[:, c % 2, :], ALU.mult).then_inc(X["act"], 1)

                    def tr(c):
                        dve.wait_ge(X["trc"], j * EC + (c + 1))
                        dve.tensor_tensor(hT_lo[:, c % 2, :, :], bank[4][:, :].rearrange("p (a b) -> p a b", a=4),
                                          hT_hi[:, c % 2, :, :].bitcast(f32), ALU.subtract).then_inc(X["trl"], 1)

                    for m, (kind, c) in enumerate(order):
                        for half in range(2):
                            u = unit(kind, c, half)
                            dve.wait_ge(X["hi"], count(j, u))
                            dve.tensor_tensor(w_lo[:, u % WB, :], slot(N_STATIC + m)[:, UNIT * half:UNIT * half + UNIT],
                                              w_hi[:, u % WB, :].bitcast(f32), ALU.subtract).then_inc(X["lo"], 1)
                        if kind == "g" and c >= 1:
                            hidden(c - 1)
                        if kind == "u" and c >= 1:
                            tr(c - 1)
                        if (kind, c) == ("g", 1):
                            scattered(j)
                        if (kind, c) == ("u", 3):
                            dve.wait_ge(X["gt"], j + 1)
                            one_hot(j + 1)
                        if (kind, c) == ("d", EC - 2):
                            gathered(j + 1, 0)
                            hidden(EC - 1)
                    tr(EC - 1)
                    gathered(j + 1, 1)
                scattered(jobs_here)
                dve.wait_ge(X["add"], jobs_here * 4 + 4)
                dv(dve.tensor_copy(small[:, 200:201], small[:, 34:35]), "final")

        @block.gpsimd
        def _(pool):
            seen = {}

            def need(sig, *key):
                n = sig.count(*key)
                if seen.get(sig.name, 0) < n:
                    seen[sig.name] = n
                    pool.wait_ge(sig.sem, n)

            for l in range(L):
                if l == 0:
                    need(dve_done, "shift", 0, 13)
                    for b in range(NB):
                        pool.dma_start(vf_mid[:, b, :], pr[:, 4 + 3 * b, :]).then_inc(vf_stored, 16)
                    pool.wait_ge(vf_stored, 16 * NB)
                    need(act_done, "yatt", 0, NB - 1)
                else:
                    need(act_done, "yatt", 1, NB - 1)
                    pool.dma_start(wk(2048, 2048, NB), vf_mid).then_inc(vf_loaded, 16)
                    need(dve_done, "vres", NB - 1)
                pool.wait_ge(h_free, l + 1)
                for v_ in (wk(*J["kapbd"]), hb(1024, 1024), wk(*J["Kbd"]), wk(*J["Bbd"]), wk(*J["vbd"])):
                    pool_done.done(pool.memset(v_, 0.0), "zeroed", l)
                pool.wait_ge(pool_done.sem, pool_done.n)

                def spread(jn):
                    need(dve_done, "bb", *jn)
                    need(act_done, "decay", *jn)
                    for h in range(2):
                        hs = slice(64 * h, 64 * h + 64)
                        s8 = lambda ap: ap.rearrange("p d (c t) -> p (d c) t", c=4)
                        pool_done.done(pool.tensor_tensor(j_B[hs, :, hs], s8(j_bb[hs, :, :]), s8(j_Q[hs, :, :]), ALU.mult), "bd", *jn)

                spread(layer_jobs(l)[0][0])
                for jn, prev, nxt in layer_jobs(l):
                    for lv in range(6):
                        for d in range(2):
                            if lv == 0:
                                need(dve_done, "gram", *jn, 1, 2 * d + 1)
                            else:
                                need(pe_done, "x", *jn, lv - 1, d)
                                if lv == 1:
                                    need(dve_done, "mn", *jn, 0, d)
                            pool_done.done(pool.tensor_tensor(j_Um[:, 4 * d:4 * d + 4, :], j_U[:, 4 * d:4 * d + 4, :],
                                                              level[:, 2 * lv + d, :].unsqueeze(1).to_broadcast([P, 4, 128]), ALU.mult),
                                           "um", *jn, lv, d)
                    if nxt is not None:
                        need(pe_done, "mn", *jn, 5, 1)
                        spread(nxt)
    return book


_OUT = (P, KT, LAT)


def kernel(**inputs):
    import numpy as _np
    import concourse.bacc as _bacc
    from concourse import mybir as _mybir
    from concourse.bass_utils import run_bass_kernel_spmd as _run

    arrays = lay_out({k: _np.asarray(v) for k, v in inputs.items()})
    book = {}
    for _ in range(2):
        nc = _bacc.Bacc("TRN2", target_bir_lowering=False, num_devices=1)
        f32 = _mybir.dt.float32
        aps = {n: nc.dram_tensor("in_" + n, v.shape, f32, kind="ExternalInput").ap() for n, v in arrays.items()}
        out = nc.dram_tensor("out_0", _OUT, f32, kind="ExternalOutput").ap()
        x_mid = nc.dram_tensor("x_mid", (P, KT, T), f32, kind="Internal").ap()
        vf_mid = nc.dram_tensor("vf_mid", (P, NB, T), f32, kind="Internal").ap()
        h_mid = nc.dram_tensor("h_mid", (P, KT * T), f32, kind="Internal").ap()
        build(nc, aps, out, x_mid, vf_mid, h_mid, book)
    r = _run(nc, [{"in_" + n: v for n, v in arrays.items()}], core_ids=[0])
    y = r.results[0]["out_0"]
    return _np.ascontiguousarray(y.transpose(2, 1, 0).reshape(1, LAT, D))


def lay_out(i):
    c32 = np.ascontiguousarray

    def kp(w):
        s = w.shape
        w = w.reshape(s[:-2] + (s[-2] // P, P, s[-1]))
        return np.swapaxes(w, -3, -2)

    def blocks(w, n):
        w = kp(w)
        return w.reshape(P, w.shape[1], n, P).transpose(0, 2, 1, 3)

    o = {}
    x = np.concatenate([i["ctx"][0], i["x"][0]], 0)
    o["x"] = c32(x.T.reshape(KT, P, T).transpose(1, 0, 2))
    c = np.stack([i["c"][0], i["c_ctx"]], -1)
    o["c"] = c32(c.reshape(KT, P, 2).transpose(1, 0, 2).reshape(P, 16))
    o["consts"] = constants()
    o["w_mod"] = c32(kp(i["w_mod"]).reshape(L, P, KT, 12, 512).transpose(0, 3, 1, 2, 4).reshape(L, 12, P, 4096))
    rw, at = 3 * RW + 256, 768
    hp = np.concatenate([np.r_[64 * h:64 * h + 64, 64 * (h + 4):64 * (h + 4) + 64] for h in range(4)])
    blk = np.arange(P)
    colsets = [3 * RW + blk, 3 * RW + 128 + blk, rw + 512 + blk, rw + 640 + blk] + [rw + hp[P * b:P * b + P] for b in range(4)]
    rwcols = [3 * RW + blk, 3 * RW + 128 + blk]
    for b in range(NB):
        for part in range(3):
            colsets.append(part * RW + P * b + blk)
            rwcols.append(part * RW + P * b + blk)
    win, wmrg, wout, pvs, mws = [], [], [], [], []
    for l in range(L):
        w = i["w_in"][l]
        bl = blocks(w[:, np.concatenate(colsets)], 20)
        win.append(bl.reshape(P, 5, 4096).transpose(1, 0, 2))
        g = w[:, rw + at:]
        g0, g1 = blocks(g[:, :D], KT), blocks(g[:, D:], KT)
        b0, b1 = blocks(i["w_br_rwkv"][l], KT), blocks(i["w_br_attn"][l][hp], KT)
        m = np.concatenate([v.reshape(P, KT, -1) for v in (g0, g1, b0, b1)], -1)
        wmrg.append(m.transpose(1, 0, 2))
        wout.append(blocks(i["w_out"][l], KT).reshape(P, 2, 4096).transpose(1, 0, 2))
        pv = np.zeros((P, NPV), np.float32)

        def put(name, v):
            pv[:, PV[name][0]:PV[name][1]] = v

        put("norm1", i["norm1"][l].reshape(KT, P).T)
        put("norm2", i["norm2"][l].reshape(KT, P).T)
        put("bmod", i["b_mod"][l].reshape(48, P).T)
        for q in range(2):
            put(f"mu{q}", np.stack([i["tshift"][l, q][cs] for cs in rwcols], 1))
        put("w0", i["w0"][l].reshape(8, P).T)
        put("a0", i["a0"][l].reshape(8, P).T)
        for n, s in (("kk", "k_k"), ("ka", "k_a"), ("lg", "lnx_g"), ("lb", "lnx_b")):
            put(n, i[s][l].reshape(NB, P).T)
        put("rk", i["r_k"][l].reshape(NB, P).T)
        if l:
            put("v0", i["v0"][l - 1].reshape(NB, P).T)
        put("qn", np.concatenate([i["q_norm"][l]] * 2)[:, None])
        put("kn", np.concatenate([i["k_norm"][l]] * 2)[:, None])
        put("sink", np.broadcast_to(i["sink"][l][None], (P, 8)))
        pvs.append(pv)
        mw = np.zeros((P, 2304), np.float32)
        mw[0:64, 0:1024] = i["w_decay_up"][l].transpose(1, 0, 2).reshape(64, 1024)
        mw[64:128, 0:1024] = i["w_iclr_up"][l].transpose(1, 0, 2).reshape(64, 1024)
        mw[:, 1024:1536] = i["w_gate_up"][l]
        if l:
            mw[:, 1536:1792] = kp(i["w_vres_down"][l - 1]).reshape(P, 256)
            mw[0:32, 1792:2304] = i["w_vres_up"][l - 1]
        mws.append(mw)
    o["w_in"], o["w_mrg"], o["w_out"] = c32(np.stack(win)), c32(np.stack(wmrg)), c32(np.stack(wout))
    o["pv"], o["mw"] = np.stack(pvs), np.stack(mws)
    g, u = blocks(i["ffn_gate"][0], NFF), blocks(i["ffn_up"][0], NFF)
    gu = np.stack([g, u], 2)
    o["w_gu"] = c32(gu.reshape(P, 11, 4096).transpose(1, 0, 2))
    o["w_dn"] = c32(blocks(i["ffn_down"][0], KT).reshape(P, KT, FF).transpose(1, 0, 2))
    o["router"] = c32(kp(i["router"][0]).reshape(P, 64))
    g = kp(i["moe_gate"][0]).reshape(NE, P, KT, EC, 512)
    u = kp(i["moe_up"][0]).reshape(NE, P, KT, EC, 512)
    d = kp(i["moe_down"][0]).reshape(NE, P, EC, 4, D)
    gu = lambda w, c: w[:, :, :, c, :].reshape(NE, P, 4096)
    parts = [gu(g, 0), gu(u, 0)]
    for c in range(1, EC):
        parts += [gu(g, c), gu(u, c), d[:, :, c - 1].reshape(NE, P, 4096)]
    parts.append(d[:, :, EC - 1].reshape(NE, P, 4096))
    w_exp = np.empty((NE, 3 * EC, P, 4096), np.float32)
    for m, p_ in enumerate(parts):
        w_exp[:, m] = p_
    o["w_exp"] = w_exp
    return o
```

```python
import numpy as np
import concourse.bass as bass
from concourse import mybir
from contextlib import ExitStack

P = 128
D = 1024
KT = D // P
CTX = LAT = 256
T = CTX + LAT
HD = 64
CH = 64
NCH = CTX // CH
RW = 512
NB = RW // P
FF = 2816
NFF = FF // P
FE = 3584
EC = FE // 512
NE = 8
NJ = NE + 3
SLOT = 4096
NS = 3
UNIT = SLOT // 2
WB = 3
WORK = 19456
MOE_F32 = 10496
L = 2
EPS = 1e-6
GN_EPS = 64e-5
DECAY = -float(np.exp(-0.5))

PV = {}
_n = 0
for _name, _w in [("norm1", 8), ("norm2", 8), ("bmod", 48), ("mu0", 14), ("mu1", 14), ("w0", 8), ("a0", 8),
                  ("kk", 4), ("ka", 4), ("rk", 4), ("lg", 4), ("lb", 4), ("v0", 4), ("qn", 1), ("kn", 1), ("sink", 8)]:
    PV[_name] = (_n, _n + _w)
    _n += _w
NPV = _n

CO = {}
_n = 0
for _name, _w in [("ident", 128), ("strict", 256), ("incl", 256), ("level", 6 * 2 * 128), ("cos", 256), ("sin", 256), ("rot", 128),
                  ("bones", 128), ("bmean", 128), ("mean", 128), ("ones", 128), ("before", 128), ("amask", 512),
                  ("iota", 128), ("sel", 2)]:
    CO[_name] = (_n, _n + _w)
    _n += _w
NCO = _n


def constants():
    c = np.zeros((P, NCO), np.float32)

    def put(name, a):
        c[:, CO[name][0]:CO[name][1]] = np.asarray(a, np.float32).reshape(P, -1)

    i = np.arange(P)
    s, t = i[:, None], i[None, :]
    bd = (s // 64) == (t // 64)
    fwd = bd & (s < t)
    put("ident", np.eye(P))
    put("strict", np.stack([fwd, fwd.T], 1))
    put("incl", np.stack([fwd | (s == t), fwd.T | (s == t)], 1))
    lv = []
    for k in range(6):
        n = 1 << k
        m = (s // (2 * n) == t // (2 * n)) & ((s // n) % 2 == 0) & ((t // n) % 2 == 1)
        lv.append(np.stack([m, m.T], 1))
    put("level", np.stack(lv, 1))
    half = HD // 2
    inv = np.float32(10000.0) ** (-np.arange(0, half, 2, dtype=np.float32) / np.float32(half))
    tok = np.arange(LAT)
    ar = (tok // 64).astype(np.float32)[:, None] * inv
    ac = (tok % 64).astype(np.float32)[:, None] * inv
    ang = np.concatenate([ar, ar, ac, ac], -1).astype(np.float32)
    put("cos", np.tile(np.cos(ang).T, (2, 1)))
    put("sin", np.tile(np.sin(ang).T, (2, 1)))
    rot = np.zeros((P, P))
    for h in range(2):
        for q in range(2):
            for j in range(16):
                a = 64 * h + 32 * q + j
                rot[a + 16, a] = -1.0
                rot[a, a + 16] = 1.0
    put("rot", rot)
    put("bones", bd)
    put("bmean", bd / 64.0)
    put("mean", np.full((P, P), 1.0 / D))
    put("ones", np.ones((P, P)))
    put("before", s < t)
    q = np.arange(P)[:, None]
    am = [np.where(np.abs(np.arange(LAT)[None] - (q + P * b)) <= 128, 0.0, -1e30) for b in range(2)]
    put("amask", np.stack(am, 1))
    put("iota", np.tile(np.arange(P), (P, 1)))
    sel = np.zeros((P, 2))
    for g in range(4):
        for v in range(2):
            sel[32 * g + v, v] = 1.0
    put("sel", sel)
    return c


class Signal:

    def __init__(self, sem, name, book):
        self.sem, self.name, self.book, self.n = sem, name, book, 0

    def done(self, ins, *key):
        ins.then_inc(self.sem, 1)
        self.n += 1
        if key:
            self.book[(self.name,) + key] = self.n

    def mark(self, *key):
        self.book[(self.name,) + key] = self.n

    def count(self, *key):
        return self.book.get((self.name,) + key, 1)


def build(nc, a, out, x_mid, vf_mid, h_mid, book):
    f32 = mybir.dt.float32
    i32 = mybir.dt.int32
    u32 = mybir.dt.uint32
    ALU = mybir.AluOpType
    ACT = mybir.ActivationFunctionType
    AX = mybir.AxisListType
    ctx = ExitStack()
    with ctx:
        def sb(name, n, dt=f32):
            return ctx.enter_context(nc.sbuf_tensor(name, [P, n], dt))

        ring = sb("ring", NS * SLOT)
        co = sb("co", NCO)
        pv = sb("pv", NPV)
        modt = sb("modt", 192)
        nrm = sb("nrm", 32)
        rstd = sb("rstd", 512)
        csil = sb("csil", KT * 32)
        ctrl = sb("ctrl", 16, i32)
        small = sb("small", 256)
        tidx = sb("tidx", 16, u32)
        sizes = [("hbuf", KT * T), ("work", WORK), ("proj", 14 * T), ("yatt", NB * T), ("mw", 2304)]
        H_AT, W_AT, P_AT, Y_AT = (sum(n_ for _, n_ in sizes[:i]) for i in range(4))
        with ExitStack() as layers:
            hbuf, work, proj, yatt, mw = (layers.enter_context(nc.sbuf_tensor(n_, [P, w_], f32)) for n_, w_ in sizes)
        f32r = mybir.dt.float32r

        def over(*parts):
            made, at = {}, 0
            with ExitStack() as s:
                for name, place, n_ in parts:
                    if place > at:
                        s.enter_context(nc.sbuf_tensor("below_" + name, [P, place - at], f32))
                    made[name] = s.enter_context(nc.sbuf_tensor(name, [P, n_], f32r))
                    at = place + n_
            return made

        BLOCK = KT * P
        R = over(("in_w", W_AT + 4096, 4 * BLOCK), ("in_h", W_AT + 10240, 12 * T), ("in_h2", W_AT + 17408, 4 * T), ("in_w2", Y_AT, 2 * BLOCK))
        R.update(over(("mo_h_lo", H_AT, KT * T), ("mo_m_lo", W_AT + 4096, KT * T), ("mo_w2", W_AT + 10240, 2 * BLOCK),
                      ("mo_h_hi", W_AT + 12288, KT * T), ("mo_w", W_AT + 16384, 3 * BLOCK), ("mo_w3", P_AT, BLOCK),
                      *((f"mo_m_hi{i}", P_AT + (3 + 3 * i) * T, 2 * T) for i in range(NB))))
        R.update(over(("gu_h_lo", H_AT, KT * T), ("gu_w2", W_AT + 17408, BLOCK), ("gu_h_hi", P_AT, KT * T),
                      ("gu_w", P_AT + KT * T, 3 * BLOCK), ("gu_w3", Y_AT, 2 * BLOCK)))
        sb("kept", KT * T + MOE_F32)
        w_hi, w_lo = (ctx.enter_context(nc.sbuf_tensor(n_, [P, WB, UNIT], f32r)) for n_ in ("w_hi", "w_lo"))
        xg_hi, xg_lo = (ctx.enter_context(nc.sbuf_tensor(n_, [P, KT, P], f32r)) for n_ in ("xg_hi", "xg_lo"))
        hT_hi, hT_lo = (ctx.enter_context(nc.sbuf_tensor(n_, [P, 2, 4, P], f32r)) for n_ in ("hT_hi", "hT_lo"))
        bank = [ctx.enter_context(nc.psum_tensor(f"bank{i}", [P, 512], f32)) for i in range(8)]

        def sem(name):
            return ctx.enter_context(nc.semaphore(name))

        pe_done = Signal(sem("pe_done"), "pe", book)
        act_done = Signal(sem("act_done"), "act", book)
        dve_done = Signal(sem("dve_done"), "dve", book)
        pool_done = Signal(sem("pool_done"), "pool", book)
        ring_full = [sem(f"ring_full{i}") for i in range(NS)]
        const_loaded, par_loaded, mw_loaded, x_loaded, c_loaded = (sem(n) for n in
                                                                   ("const_loaded", "par_loaded", "mw_loaded", "x_loaded", "c_loaded"))
        x_stored, vf_stored, vf_loaded, out_stored = (sem(n) for n in ("x_stored", "vf_stored", "vf_loaded", "out_stored"))
        h_stored, h_free, h_loaded = (sem(n) for n in ("h_stored", "h_free", "h_loaded"))
        X = {n: sem("moe_" + n) for n in ("key", "key2", "gat", "xg", "gt", "gtc", "silu", "act", "tr", "trc", "trl", "yc", "xl", "hi", "lo", "wused", "sc", "add", "zero")}

        def C(name, *dims):
            v = co[:, CO[name][0]:CO[name][1]]
            return v if not dims else v.rearrange("p (a b) -> p a b", a=dims[0])

        ident = C("ident")
        strict = C("strict", 2)
        incl = C("incl", 2)
        level = C("level", 12)
        amask = C("amask", 2)

        def V(name, i=0):
            o = PV[name][0] + i
            return pv[:, o:o + 1]

        def wk(off, n, *dims):
            v = work[:, off:off + n]
            if len(dims) == 1:
                return v.rearrange("p (a b) -> p a b", a=dims[0])
            if len(dims) == 2:
                return v.rearrange("p (a b c) -> p a b c", a=dims[0], b=dims[1])
            return v

        h3 = hbuf[:, :].rearrange("p (k t) -> p k t", k=KT)
        pr = proj[:, :].rearrange("p (k t) -> p k t", k=14)
        ya = yatt[:, :].rearrange("p (k t) -> p k t", k=NB)
        x3 = wk(0, 4096, KT)
        modv_of = [modt[:, 96 * l:96 * l + 96].rearrange("p (m v) -> p m v", v=2) for l in range(L)]

        mod_item = lambda l, n: (a["w_mod"][l, n], 4096)
        items = []
        for l in range(L):
            proj_items = [(a["w_in"][l, n], 4096, ("in", l, n)) for n in range(5)]
            if l == 0:
                items += [mod_item(0, n) for n in range(4)]
                for n in range(5):
                    items += [proj_items[n]] + ([mod_item(0, 4 + n)] if n < 4 else [])
                items += [mod_item(0, n) for n in range(8, 12)]
            else:
                items += proj_items
            items += [(a["w_mrg"][l, n], 3072, ("mg", l, n)) for n in range(8)]
            items += [(a["w_out"][l, n], 4096, ("wo", l, n)) for n in range(2)]
            if l == 0:
                for n in range(11):
                    items += [(a["w_gu"][n], 4096, ("gu", l, n)), mod_item(1, n)]
                for n in range(8):
                    items += [(a["w_dn"][n], 2816)] + ([mod_item(1, 11)] if n == 0 else [])
        items += [(a["router"], 64)]
        N_STATIC = len(items)
        item_at = {it[2]: i for i, it in enumerate(items) if len(it) > 2}
        DB = 3
        blocks_of = {"in": 20, "mo": 24, "gu": 44}

        def block_item(stage, l, i):
            if stage == "mo" and i < 16:
                return item_at["mg", l, i // 2], i % 2, i % 2 == 1
            key, i = ("wo", i - 16) if stage == "mo" else (stage, i)
            return item_at[key, l, i // 4], i % 4, i % 4 == 3

        def raw_block(stage, l, i):
            item, place, _ = block_item(stage, l, i)
            return slot(item)[:, BLOCK * place:BLOCK * place + BLOCK]

        last_block = {block_item(st_, l, i)[0]: (st_, l, i) for st_, l in (("in", 0), ("in", 1), ("mo", 0), ("mo", 1), ("gu", 0))
                      for i in range(blocks_of[st_]) if block_item(st_, l, i)[2]}

        def block_parts(stage, i):
            j = i % DB
            if stage == "in":
                return R["in_w"][:, BLOCK * j:BLOCK * j + BLOCK], R["in_w"][:, 3 * BLOCK:] if j == 0 else R["in_w2"][:, BLOCK * (j - 1):BLOCK * j]
            lo, lo2 = (R["mo_w3"], R["mo_w2"]) if stage == "mo" else (R["gu_w2"], R["gu_w3"])
            return R[stage + "_w"][:, BLOCK * j:BLOCK * j + BLOCK], lo[:, :] if j == 0 else lo2[:, BLOCK * (j - 1):BLOCK * j]

        def h_parts(stage, l, k):
            c0, nt = cols(l)
            at = slice(T * k, T * k + T)
            if stage == "mg":
                return R["mo_h_hi"][:, T * k:T * k + nt], R["mo_h_lo"][:, T * k + c0:T * k + c0 + nt]
            if stage == "wo":
                return R[f"mo_m_hi{k // 2}"][:, T * (k % 2):T * (k % 2) + nt], R["mo_m_lo"][:, T * k:T * k + nt]
            if stage == "in":
                return R["in_h"][:, at], R["in_h"][:, T * (KT + k):T * (KT + k) + T] if k < 4 else R["in_h2"][:, T * (k - 4):T * (k - 4) + T]
            return R["gu_h_hi"][:, at], R["gu_h_lo"][:, at]
        order = [("g", 0), ("u", 0)]
        for c in range(1, EC):
            order += [("g", c), ("u", c), ("d", c - 1)]
        order += [("d", EC - 1)]
        place_of = {x: i for i, x in enumerate(order)}

        NU = 6 * EC

        def unit(kind, c, half):
            return 2 * place_of[kind, c] + half

        def count(j, u):
            return j * NU + (u + 1)

        taken = [0]

        def slot(i):
            return ring[:, (i % NS) * SLOT:(i % NS + 1) * SLOT]

        QK = 3072
        att = wk(0, QK, 6)

        def attention_units(l):
            return [(b, hh, qb) for b in range(NB) for hh in range(2) for qb in ((0, 1, 2, 3) if l == 0 else (2, 3))]

        def key_blocks(qb):
            return 2 if qb < 2 else 4

        def mod_bank(l, n):
            return bank[7] if l == 0 and n >= 8 or n % 2 else bank[6]

        mod_row = lambda n: wk(16384 + 512 * (n % 2), 512)

        def mod_beside(place, i):
            if place == "proj":
                return (0, 4 + i // 4) if i % 4 == 3 and i < 16 else None, (0, 3 + i // 4) if i % 4 == 0 and 4 <= i <= 16 else None
            if place == "att":
                return (0, 7 + i // 4) if i % 4 == 0 and 4 <= i <= 16 else None, (0, 7 + i // 4) if i % 4 == 1 and 4 < i <= 17 else None
            return (1, i) if i < 12 else None, (1, i - 1) if 1 <= i <= 12 else None

        def norm_at(bi):
            return (bi - 9) // 2 if 9 <= bi <= 17 and bi % 2 else None

        score_bank = lambda u: bank[(0, 1, 6)[u % 3]]
        soft = lambda u: small[:, 8 * (u % 3):8 * (u % 3) + 8]
        probs = lambda u, nk: wk(4608 + 512 * (u % 3), 128 * nk)
        probs_T = lambda u: wk(6656 + 512 * (u % 2), 512)

        o = 0
        J = {}
        for n_, w_ in [("kr", 1024), ("kapbd", 1024), ("Kbd", 1024), ("Bbd", 1024), ("vbd", 512), ("LkT", 1024), ("QkT", 1024),
                       ("U", 1024), ("QbT", 1024), ("N", 1024), ("Um", 1024), ("Ktok", 1024), ("Btok", 1024), ("Vtok", 512),
                       ("lw", 512), ("Lc", 512), ("Pc", 512), ("Qc", 512), ("ic", 512), ("kh", 512), ("bb", 512),
                       ("kk", 256), ("kkt", 256), ("cv", 256), ("sq", 256), ("rs", 256), ("Y", 256), ("S", 256), ("Rs", 256), ("Un", 256)]:
            J[n_] = (o, w_)
            o += w_
        assert o <= 19200, o

        def j3(name, n):
            return wk(*J[name], n)

        def hb(off, n, *dims):
            v = hbuf[:, off:off + n]
            if len(dims) == 1:
                return v.rearrange("p (a b) -> p a b", a=dims[0])
            if len(dims) == 2:
                return v.rearrange("p (a b c) -> p a b c", a=dims[0], b=dims[1])
            return v

        jj_kr = [wk(*J["kr"], 8, 2), hb(0, 1024, 8, 2)]
        jj_kap = [j3("kapbd", 8), hb(1024, 1024, 8)]
        jj_P = [j3("Pc", 2), hb(2048, 512, 2)]
        jj_cv = [wk(*J["cv"]), hb(2560, 256)]
        j_sqp, j_rsp = hb(2816, 256), hb(3072, 256)
        j_K, j_B = j3("Kbd", 8), j3("Bbd", 8)
        j_M, j_X = j_K, j_B
        j_v, j_Lk, j_Qk, j_U, j_Qb, j_N, j_Um = j3("vbd", 4), j3("LkT", 8), j3("QkT", 8), j3("U", 8), j3("QbT", 8), j3("N", 8), j3("Um", 8)
        j_Kt, j_Bt, j_Vt = j3("Ktok", 8), j3("Btok", 8), j3("Vtok", 4)
        j_lw, j_L, j_Q, j_ic, j_kh, j_bb = (j3(n, 2) for n in ("lw", "Lc", "Qc", "ic", "kh", "bb"))
        j_kk, j_kkt, j_sq, j_rs, j_Y = (wk(*J[n]) for n in ("kk", "kkt", "sq", "rs", "Y"))
        j_S, j_R, j_Un = (j3(n, 2) for n in ("S", "Rs", "Un"))
        mup = mw[:, 0:1024].rearrange("p (d c) -> p d c", d=2)
        mgate = mw[:, 1024:1536]
        mvd = mw[:, 1536:1792].rearrange("p (k c) -> p k c", k=KT)
        mvu = mw[:, 1792:2304]

        def layer_jobs(l):
            js = [(l, b, q) for b in range(NB) for q in range(2)]
            return list(zip(js, [None] + js[:-1], js[1:] + [None]))

        head_at = {1: 0, 2: 1, 4: 2, 5: 3}
        post_at = {1: 0, 2: 1, 3: 2}

        def turn(jn):
            return jn[2]

        def emits(jn):
            return jn[0] == 0 or jn[2] == 1

        def cols(l):
            return (0, T) if l == 0 else (CTX, LAT)

        o = 4096
        M = {}
        for n_, w_ in [("htok", 2048), ("sil", 1024), ("hid", 1024), ("G", 256), ("Gw", 256), ("GwT", 256),
                       ("y", 1024), ("rt", 512)]:
            M[n_] = (o, w_)
            o += w_
        assert o == MOE_F32, o
        m_htok = wk(*M["htok"], 2)
        m_sil = wk(*M["sil"], 2)
        m_hid = wk(*M["hid"], 2)
        m_G = wk(*M["G"], 2)
        m_Gw = wk(*M["Gw"], 2)
        m_GwT = wk(*M["GwT"])
        m_y = wk(*M["y"])
        rt = wk(*M["rt"])

        block = ctx.enter_context(nc.Block())

        @block.sync
        def _(sp):
            def slot_free(before):
                if before in last_block:
                    sig = pool_done if last_block[before][0] == "in" else dve_done
                    sp.wait_ge(sig.sem, sig.count("wlo", *last_block[before]))
                if before not in last_block or items[before][2][0] == "mg":
                    sp.wait_ge(pe_done.sem, pe_done.count("item", before))

            for i, (src, n, *_) in enumerate(items):
                if i >= NS:
                    slot_free(i - NS)
                sp.dma_start(slot(i)[:, 0:n], src).then_inc(ring_full[i % NS], 16)

            def expert(e, j):
                for m in range(3 * EC):
                    if isinstance(j, int) and m < NS:
                        slot_free(N_STATIC + m - NS)
                    else:
                        sp.wait_ge(X["lo"], j * NU + (2 * (m - NS) + 2))
                    src = a["w_exp"][e, m] if isinstance(e, int) else a["w_exp"][bass.ds(e, 1), m, :, :].rearrange("e p n -> p (e n)")
                    sp.dma_start(slot(N_STATIC + m), src).then_inc(ring_full[(N_STATIC + m) % NS], 16)

            expert(0, 0)
            with sp.Fori(1, NE) as j:
                expert(j, j)
            sp.wait_ge(dve_done.sem, dve_done.count("ctrl"))
            more = sp.value_load(ctrl[0:1, NJ:NJ + 1], min_val=0, max_val=3)
            with sp.If(more > 0):
                with sp.Fori(0, more) as j2:
                    r = sp.value_load(ctrl[0:1, bass.ds(j2 + NE, 1)], min_val=0, max_val=NE - 1)
                    expert(r, j2 + NE)
            sp.wait_ge(dve_done.sem, dve_done.count("final"))
            sp.dma_start(out, x3[:, :, CTX:T]).then_inc(out_stored, 16)
            sp.wait_ge(out_stored, 16)

        @block.tensor
        def _(pe):
            seen = {}

            def need(sig, *key):
                n = sig.count(*key)
                if seen.get(sig.name, 0) < n:
                    seen[sig.name] = n
                    pe.wait_ge(sig.sem, n)

            def mm(o_, lhsT, rhs, start=True, stop=True, **kw):
                return pe.matmul(o_, lhsT, rhs, start=start, stop=stop, **kw)

            def next_item():
                i = taken[0]
                taken[0] += 1
                pe.wait_ge(ring_full[i % NS], 16 * (i // NS + 1))
                return slot(i)

            def item_done():
                book[("pe", "item", taken[0] - 1)] = pe_done.n

            def mod_rows(l, n):
                w = next_item()[:, :].rearrange("p (k c) -> p k c", k=KT)
                cs3 = csil[:, :].rearrange("p (k c) -> p k c", k=KT)
                before = (l, n - 1 if l == 0 and n >= 8 else n - 2)
                if before[1] >= 0:
                    need(dve_done, "modt", *before)
                for k in range(KT):
                    g = k % 4
                    ins = mm(mod_bank(l, n)[32 * g:32 * g + 32, :], cs3[:, k, :], w[:, k, :], start=(k < 4), stop=(k >= 4),
                             tile_position=(0, 32 * g), skip_group_check=True)
                pe_done.done(ins, "modrow", l, n)
                item_done()

            def split_product(o_, stage, l, i):
                sig = pool_done if stage == "in" else dve_done
                need(sig, "wlo", stage, l, i)
                wh, wl = (w_.rearrange("p (k c) -> p k c", k=KT) for w_ in block_parts(stage, i))
                what = stage if stage != "mo" else "mg" if i < 16 else "wo"
                for k in range(KT):
                    need(dve_done, "hlo", what, l, k)
                    hh, hl = h_parts(what, l, k)
                    mm(o_, wh[:, k, :], hh, start=(k == 0), stop=False)
                    mm(o_, wl[:, k, :], hh, start=False, stop=False)
                    ins = mm(o_, wh[:, k, :], hl, start=False, stop=(k == KT - 1))
                pe_done.done(ins, "used", stage, l, i)
                if what != "mg" and i % 4 == 3:
                    taken[0] += 1

            def mod_turn(l, n):
                need(act_done, "modrow", l, n)
                for j in range(4):
                    ins = mm(mod_bank(l, n)[:, 2 * j:2 * j + 2], mod_row(n)[:, 128 * j:128 * j + 128], C("sel"))
                pe_done.done(ins, "modt", l, n)

            def mod_step(place, i):
                starts, ends = mod_beside(place, i)
                if ends:
                    mod_turn(*ends)
                if starts:
                    mod_rows(*starts)

            def first_norm(l):
                for k in range(KT):
                    need(act_done, "sq1", l, k)
                    ins = mm(bank[2][:, :], C("mean"), proj[:, T * k:T * k + T], start=(k == 0), stop=(k == KT - 1))
                pe_done.done(ins, "ms1", l)

            for l in range(L):
                if l == 0:
                    need(act_done, "csil")
                    mod_rows(0, 0)
                    mod_rows(0, 1)
                    pe.wait_ge(const_loaded, 16)
                    mod_turn(0, 0)
                    first_norm(0)
                    for n in range(2, 5):
                        if n < 4:
                            mod_rows(0, n)
                        mod_turn(0, n - 1)
                else:
                    first_norm(1)
                for n in range(5):
                    for j in range(4):
                        bi = 4 * n + j
                        if bi >= 4:
                            need(act_done, "proj", l, bi - 4)
                        else:
                            need(act_done, "rms1", l)
                        split_product(bank[bi % 4][:, :], "in", l, bi)
                        pe_done.mark("proj", l, bi)
                        i = norm_at(bi)
                        if i is not None:
                            need(act_done, "qsq", l, i)
                            if i >= 1:
                                need(act_done, "qrms", l, i - 1)
                            pe_done.done(mm(bank[4][:, :], C("bmean"), wk(3072 + 512 * (i % 2), 512)), "qms", l, i)
                        i = norm_at(bi - 1)
                        if i is not None:
                            need(dve_done, "qn", l, i)
                            if i >= 1:
                                need(dve_done, "qrot", l, i - 1)
                            pe_done.done(mm(bank[5][:, 0:256], C("rot"), att[:, i, CTX:T]), "qrot", l, i)
                        if l == 0:
                            mod_step("proj", bi)
                for tb in range(4):
                    if tb == 0:
                        need(act_done, "proj", l, 19)
                        need(dve_done, "qrot", l, 4)
                    ins = pe.transpose(bank[4][:, 128 * tb:128 * tb + 128], att[:, 5, 128 * tb:128 * tb + 128], ident)
                pe_done.done(ins, "vtok", l)
                need(act_done, "vtok", l)
                vt = wk(4096, 512, 4)
                units = attention_units(l)

                def score(u):
                    b, hh, qb = units[u]
                    if u >= 3:
                        need(act_done, "exp", l, u - 3)
                    q_ = att[64 * hh:64 * hh + 64, b, 128 * qb:128 * qb + 128]
                    k_ = att[64 * hh:64 * hh + 64, 4, :]
                    ins = mm(score_bank(u)[:, 0:256], q_, k_[:, 0:256])
                    if key_blocks(qb) == 4:
                        mm(score_bank(u)[:, 256:512], q_, k_[:, 256:512], stop=False)
                        ins = mm(score_bank(u)[:, 256:512], ident, amask[:, qb - 2, :], start=False)
                    pe_done.done(ins, "score", l, u)

                def turn_probs(u):
                    nk = key_blocks(units[u][2])
                    need(dve_done, "prob", l, u)
                    if u >= 2:
                        need(act_done, "pT", l, u - 2)
                    for kb in range(nk):
                        ins = pe.transpose(bank[2 + u % 2][:, 128 * kb:128 * kb + 128], probs(u, nk)[:, 128 * kb:128 * kb + 128], ident)
                    pe_done.done(ins, "pT", l, u)

                def times_values(u):
                    b, hh, qb = units[u]
                    nk = key_blocks(qb)
                    need(act_done, "pT", l, u)
                    if (hh, qb) == units[0][1:] and b >= 2:
                        need(act_done, "yatt", l, b - 2)
                    for kb in range(nk):
                        ins = mm(bank[4 + b % 2][64 * hh:64 * hh + 64, 128 * qb:128 * qb + 128], vt[:, kb, 64 * hh:64 * hh + 64],
                                 probs_T(u)[:, 128 * kb:128 * kb + 128], start=(kb == 0), stop=(kb == nk - 1))
                    pe_done.done(ins, "pv", l, u)

                for u in range(len(units) + 3):
                    if u < len(units):
                        score(u)
                    if 2 <= u < len(units) + 2:
                        turn_probs(u - 2)
                    if u >= 3:
                        times_values(u - 3)
                    if l == 0:
                        mod_step("att", u)
                if l == 1:
                    pe.wait_ge(mw_loaded, 32)
                    need(act_done, "yatt", 1, NB - 1)
                    for k in range(KT):
                        ins = mm(bank[7][0:32, :], mvd[:, k, :], h3[:, k, :], start=(k == 0), stop=(k == KT - 1))
                    pe_done.done(ins, "vdown")
                    need(act_done, "vdown")
                    for b in range(NB):
                        if b >= 1:
                            need(act_done, "vsig", b - 1)
                        pe_done.done(mm(bank[7][:, :], mvu[0:32, P * b:P * b + P], rstd[0:32, :]), "vup", b)
                pe.wait_ge(mw_loaded, 16 * (l + 1))
                def head(jn, i):
                    _, b, q = jn
                    q0 = 256 * q
                    if i == 1:
                        need(act_done, "kksq", *jn)
                        pe_done.done(mm(bank[6][:, 256:512], C("bones"), j_sq), "kkss", *jn)
                    if i == 2:
                        need(act_done, "kkrms", *jn)
                        for d in range(2):
                            mm(bank[7][:, 256 * d:256 * d + 256], mup[0:64, d, P * b:P * b + P], pr[0:64, 0, q0:q0 + 256])
                        for d in range(2):
                            ins = mm(bank[6][:, 256 * d:256 * d + 256], mup[64:128, d, P * b:P * b + P], pr[64:128, 0, q0:q0 + 256])
                        pe_done.done(ins, "lora", *jn)
                    if i == 4:
                        need(dve_done, "coef", *jn)
                        need(act_done, "sig", *jn)
                        pe_done.done(mm(bank[7][:, 0:256], C("bones"), j_rs), "coef", *jn)

                def post(jn, i):
                    _, b, q = jn
                    if not emits(jn):
                        return
                    if i == 0:
                        need(act_done, "y", *jn)
                        pe_done.done(mm(bank[7][:, 0:256], C("bmean"), j_Y), "ymean", *jn)
                    if i == 1:
                        need(act_done, "ysq", *jn)
                        pe_done.done(mm(bank[7][:, 256:512], C("bmean"), j_sqp), "yvar", *jn)
                        pe_done.done(mm(bank[6][:, 0:256], mgate[:, P * b:P * b + P], pr[:, 1, 256 * q:256 * q + 256]), "gate", *jn)
                    if i == 2:
                        need(act_done, "yrms", *jn)
                        need(dve_done, "post", *jn)

                first = layer_jobs(l)[0][0]
                need(dve_done, "ready", l)
                for i in range(5):
                    head(first, i)
                for jn, prev, nxt in layer_jobs(l):
                    b, q = jn[1:]
                    emit = emits(jn)
                    j_kr, j_kap = jj_kr[turn(jn)], jj_kap[turn(jn)]
                    need(dve_done, "kr", *jn)
                    need(dve_done, "bd", *jn)
                    need(pool_done, "bd", *jn)
                    need(act_done, "bd", *jn)
                    need(dve_done, "cv", *jn)
                    if prev is not None:
                        need(dve_done, "state", *prev, NCH - 1, 1)
                    for w_, src in enumerate((j_K, j_B)):
                        for s in range(8):
                            if w_ == 1 and s == 4 and prev is not None and emits(prev):
                                need(act_done, "y", *prev)
                            rhs = j_kr[:, s, :, :].rearrange("p a b -> p (a b)").unsqueeze(1).to_broadcast([P, 2, 128])
                            ins = mm(bank[4 * w_ + s // 2][:, 256 * (s % 2):256 * (s % 2) + 256], src[:, s, :], rhs)
                            if s % 2:
                                pe_done.done(ins, "gram", *jn, w_, s // 2)
                    n = 0
                    for src, m_ in ((j_K, 8), (j_B, 8), (j_v, 4)):
                        for g in range(m_ // 4):
                            if n < 2:
                                need(dve_done, "gram", *jn, 1, 2 + n)
                            else:
                                need(act_done, "tok", *jn, n - 2)
                            for s in range(4):
                                ins = pe.transpose(bank[6 + n % 2][:, 128 * s:128 * s + 128], src[:, 4 * g + s, :], ident)
                            pe_done.done(ins, "tok", *jn, n)
                            n += 1
                    for lv in range(6):
                        for d in range(2):
                            need(pool_done, "um", *jn, lv, d)
                            if lv == 0:
                                for c in range(4):
                                    ins = pe.transpose(bank[3 * d][:, 128 * c:128 * c + 128], j_Um[:, 4 * d + c, :], ident)
                                pe_done.done(ins, "x", *jn, lv, d)
                                continue
                            need(dve_done, "mn", *jn, lv - 1, d)
                            for c in range(4):
                                s = 4 * d + c
                                ins = mm(bank[3 * d][:, 128 * c:128 * c + 128], j_Um[:, s, :], j_M[:, s, :])
                            pe_done.done(ins, "x", *jn, lv, d)
                        if lv == 0:
                            continue
                        for d in range(2):
                            need(act_done, "x", *jn, lv, d)
                            for c in range(4):
                                s = 4 * d + c
                                if lv < 5:
                                    mm(bank[3 * d + 1][:, 128 * c:128 * c + 128], j_N[:, s, :], j_X[:, s, :])
                            for c in range(4):
                                s = 4 * d + c
                                ins = mm(bank[3 * d + 2][:, 128 * c:128 * c + 128], j_X[:, s, :], j_N[:, s, :])
                            pe_done.done(ins, "mn", *jn, lv, d)
                        if lv == 1:
                            need(act_done, "tok", *jn, 4)
                            need(act_done, "tok", *jn, 3)
                        if prev is not None:
                            post(prev, {1: 0, 2: 1, 4: 2}.get(lv))
                        if nxt is not None:
                            head(nxt, head_at.get(lv))
                    for c in range(NCH):
                        for d in range(2):
                            ch = c if d == 0 else NCH - 1 - c
                            s = 4 * d + ch
                            if c == 0:
                                need(dve_done, "mn", *jn, 5, d)
                                need(act_done, "tok", *jn, 4)
                            else:
                                need(dve_done, "state", *jn, c - 1, d)
                            mm(bank[3 * d][:, 0:128], j_Lk[:, s, :], j_Vt[:, ch, :], stop=False)
                            pe_done.done(mm(bank[3 * d][:, 0:128], j_kap[:, s, :], j_S[:, d, :], start=False), "R", *jn, c, d)
                            if emit:
                                r_dup = j_kr[:, s, 1, :].unsqueeze(1).to_broadcast([P, 2, CH])
                                yb = bank[6][:, 128 * ch:128 * ch + 128]
                                if c == 0 and d == 0 and nxt is not None:
                                    need(act_done, "sig", *nxt)
                                mm(yb, j_S[:, d, :], r_dup, start=(c == 0 and d == 0), stop=False, skip_group_check=True)
                                mm(yb, j_Vt[:, ch, :], j_Qk[:, s, :], start=False, stop=False, skip_group_check=True)
                        for d in range(2):
                            ch = c if d == 0 else NCH - 1 - c
                            s = 4 * d + ch
                            need(act_done, "R", *jn, c, d)
                            pe_done.done(mm(bank[3 * d][:, 128:256], j_N[:, s, :], j_R[:, d, :]), "U", *jn, c, d)
                        for d in range(2):
                            ch = c if d == 0 else NCH - 1 - c
                            s = 4 * d + ch
                            need(dve_done, "U", *jn, c, d)
                            mm(bank[3 * d][:, 256:384], j_Kt[:, s, :], j_Vt[:, ch, :], stop=False)
                            pe_done.done(mm(bank[3 * d][:, 256:384], j_Bt[:, s, :], j_Un[:, d, :], start=False), "state", *jn, c, d)
                            if emit:
                                ins = mm(bank[6][:, 128 * ch:128 * ch + 128], j_Un[:, d, :], j_Qb[:, s, :], start=False,
                                         stop=(c == NCH - 1 and d == 1), skip_group_check=True)
                                pe_done.done(ins, "y", *jn, c, d)
                        if c == 1 and nxt is not None:
                            head(nxt, 4)
                for i in range(3):
                    post(jn, i)
                c0, nt = cols(l)
                for n in range(KT):
                    wb = next_item()[:, 2048:3072].rearrange("p (g k c) -> p g k c", g=2, k=NB)
                    st = 4 * (n % 2)
                    if n == 0:
                        need(act_done, "yatt", l, NB - 1)
                        need(act_done, "y", *layer_jobs(l)[-1][0])
                    if n >= 2:
                        need(dve_done, "merge", l, n - 2)
                    for g in (1, 0):
                        if n == 0 and g == 0:
                            need(dve_done, "yrw", l)
                        for k in range(NB):
                            rhs = pr[:, 2 + 3 * k, c0:c0 + nt] if g == 0 else ya[:, k, c0:c0 + nt]
                            ins = mm(bank[st + 2 + g][:, 0:nt], wb[:, g, k, :], rhs, start=(k == 0), stop=(k == NB - 1))
                        pe_done.done(ins, "mb", l, n, g)
                    item_done()
                    for g in range(2):
                        split_product(bank[st + g][:, 0:nt], "mo", l, 2 * n + g)
                        pe_done.mark("mg", l, n, g)
                for di in range(KT):
                    if di == 0:
                        need(dve_done, "merge", l, KT - 1)
                    if di >= 2:
                        need(dve_done, "res1", l, di - 2)
                    split_product(bank[di % 2][:, 0:nt], "mo", l, 16 + di)
                    pe_done.mark("wo", l, di)
                for k in range(KT):
                    need(act_done, "sq2", l, k)
                    if k == 0:
                        need(dve_done, "res1", l, KT - 1)
                    ins = mm(bank[0][:, 0:nt], C("mean"), wk(12288 + 512 * k, nt), start=(k == 0), stop=(k == KT - 1))
                pe_done.done(ins, "ms2", l)
                if l == 1:
                    need(act_done, "h2", l)
                    need(dve_done, "h2", l)
                if l == 0:
                    need(act_done, "rms2", l)
                    for n in range(11):
                        for j in range(4):
                            f, g = 2 * n + j // 2, j % 2
                            if f >= 2 and g == 0:
                                need(dve_done, "hff", f - 2)
                            split_product(bank[2 * (f % 2) + g][:, :], "gu", l, 4 * n + j)
                            pe_done.mark("gu", f, g)
                        mod_step("ffn", n)
                    for n in range(KT):
                        w = next_item()[:, 0:2816].rearrange("p (k c) -> p k c", k=NFF)
                        if n == 0:
                            need(dve_done, "hff", NFF - 1)
                        if n >= 2:
                            need(dve_done, "res2", n - 2)
                        for k in range(NFF):
                            ins = mm(bank[n % 2][:, :], w[:, k, :], wk(4096 + 512 * k, 512), start=(k == 0), stop=(k == NFF - 1))
                        pe_done.done(ins, "dn", n)
                        item_done()
                        mod_step("ffn", 11 + n)
                else:
                    w = next_item()[:, 0:64].rearrange("p (k e) -> p k e", k=KT)
                    for tb in range(2):
                        for k in range(KT):
                            ins = mm(bank[1][:, 8 * tb:8 * tb + 8], h3[:, k, CTX + P * tb:CTX + P * tb + P], w[:, k, :],
                                     start=(k == 0), stop=(k == KT - 1))
                    pe_done.done(ins, "logits")
                    item_done()
                    for tb in range(2):
                        for g in range(2):
                            for k in range(4):
                                ins = pe.transpose(bank[4 + 2 * tb + g][:, 128 * k:128 * k + 128],
                                                   h3[:, 4 * g + k, CTX + P * tb:CTX + P * tb + P], ident)
                            pe_done.done(ins, "htok", tb, g)
                    need(dve_done, "mask")
                    rmask = rt[:, 0:16].rearrange("p (t e) -> p t e", t=2)
                    mm(bank[0][:, 0:8], C("before"), rmask[:, 0, :]).then_inc(X["wused"], 1)
                    mm(bank[0][:, 8:16], C("before"), rmask[:, 1, :], stop=False).then_inc(X["wused"], 1)
                    mm(bank[0][:, 8:16], C("ones"), rmask[:, 0, :], start=False).then_inc(X["wused"], 1)
                    mm(bank[0][:, 16:24], C("ones"), rmask[:, 0, :], stop=False)
                    pe_done.done(mm(bank[0][:, 16:24], C("ones"), rmask[:, 1, :], start=False), "rank")
                    need(dve_done, "ctrl")
                    need(act_done, "htok", 1, 1)
                    need(dve_done, "gwt0")
                    jobs_here = pe.value_load(ctrl[0:1, NJ + 1:NJ + 2], min_val=NE, max_val=NJ)

                    def gather(j, g):
                        if g == 0:
                            pe.wait_ge(X["key"], j + 1)
                            if not isinstance(j, int):
                                pe.wait_ge(X["gtc"], j)
                        else:
                            pe.wait_ge(X["xl"], j * 2 + 1)
                        for k in range(4):
                            for tb in range(2):
                                ins = mm(bank[6][:, 128 * k:128 * k + 128], m_htok[:, tb, P * (4 * g + k):P * (4 * g + k) + P],
                                         m_G[:, tb, :], start=(tb == 0), stop=(tb == 1))
                        ins.then_inc(X["gat"], 1)

                    def scatter(j):
                        pe.wait_ge(X["yc"], j * 2 + 2)
                        pe.wait_ge(X["xl"], j * 2 + 2)
                        for g in range(4):
                            for k in range(2):
                                kk_ = 2 * g + k
                                ins = mm(bank[4 + g][:, 256 * k:256 * k + 256], m_y[:, P * kk_:P * kk_ + P], m_GwT)
                            ins.then_inc(X["sc"], 1)

                    for g in range(2):
                        gather(0, g)
                    for i in range(2):
                        ins = mm(bank[[5, 7][i]][:, :], m_GwT[:, 0:P], m_htok[:, 0, 0:512])
                    ins.then_inc(X["zero"], 1)
                    with pe.Fori(0, jobs_here) as j:
                        pe.wait_ge(X["xl"], j * 2 + 2)

                        def transposes(c):
                            pe.wait_ge(X["act"], j * EC + (c + 1))
                            if c >= 1:
                                pe.wait_ge(X["trl"], j * EC + c)
                            else:
                                pe.wait_ge(X["add"], j * 4 + 1)
                            for k in range(4):
                                ins = pe.transpose(bank[4][:, 128 * k:128 * k + 128], m_hid[:, c % 2, 128 * k:128 * k + 128], ident)
                            ins.then_inc(X["tr"], 1)

                        def parts(o_, x_hi, x_lo, wh, wl, first, last):
                            mm(o_, x_hi, wh, start=first, stop=False)
                            mm(o_, x_hi, wl, start=False, stop=False)
                            return mm(o_, x_lo, wh, start=False, stop=last)

                        for kind, c in order:
                            for half in range(2):
                                u = unit(kind, c, half)
                                if kind == "d" and half == 0:
                                    pe.wait_ge(X["trl"], j * EC + (c + 1))
                                    if c == 0:
                                        pe.wait_ge(X["add"], j * 4 + 4)
                                if kind == "g" and half == 0 and c >= 2:
                                    pe.wait_ge(X["act"], j * EC + (c - 1))
                                pe.wait_ge(X["lo"], count(j, u))
                                wh, wl = w_hi[:, u % WB, :], w_lo[:, u % WB, :]
                                if kind == "d":
                                    for k in range(2):
                                        kk_ = 2 * half + k
                                        for g in range(2):
                                            cs = slice(1024 * k + 512 * g, 1024 * k + 512 * g + 512)
                                            ins = parts([bank[5], bank[7]][g][:, :], hT_hi[:, c % 2, kk_, :], hT_lo[:, c % 2, kk_, :],
                                                        wh[:, cs], wl[:, cs], c == 0 and kk_ == 0, c == EC - 1 and kk_ == 3)
                                else:
                                    for k in range(4):
                                        kk_ = 4 * half + k
                                        cs = slice(512 * k, 512 * k + 512)
                                        ins = parts(bank[2 * (c % 2) + (kind == "u")][:, :], xg_hi[:, kk_, :], xg_lo[:, kk_, :],
                                                    wh[:, cs], wl[:, cs], kk_ == 0, kk_ == KT - 1)
                                ins.then_inc(X["wused"], 1)
                            if kind == "g" and c >= 1:
                                transposes(c - 1)
                            if (kind, c) == ("u", 0):
                                scatter(j)
                            if (kind, c) == ("d", 0):
                                for tb in range(2):
                                    ins = pe.transpose(bank[6][:, 128 * tb:128 * tb + 128], m_Gw[:, tb, :], ident)
                                ins.then_inc(X["gt"], 1)
                            if (kind, c) == ("u", EC - 1):
                                gather(j + 1, 0)
                            if (kind, c) == ("d", EC - 2):
                                transposes(EC - 1)
                                gather(j + 1, 1)
                    scatter(jobs_here)

        @block.scalar
        def _(act):
            seen = {}

            def need(sig, *key):
                n = sig.count(*key)
                if seen.get(sig.name, 0) < n:
                    seen[sig.name] = n
                    act.wait_ge(sig.sem, n)

            def af(o_, i_, f, *key, **kw):
                act_done.done(act.activation(o_, i_, f, **kw), *key)

            def own():
                act.wait_ge(act_done.sem, act_done.n)

            act.dma_start(rstd[:, 0:16], a["c"]).then_inc(c_loaded, 16)
            act.dma_start(x3, a["x"]).then_inc(x_loaded, 16)
            act.dma_start(co[:, :], a["consts"]).then_inc(const_loaded, 16)
            act.dma_start(pv[:, :], a["pv"][0]).then_inc(par_loaded, 16)
            act.dma_start(mw[:, :], a["mw"][0]).then_inc(mw_loaded, 16)
            need(dve_done, "eps")
            act.wait_ge(c_loaded, 16)
            cs3 = csil[:, :].rearrange("p (k c) -> p k c", k=KT)
            af(cs3[:, :, 0:2], rstd[:, 0:16].rearrange("p (k c) -> p k c", k=KT), ACT.Silu, "csil")

            def mod_rows(l, n):
                need(pe_done, "modrow", l, n)
                if n >= 2:
                    need(pe_done, "modt", l, n - 2)
                af(mod_row(n), mod_bank(l, n)[:, :], ACT.Copy, "modrow", l, n)

            def mod_step(place, i):
                starts, _ = mod_beside(place, i)
                if starts:
                    mod_rows(*starts)

            def high_part(stage, l, i):
                if i >= blocks_of[stage]:
                    return
                j, place, _ = block_item(stage, l, i)
                if place == 0:
                    act.wait_ge(ring_full[j % NS], 16 * (j // NS + 1))
                if i >= DB:
                    need(pe_done, "used", stage, l, i - DB)
                af(block_parts(stage, i)[0], raw_block(stage, l, i), ACT.Copy, "whi", stage, l, i)

            def modulated(stage, l):
                i = 0 if stage == "in" else 1
                need(dve_done, "scale", l, i)
                for k in range(KT + 1):
                    if k < KT:
                        need(dve_done, "xr", stage, l, k)
                        af(h3[:, k, 0:CTX], h3[:, k, 0:CTX], ACT.Identity, "hctx", stage, l, k,
                           scale=nrm[:, 16 * i + 2 * k + 1:16 * i + 2 * k + 2], bias=modv[:, 24 * i + k, 1:2])
                    if k >= 1:
                        need(act_done, "hctx", stage, l, k - 1)
                        need(dve_done, "hlat", stage, l, k - 1)
                        af(h_parts(stage, l, k - 1)[0], h3[:, k - 1, :], ACT.Copy, "hhi", stage, l, k - 1)

            for l in range(L):
                modv = modv_of[l]
                if l == 0:
                    mod_rows(0, 0)
                    mod_rows(0, 1)
                    act.wait_ge(x_loaded, 16)
                for k in range(KT):
                    if l:
                        need(dve_done, "res2", k)
                    af(proj[:, T * k:T * k + T], x3[:, k, :], ACT.Square, "sq1", l, k)
                if l:
                    act.dma_start(x_mid, x3).then_inc(x_stored, 16)
                need(pe_done, "ms1", l)
                af(rstd[:, :], bank[2][:, :], ACT.Sqrt, "rms1", l, bias=small[:, 240:241])
                if l == 0:
                    mod_rows(0, 2)
                    mod_rows(0, 3)
                for i in range(2):
                    high_part("in", l, i)
                modulated("in", l)
                act.dma_start(h_mid, hbuf[:, :]).then_inc(h_stored, 16)
                def q_rms(i):
                    need(pe_done, "qms", l, i)
                    if i >= 1:
                        need(dve_done, "qn", l, i - 1)
                    if i < 4:
                        af(rstd[:, :], bank[4][:, :], ACT.Sqrt, "qrms", l, i, scale=float(HD), bias=small[:, 243:244])
                    else:
                        af(rstd[:, :], bank[4][:, :], ACT.Sqrt, "qrms", l, i, bias=small[:, 240:241])

                for bi in range(20):
                    high_part("in", l, bi + 2)
                    need(pe_done, "proj", l, bi)
                    if 2 <= bi < 8:
                        if l == 1 and bi == 2:
                            act.wait_ge(x_stored, 16)
                        src = [4, 5, 0, 1, 2, 3][bi - 2]
                        af(att[:, src, :], bank[bi % 4][:, :], ACT.Copy, "proj", l, bi)
                    else:
                        m = bi if bi < 2 else bi - 6
                        if m >= 2:
                            need(dve_done, "shift", l, m - 2)
                        pad = wk(8192 + 516 * (m % 2), 516, 2)
                        af(pad[:, :, 1:257], bank[bi % 4][:, :].rearrange("p (a b) -> p a b", a=2), ACT.Copy, "proj", l, bi)
                    if bi == 8:
                        need(dve_done, "shift", l, 1)
                        own()
                        af(pr[0:64, 0, :], pr[0:64, 0, :], ACT.Tanh, "tanh", l)
                        af(pr[:, 1, :], pr[:, 1, :], ACT.Sigmoid, "glo", l)
                    i = norm_at(bi + 1)
                    if i is not None:
                        if i >= 2:
                            need(pe_done, "qms", l, i - 2)
                        af(wk(3072 + 512 * (i % 2), 512), att[:, i, :], ACT.Square, "qsq", l, i)
                    i = norm_at(bi)
                    if i is not None:
                        q_rms(i)
                    if l == 0:
                        mod_step("proj", bi)
                need(pe_done, "vtok", l)
                af(wk(4096, 512), bank[4][:, :], ACT.Copy, "vtok", l)
                units = attention_units(l)
                for u in range(len(units) + 3):
                    if u < len(units):
                        b, hh, qb = units[u]
                        nk = key_blocks(qb)
                        need(dve_done, "max", l, u)
                        if u >= 3:
                            need(pe_done, "pT", l, u - 3)
                        af(probs(u, nk), score_bank(u)[:, 0:128 * nk], ACT.Exp, bias=soft(u)[:, 1:2], accum_out=soft(u)[:, 2:3])
                        af(soft(u)[:, 3:4], V("sink", b + 4 * hh), ACT.Exp, "exp", l, u, bias=soft(u)[:, 1:2])
                    if 2 <= u < len(units) + 2:
                        v = u - 2
                        nk = key_blocks(units[v][2])
                        need(pe_done, "pT", l, v)
                        if v >= 2:
                            need(pe_done, "pv", l, v - 2)
                        af(probs_T(v)[:, 0:128 * nk], bank[2 + v % 2][:, 0:128 * nk], ACT.Copy, "pT", l, v)
                    if u >= 3:
                        v = u - 3
                        b = units[v][0]
                        if v + 1 == len(units) or units[v + 1][0] != b:
                            need(pe_done, "pv", l, v)
                            c0_, n_ = cols(l)
                            af(ya[:, b, c0_:c0_ + n_], bank[4 + b % 2][:, c0_:c0_ + n_], ACT.Copy, "yatt", l, b)
                    if l == 0:
                        mod_step("att", u)
                if l == 1:
                    need(pe_done, "vdown")
                    af(rstd[0:32, :], bank[7][0:32, :], ACT.Copy, "vdown")
                    for b in range(NB):
                        need(pe_done, "vup", b)
                        if b >= 2:
                            need(dve_done, "vres", b - 2)
                        af(wk(512 * (b % 2), 512), bank[7][:, :], ACT.Sigmoid, "vsig", b, bias=V("v0", b))
                def head(jn, i):
                    _, b, q = jn
                    if i == 0:
                        need(dve_done, "kkt", *jn)
                        af(j_sq, j_kkt, ACT.Square, "kksq", *jn)
                    if i == 1:
                        need(pe_done, "kkss", *jn)
                        af(j_rs, bank[6][:, 256:512], ACT.Sqrt, "kkrms", *jn, bias=small[:, 241:242])
                    if i == 2:
                        need(pe_done, "lora", *jn)
                        for d in range(2):
                            af(j_lw[:, d, :], bank[7][:, 256 * d:256 * d + 256], ACT.Sigmoid, bias=V("w0", 4 * d + b))
                        for d in range(2):
                            af(j_ic[:, d, :], bank[6][:, 256 * d:256 * d + 256], ACT.Sigmoid, "sig", *jn, bias=V("a0", 4 * d + b))
                    if i == 3:
                        need(dve_done, "cum", *jn)
                        af(jj_P[turn(jn)], j_L, ACT.Exp)
                        af(j_Q, j_L, ACT.Exp, "decay", *jn, scale=-1.0)

                def spread(jn, c):
                    _, b, q = jn
                    if c == 2:
                        for h in range(2):
                            af(j_v[64 * h:64 * h + 64, :, 64 * h:64 * h + 64],
                               pr[64 * h:64 * h + 64, 4 + 3 * b, 256 * q:256 * q + 256].rearrange("p (c t) -> p c t", c=4), ACT.Copy)
                    if c == 3:
                        need(dve_done, "kr", *jn)
                        for h in range(2):
                            af(jj_kap[turn(jn)][64 * h:64 * h + 64, :, 64 * h:64 * h + 64], jj_kr[turn(jn)][64 * h:64 * h + 64, :, 0, :],
                               ACT.Copy, "bd", *jn)

                def post(jn, i):
                    if not emits(jn):
                        return
                    if i == 0:
                        need(dve_done, "yc", *jn)
                        af(j_sqp, j_Y, ACT.Square, "ysq", *jn)
                    if i == 1:
                        need(pe_done, "yvar", *jn)
                        af(j_rsp, bank[7][:, 256:512], ACT.Sqrt, "yrms", *jn, bias=small[:, 242:243])

                first = layer_jobs(l)[0][0]
                need(pe_done, "proj", l, 19)
                if l == 1:
                    need(pe_done, "vdown")
                act.wait_ge(h_stored, 16 * (l + 1))
                act.sem_inc(h_free, 1)
                need(dve_done, "ready", l)
                need(pool_done, "zeroed", l)
                for i in range(4):
                    head(first, i)
                for c in range(4):
                    spread(first, c)
                for jn, prev, nxt in layer_jobs(l):
                    b, q = jn[1:]
                    for n in range(5):
                        need(pe_done, "tok", *jn, n)
                        dst = [j_Kt[:, 0:4, :], j_Kt[:, 4:8, :], j_Bt[:, 0:4, :], j_Bt[:, 4:8, :], j_Vt[:, :, :]][n]
                        af(dst, bank[6 + n % 2][:, :].rearrange("p (a b) -> p a b", a=4), ACT.Copy, "tok", *jn, n)
                    for lv in range(1, 6):
                        for d in range(2):
                            need(pe_done, "x", *jn, lv, d)
                            af(j_X[:, 4 * d:4 * d + 4, :], bank[3 * d][:, :].rearrange("p (a b) -> p a b", a=4), ACT.Copy, "x", *jn, lv, d)
                        if prev is not None:
                            post(prev, post_at.get(lv))
                        if nxt is not None:
                            head(nxt, head_at.get(lv))
                    for c in range(NCH):
                        for d in range(2):
                            need(pe_done, "R", *jn, c, d)
                            af(j_R[:, d, :], bank[3 * d][:, 0:128], ACT.Copy, "R", *jn, c, d)
                        if nxt is not None:
                            spread(nxt, c)
                    if emits(jn):
                        need(pe_done, "y", *jn, NCH - 1, 1)
                        for h in range(2):
                            af(j_Y[64 * h:64 * h + 64, :].rearrange("p (c t) -> p c t", c=4),
                               bank[6][64 * h:64 * h + 64, :].rearrange("p (c h t) -> p c h t", c=4, h=2)[:, :, h, :], ACT.Copy, "y", *jn)
                for i in range(3):
                    post(jn, i)
                need(dve_done, "yrw", l)
                own()
                act.dma_start(hbuf[:, :], h_mid).then_inc(h_loaded, 16)
                c0, nt = cols(l)
                for i in range(2):
                    high_part("mo", l, i)
                act.wait_ge(h_loaded, 16 * (l + 1))
                for k in range(KT):
                    af(h_parts("mg", l, k)[0], h3[:, k, c0:c0 + nt], ACT.Copy, "hhi", "mg", l, k)

                def merged_high(n):
                    need(dve_done, "merge", l, n)
                    af(h_parts("wo", l, n)[0], wk(4096 + 512 * n, nt), ACT.Copy, "hhi", "wo", l, n)

                for n in range(KT):
                    st = 4 * (n % 2)
                    if n >= 2:
                        need(dve_done, "merge", l, n - 2)
                    for g in range(2):
                        high_part("mo", l, 2 * n + 2 + g)
                        need(pe_done, "mg", l, n, g)
                        af(wk(8192 + 512 * (2 * (n % 2) + g), nt), bank[st + g][:, 0:nt], ACT.Sigmoid, "mg", l, n, g)
                    if n == 0:
                        act.dma_start(x3, a["x"] if l == 0 else x_mid).then_inc(x_loaded, 16)
                    else:
                        merged_high(n - 1)
                merged_high(KT - 1)
                for k in range(KT):
                    high_part("mo", l, 18 + k)
                    need(dve_done, "res1", l, k)
                    af(wk(12288 + 512 * k, nt), x3[:, k, c0:c0 + nt], ACT.Square, "sq2", l, k)
                need(pe_done, "ms2", l)
                af(rstd[:, 0:nt], bank[0][:, 0:nt], ACT.Sqrt, "rms2", l, bias=small[:, 240:241])
                if l == 1:
                    need(dve_done, "xr2", l)
                    for k in range(KT):
                        af(h3[:, k, CTX:CTX + 128], h3[:, k, CTX:CTX + 128], ACT.Identity, *(("h2", l) if k == KT - 1 else ()),
                           scale=nrm[:, 16 + 2 * k:17 + 2 * k], bias=modv[:, 24 + k, 0:1])
                if l == 0:
                    for i in range(2):
                        high_part("gu", l, i)
                    modulated("gu", l)
                    act.dma_start(pv[:, :], a["pv"][1]).then_inc(par_loaded, 16)
                    act.dma_start(mw[:, :], a["mw"][1]).then_inc(mw_loaded, 16)
                    for f in range(NFF):
                        high_part("gu", l, 2 * f + 2)
                        need(pe_done, "gu", f, 0)
                        if f >= 2:
                            need(dve_done, "hff", f - 2)
                        af(wk(15360 + 512 * (f % 2), 512), bank[2 * (f % 2)][:, :], ACT.Silu, "silu", f)
                        high_part("gu", l, 2 * f + 3)
                        if f % 2:
                            mod_step("ffn", f // 2)
                    mod_step("ffn", 11)
                else:
                    for tb in range(2):
                        for g in range(2):
                            need(pe_done, "htok", tb, g)
                            af(m_htok[:, tb, 512 * g:512 * g + 512], bank[4 + 2 * tb + g][:, :], ACT.Copy, "htok", tb, g)
                    need(dve_done, "gap")
                    af(small[:, 32:34], small[:, 34:36], ACT.Exp, "gap")
                    need(dve_done, "ctrl")
                    jobs_here = act.value_load(ctrl[0:1, NJ + 1:NJ + 2], min_val=NE, max_val=NJ)

                    def gathered(j, g):
                        act.wait_ge(X["gat"], j * 2 + (g + 1))
                        act.activation(xg_hi[:, 4 * g:4 * g + 4, :], bank[6][:, :].rearrange("p (a b) -> p a b", a=4),
                                       ACT.Copy).then_inc(X["xg"], 1)

                    def outputs(j):
                        act.wait_ge(X["wused"], j * NU + WB)
                        for g in range(2):
                            act.activation(m_y[:, 512 * g:512 * g + 512], [bank[5], bank[7]][g][:, :], ACT.Copy).then_inc(X["yc"], 1)

                    for g in range(2):
                        gathered(0, g)
                    act.wait_ge(X["zero"], 1)
                    with act.Fori(0, jobs_here) as j:
                        def silu(c):
                            act.wait_ge(X["wused"], j * NU + (WB + unit("g", c, 1) + 1))
                            if c >= 2:
                                act.wait_ge(X["act"], j * EC + (c - 1))
                            act.activation(m_sil[:, c % 2, :], bank[2 * (c % 2)][:, :], ACT.Silu).then_inc(X["silu"], 1)

                        def tr(c):
                            act.wait_ge(X["tr"], j * EC + (c + 1))
                            act.activation(hT_hi[:, c % 2, :, :], bank[4][:, :].rearrange("p (a b) -> p a b", a=4), ACT.Copy)\
                               .then_inc(X["trc"], 1)

                        for m, (kind, c) in enumerate(order):
                            i = N_STATIC + m
                            act.wait_ge(ring_full[i % NS], j * (16 * EC) + 16 * (len(range(i % NS, i, NS)) + 1))
                            for half in range(2):
                                u = unit(kind, c, half)
                                act.wait_ge(X["wused"], count(j, u))
                                act.activation(w_hi[:, u % WB, :], slot(i)[:, UNIT * half:UNIT * half + UNIT], ACT.Copy).then_inc(X["hi"], 1)
                                if (kind, c, half) == ("g", 1, 0):
                                    silu(0)
                                if kind == "d" and half == 0:
                                    if c < EC - 1:
                                        silu(c + 1)
                            if kind == "u" and c >= 1:
                                tr(c - 1)
                            if (kind, c) == ("g", 0):
                                outputs(j)
                            if (kind, c) == ("u", 2):
                                act.wait_ge(X["gt"], j + 1)
                                act.activation(m_GwT, bank[6][:, 0:256], ACT.Copy).then_inc(X["gtc"], 1)
                            if (kind, c) == ("d", EC - 2):
                                gathered(j + 1, 0)
                        tr(EC - 1)
                        gathered(j + 1, 1)
                    outputs(jobs_here)

        @block.vector
        def _(dve):
            seen = {}

            def need(sig, *key):
                n = sig.count(*key)
                if seen.get(sig.name, 0) < n:
                    seen[sig.name] = n
                    dve.wait_ge(sig.sem, n)

            def dv(ins, *key, hold=True):
                dve_done.done(ins, *key)
                if hold:
                    dve.wait_ge(dve_done.sem, dve_done.n)

            tt = dve.tensor_tensor
            ts = dve.tensor_scalar
            stt = dve.scalar_tensor_tensor
            dv(dve.memset(csil[:, :], 0.0), "czero")
            for i, e_ in enumerate((EPS, 1e-12, GN_EPS, HD * EPS)):
                dv(dve.memset(small[:, 240 + i:241 + i], e_), "eps")
            dve.wait_ge(const_loaded, 16)

            def mod_turned(l, n):
                need(pe_done, "modt", l, n)
                dve.wait_ge(par_loaded, 16 * (l + 1))
                bm = pv[:, PV["bmod"][0] + 4 * n:PV["bmod"][0] + 4 * n + 4].unsqueeze(2).to_broadcast([P, 4, 2])
                dv(tt(modv_of[l][:, 4 * n:4 * n + 4, :], mod_bank(l, n)[:, 0:8].rearrange("p (m v) -> p m v", v=2), bm, ALU.add), "modt", l, n)

            def mod_step(place, i):
                _, ends = mod_beside(place, i)
                if ends:
                    mod_turned(*ends)

            def norm_scale(i):
                g_ = pv[:, PV[("norm1", "norm2")[i]][0]:][:, 0:KT].unsqueeze(2).to_broadcast([P, KT, 2])
                n3 = nrm[:, 16 * i:16 * i + 16].rearrange("p (k v) -> p k v", v=2)
                dv(tt(n3, modv[:, 24 * i + 8:24 * i + 16, :], g_, ALU.mult))
                dv(tt(n3, n3, g_, ALU.add), "scale", l, i)

            def low_part(stage, l, i):
                if i >= blocks_of[stage]:
                    return
                need(act_done, "whi", stage, l, i)
                hi, lo = block_parts(stage, i)
                dv(tt(lo, raw_block(stage, l, i), hi.bitcast(f32), ALU.subtract), "wlo", stage, l, i, hold=False)

            def normed(stage, l, k):
                dv(tt(h3[:, k, :], x3[:, k, :], rstd[:, :], ALU.mult), "xr", stage, l, k)

            def modulated(stage, l):
                i = 0 if stage == "in" else 1
                for k in range(KT + 2):
                    if k < KT:
                        if (stage, l) != ("in", 0):
                            normed(stage, l, k)
                        dv(ts(h3[:, k, CTX:T], h3[:, k, CTX:T], nrm[:, 16 * i + 2 * k:16 * i + 2 * k + 1], modv[:, 24 * i + k, 0:1],
                              ALU.mult, ALU.add), "hlat", stage, l, k, hold=False)
                    if k >= 2:
                        need(act_done, "hhi", stage, l, k - 2)
                        hi, lo = h_parts(stage, l, k - 2)
                        dv(tt(lo, h3[:, k - 2, :], hi.bitcast(f32), ALU.subtract), "hlo", stage, l, k - 2, hold=False)

            for l in range(L):
                modv = modv_of[l]
                if l == 0:
                    mod_turned(0, 0)
                need(act_done, "rms1", l)
                dv(dve.reciprocal(rstd[:, :], rstd[:, :]))
                if l == 0:
                    mod_turned(0, 1)
                    dve.wait_ge(x_loaded, 16)
                    for k in range(KT):
                        normed("in", 0, k)
                    for n in range(2, 4):
                        mod_turned(0, n)
                norm_scale(0)
                modulated("in", l)
                c0m = small[:, 64:78]
                mu0 = pv[:, PV["mu0"][0]:PV["mu0"][1]]
                mu1 = pv[:, PV["mu1"][0]:PV["mu1"][1]]
                dv(tt(c0m, mu0, mu1, ALU.add))
                dv(ts(c0m, c0m, -1.0, 1.0, ALU.mult, ALU.add))
                for i in range(2):
                    pad = wk(8192 + 516 * i, 516, 2)
                    dv(dve.memset(pad[:, :, 0:1], 0.0), hold=False)
                    dv(dve.memset(pad[:, :, 257:258], 0.0))
                for m in range(14):
                    if l == 0 and m == 2:
                        mod_step("proj", 4)
                    need(act_done, "proj", l, m if m < 2 else m + 6)
                    pad = wk(8192 + 516 * (m % 2), 516, 2)
                    o_ = pr[:, m, :].rearrange("p (a b) -> p a b", a=2)
                    dv(ts(o_, pad[:, :, 1:257], c0m[:, m:m + 1], None, ALU.mult))
                    dv(stt(o_, pad[:, :, 0:256], V("mu0", m), o_, ALU.mult, ALU.add))
                    dv(stt(o_, pad[:, :, 2:258], V("mu1", m), o_, ALU.mult, ALU.add), "shift", l, m)
                    i = norm_at(m + 6)
                    if i is not None:
                        need(act_done, "qrms", l, i)
                        dv(dve.reciprocal(rstd[:, :], rstd[:, :]))
                        dv(stt(att[:, i, :], att[:, i, :], V("qn") if i < 4 else V("kn"), rstd[:, :], ALU.mult, ALU.mult), "qn", l, i)
                    i = norm_at(m + 5)
                    if i is not None:
                        need(pe_done, "qrot", l, i)
                        t_ = wk(9728, 256)
                        dv(tt(t_, bank[5][:, 0:256], C("sin"), ALU.mult))
                        dv(tt(att[:, i, CTX:T], att[:, i, CTX:T], C("cos"), ALU.mult))
                        dv(tt(att[:, i, CTX:T], att[:, i, CTX:T], t_, ALU.add), "qrot", l, i)
                    if l == 0 and m >= 2:
                        mod_step("proj", m + 6)
                units = attention_units(l)
                for u in range(len(units) + 1):
                    if u < len(units):
                        b, hh, qb = units[u]
                        need(pe_done, "score", l, u)
                        dv(dve.tensor_reduce(soft(u)[:, 0:1], score_bank(u)[:, 0:128 * key_blocks(qb)], AX.X, ALU.max))
                        dv(ts(soft(u)[:, 1:2], soft(u)[:, 0:1], V("sink", b + 4 * hh), -1.0, ALU.max, ALU.mult), "max", l, u)
                    if u >= 1:
                        v = u - 1
                        need(act_done, "exp", l, v)
                        dv(tt(soft(v)[:, 4:5], soft(v)[:, 2:3], soft(v)[:, 3:4], ALU.add))
                        dv(dve.reciprocal(soft(v)[:, 5:6], soft(v)[:, 4:5]))
                        p_ = probs(v, key_blocks(units[v][2]))
                        dv(ts(p_, p_, soft(v)[:, 5:6], None, ALU.mult), "prob", l, v)
                        if l == 0:
                            mod_step("att", v)
                norm_scale(1)
                if l == 1:
                    for b in range(NB):
                        need(act_done, "vsig", b)
                        dve.wait_ge(vf_loaded, 16)
                        v_ = pr[:, 4 + 3 * b, :]
                        t_ = wk(1024, 512)
                        dv(tt(t_, wk(2048 + 512 * b, 512), v_, ALU.subtract))
                        dv(tt(t_, t_, wk(512 * (b % 2), 512), ALU.mult))
                        dv(tt(v_, v_, t_, ALU.add), "vres", b)
                need(act_done, "glo", l)
                need(act_done, "yatt", l, NB - 1)
                need(pool_done, "zeroed", l)
                dve.wait_ge(h_free, l + 1)
                dv(dve.memset(wk(*J["S"]), 0.0), "ready", l)
                c4 = lambda ap: ap.rearrange("p (c t) -> p c t", c=4)

                def rkv(jn):
                    _, b, q = jn
                    return (pr[:, 2 + 3 * b + i, 256 * q:256 * q + 256] for i in range(3))

                def head(jn, i):
                    _, b, q = jn
                    r_, k_, v_ = rkv(jn)
                    j_cv = jj_cv[turn(jn)]
                    if i == 0:
                        dv(ts(j_kkt, k_, V("kk", b), None, ALU.mult), "kkt", *jn)
                    if i == 1:
                        need(act_done, "kkrms", *jn)
                        dv(dve.reciprocal(j_rs, j_rs))
                        dv(tt(j_kk, j_kkt, j_rs, ALU.mult))
                    if i == 2:
                        need(act_done, "sig", *jn)
                        dv(ts(j_lw, j_lw, DECAY, None, ALU.mult))
                        for d in range(2):
                            for c in range(4):
                                o_, i_ = j_L[:, d, CH * c:CH * c + CH], j_lw[:, d, CH * c:CH * c + CH]
                                if d:
                                    o_, i_ = o_[:, ::-1], i_[:, ::-1]
                                dv(dve.tensor_tensor_scan(out=o_, data0=i_, data1=i_, initial=0.0, op0=ALU.add, op1=ALU.bypass),
                                   *(("cum",) + jn if (d, c) == (1, 3) else ()), hold=(d, c) == (1, 3))
                    if i == 3:
                        dv(ts(j_kh, j_ic, 1.0, V("ka", b), ALU.subtract, ALU.mult))
                        k2 = k_.unsqueeze(1).to_broadcast([P, 2, 256])
                        dv(stt(j_kh, j_kh, 1.0, k2, ALU.add, ALU.mult))
                        dv(tt(j_bb, j_ic, j_kk.unsqueeze(1).to_broadcast([P, 2, 256]), ALU.mult), "bb", *jn)
                    if i == "coef":
                        dv(tt(j_rs, j_kh[:, 0, :], j_kh[:, 1, :], ALU.add))
                        dv(stt(j_rs, j_rs, V("rk", b), r_, ALU.mult, ALU.mult), "coef", *jn)
                    if i == 4:
                        need(pe_done, "coef", *jn)
                        dv(tt(j_cv, bank[7][:, 0:256], v_, ALU.mult), "cv", *jn)

                def spread(jn, c):
                    r_, k_, v_ = rkv(jn)
                    if c == 0:
                        need(act_done, "decay", *jn)
                        for h in range(2):
                            hs = slice(64 * h, 64 * h + 64)
                            s8 = lambda ap: ap.rearrange("p d (c t) -> p (d c) t", c=4)
                            dv(tt(j_K[hs, :, hs], s8(j_kh[hs, :, :]), s8(j_Q[hs, :, :]), ALU.mult), *(("bd",) + jn if h else ()), hold=False)
                    if c in (1, 2):
                        d = c - 1
                        kkc = c4(j_kk)
                        Pd = c4(jj_P[turn(jn)][:, d, :])
                        kr = jj_kr[turn(jn)]
                        dv(tt(kr[:, 4 * d:4 * d + 4, 1, :], c4(r_), Pd, ALU.mult), hold=False)
                        if d == 0:
                            dv(tt(kr[:, 0:4, 0, 1:64], kkc[:, :, 1:64], Pd[:, :, 0:63], ALU.mult), hold=False)
                            dv(dve.tensor_copy(kr[:, 0:4, 0, 0:1], kkc[:, :, 0:1]), hold=False)
                        else:
                            dv(tt(kr[:, 4:8, 0, 0:63], kkc[:, :, 0:63], Pd[:, :, 1:64], ALU.mult), hold=False)
                            dv(dve.tensor_copy(kr[:, 4:8, 0, 63:64], kkc[:, :, 63:64]), "kr", *jn, hold=False)

                def post(jn, i):
                    _, b, q = jn
                    if not emits(jn):
                        return
                    if i == 0:
                        need(pe_done, "ymean", *jn)
                        dv(tt(j_Y, j_Y, bank[7][:, 0:256], ALU.subtract), "yc", *jn)
                    if i == 2:
                        need(act_done, "yrms", *jn)
                        dv(dve.reciprocal(j_rsp, j_rsp))
                        dv(tt(j_Y, j_Y, j_rsp, ALU.mult))
                        dv(ts(j_Y, j_Y, V("lg", b), V("lb", b), ALU.mult, ALU.add))
                        dv(tt(j_Y, j_Y, jj_cv[turn(jn)], ALU.add))
                        need(pe_done, "gate", *jn)
                        r_, _, _ = rkv(jn)
                        dv(tt(r_, j_Y, bank[6][:, 0:256], ALU.mult), "post", *jn)

                first = layer_jobs(l)[0][0]
                for i in (0, 1, 2, 3, "coef", 4):
                    head(first, i)
                for c in range(4):
                    spread(first, c)
                for jn, prev, nxt in layer_jobs(l):
                    b, q = jn[1:]
                    emit = emits(jn)
                    j_P = jj_P[turn(jn)]
                    if q == 0 and b:
                        dv(dve.memset(wk(*J["S"]), 0.0), hold=False)
                    for w_ in range(2):
                        for sp_ in range(4):
                            need(pe_done, "gram", *jn, w_, sp_)
                            d = sp_ // 2
                            g5 = bank[4 * w_ + sp_][:, :].rearrange("p (s h r t) -> p s h r t", s=2, h=2, r=2)
                            for r2, (dst, msk) in enumerate(((j_Lk, strict), (j_Qk, incl)) if w_ == 0 else ((j_U, strict), (j_Qb, incl))):
                                if r2 == 1 and not emit:
                                    continue
                                dv(tt(dst[:, 2 * sp_:2 * sp_ + 2, :].rearrange("p s (h t) -> p s h t", h=2), g5[:, :, :, r2, :],
                                      msk[:, d, :].rearrange("p (h t) -> p h t", h=2).unsqueeze(1).to_broadcast([P, 2, 2, 64]), ALU.mult),
                                   "gram", *jn, w_, sp_, hold=False)
                    idb = ident.unsqueeze(1).to_broadcast([P, 4, 128])
                    for d in range(2):
                        need(pool_done, "um", *jn, 0, d)
                        dv(stt(j_N[:, 4 * d:4 * d + 4, :], j_Um[:, 4 * d:4 * d + 4, :], -1.0, idb, ALU.mult, ALU.add), "n", *jn, d, hold=False)
                    for lv in range(6):
                        for d in range(2):
                            N_, M_ = j_N[:, 4 * d:4 * d + 4, :], j_M[:, 4 * d:4 * d + 4, :]
                            if lv == 0:
                                need(pe_done, "x", *jn, lv, d)
                                need(pe_done, "tok", *jn, 1)
                                dv(stt(M_, bank[3 * d][:, :].rearrange("p (a b) -> p a b", a=4), -1.0, idb, ALU.mult, ALU.add),
                                   "mn", *jn, lv, d, hold=d == 1)
                            else:
                                need(pe_done, "mn", *jn, lv, d)
                                if lv < 5:
                                    dv(tt(M_, M_, bank[3 * d + 1][:, :].rearrange("p (a b) -> p a b", a=4), ALU.subtract), hold=False)
                                dv(tt(N_, N_, bank[3 * d + 2][:, :].rearrange("p (a b) -> p a b", a=4), ALU.subtract), "mn", *jn, lv, d,
                                   hold=d == 1)
                        if lv and prev is not None:
                            post(prev, post_at.get(lv))
                        if lv and nxt is not None:
                            head(nxt, head_at.get(lv))
                    for c in range(NCH):
                        for d in range(2):
                            need(pe_done, "U", *jn, c, d)
                            dv(ts(j_Un[:, d, :], bank[3 * d][:, 128:256], -1.0, None, ALU.mult), "U", *jn, c, d, hold=False)
                        for d in range(2):
                            need(pe_done, "state", *jn, c, d)
                            ch = c if d == 0 else NCH - 1 - c
                            last = CH * ch + (CH - 1 if d == 0 else 0)
                            dv(tt(j_S[:, d, :], j_S[:, d, :], bank[3 * d][:, 256:384], ALU.add))
                            dv(ts(j_S[:, d, :], j_S[:, d, :], j_P[:, d, last:last + 1], None, ALU.mult), "state", *jn, c, d)
                        if nxt is not None:
                            spread(nxt, c)
                            if c == 0:
                                head(nxt, "coef")
                            if c == 2:
                                head(nxt, 4)
                for i in range(3):
                    post(jn, i)
                dve_done.book[("dve", "yrw", l)] = dve_done.n
                c0, nt = cols(l)
                for i in range(2):
                    low_part("mo", l, i)
                for k in range(KT):
                    need(act_done, "hhi", "mg", l, k)
                    hi, lo = h_parts("mg", l, k)
                    dv(tt(lo, h3[:, k, c0:c0 + nt], hi.bitcast(f32), ALU.subtract), "hlo", "mg", l, k, hold=False)

                def merged_low(n):
                    need(act_done, "hhi", "wo", l, n)
                    hi, lo = h_parts("wo", l, n)
                    dv(tt(lo, wk(4096 + 512 * n, nt), hi.bitcast(f32), ALU.subtract), "hlo", "wo", l, n, hold=False)

                for n in range(KT):
                    for g in range(2):
                        low_part("mo", l, 2 * n + 2 + g)
                    st = 4 * (n % 2)
                    s0, s1 = (wk(8192 + 512 * (2 * (n % 2) + g), nt) for g in range(2))
                    m_ = wk(4096 + 512 * n, nt)
                    need(act_done, "mg", l, n, 1)
                    need(pe_done, "mb", l, n, 0)
                    dv(tt(m_, bank[st + 2][:, 0:nt], s0, ALU.mult), hold=False)
                    dv(tt(s1, bank[st + 3][:, 0:nt], s1, ALU.mult))
                    dv(tt(m_, m_, s1, ALU.add), "merge", l, n)
                    if n >= 1:
                        merged_low(n - 1)
                merged_low(KT - 1)
                dve.wait_ge(x_loaded, 16 * (l + 2))
                spans = [(0, CTX, 1), (CTX, LAT, 0)] if l == 0 else [(CTX, LAT, 0)]
                for n in range(KT):
                    low_part("mo", l, 18 + n)
                    need(pe_done, "wo", l, n)
                    for s0_, n_, v in spans:
                        dv(stt(x3[:, n, s0_:s0_ + n_], bank[n % 2][:, s0_ - c0:s0_ - c0 + n_], modv[:, 16 + n, v:v + 1],
                               x3[:, n, s0_:s0_ + n_], ALU.mult, ALU.add), "res1", l, n, hold=False)
                need(act_done, "rms2", l)
                dv(dve.reciprocal(rstd[:, 0:nt], rstd[:, 0:nt]))
                if l == 1:
                    dv(tt(h3[:, :, c0:c0 + nt], x3[:, :, c0:c0 + nt], rstd[:, 0:nt].unsqueeze(1).to_broadcast([P, KT, nt]), ALU.mult), "xr2", l)
                    for k in range(KT):
                        dv(ts(h3[:, k, CTX + 128:T], h3[:, k, CTX + 128:T], nrm[:, 16 + 2 * k:17 + 2 * k], modv[:, 24 + k, 0:1], ALU.mult, ALU.add),
                           *(("h2", l) if k == KT - 1 else ()), hold=False)
                if l == 0:
                    for i in range(2):
                        low_part("gu", l, i)
                    modulated("gu", l)
                    for f in range(NFF):
                        low_part("gu", l, 2 * f + 2)
                        need(act_done, "silu", f)
                        need(pe_done, "gu", f, 1)
                        dv(tt(wk(4096 + 512 * f, 512), bank[2 * (f % 2) + 1][:, :], wk(15360 + 512 * (f % 2), 512), ALU.mult), "hff", f, hold=False)
                        low_part("gu", l, 2 * f + 3)
                        if f % 2:
                            mod_step("ffn", f // 2)
                    for n in range(KT):
                        need(pe_done, "dn", n)
                        for s0_, n_, v in spans:
                            dv(stt(x3[:, n, s0_:s0_ + n_], bank[n % 2][:, s0_:s0_ + n_], modv[:, 40 + n, v:v + 1],
                                   x3[:, n, s0_:s0_ + n_], ALU.mult, ALU.add), "res2", n)
                        mod_step("ffn", 11 + n)
                    dve_done.book[("dve", "ffn", 0)] = dve_done.n
                    continue
                need(pe_done, "logits")
                lg = small[:, 96:112].rearrange("p (t e) -> p t e", t=2)
                top = small[:, 112:128].rearrange("p (t e) -> p t e", t=2)
                dv(dve.tensor_copy(lg, bank[1][:, 0:16].rearrange("p (t e) -> p t e", t=2)))
                ti = tidx[:, :].rearrange("p (t e) -> p t e", t=2)
                for tb in range(2):
                    dv(dve.max(top[:, tb, :], lg[:, tb, :]))
                    dv(dve.max_index(ti[:, tb, :], top[:, tb, :], lg[:, tb, :]))
                tf = small[:, 128:144].rearrange("p (t e) -> p t e", t=2)
                dv(dve.tensor_copy(tf, ti))
                dv(tt(small[:, 34:36].unsqueeze(2), top[:, :, 1:2], top[:, :, 0:1], ALU.subtract), "gap")
                mask = rt[:, 0:16].rearrange("p (t e) -> p t e", t=2)
                w8 = rt[:, 16:32].rearrange("p (t e) -> p t e", t=2)
                one1 = rt[:, 32:48].rearrange("p (t e) -> p t e", t=2)
                iota = C("iota")
                for tb in range(2):
                    dv(ts(one1[:, tb, :], iota[:, 0:8], tf[:, tb, 0:1], None, ALU.is_equal))
                    dv(ts(w8[:, tb, :], iota[:, 0:8], tf[:, tb, 1:2], None, ALU.is_equal))
                dv(tt(mask, one1, w8, ALU.add), "mask")
                need(act_done, "gap")
                dv(ts(small[:, 36:38], small[:, 32:34], 1.0, None, ALU.add))
                dv(dve.reciprocal(small[:, 38:40], small[:, 36:38]))
                dv(tt(small[:, 40:42], small[:, 32:34], small[:, 38:40], ALU.mult))
                for tb in range(2):
                    dv(ts(w8[:, tb, :], w8[:, tb, :], small[:, 40 + tb:41 + tb], None, ALU.mult))
                    dv(stt(w8[:, tb, :], one1[:, tb, :], small[:, 38 + tb:39 + tb], w8[:, tb, :], ALU.mult, ALU.add))
                need(pe_done, "rank")
                keys = rt[:, 48:80].rearrange("p (t e) -> p t e", t=2)
                wts = rt[:, 80:112].rearrange("p (t e) -> p t e", t=2)
                dv(dve.memset(rt[:, 48:112], 0.0))
                rank = bank[0][:, 0:16].rearrange("p (t e) -> p t e", t=2)
                dv(tt(keys[:, :, 0:8], rank, mask, ALU.mult))
                dv(ts(one1, mask, 1.0, 1e4, ALU.subtract, ALU.mult))
                dv(tt(keys[:, :, 0:8], keys[:, :, 0:8], one1, ALU.add))
                dv(dve.tensor_copy(wts[:, :, 0:8], w8))
                over = rt[:, 112:120]
                place = rt[:, 120:128]
                dv(ts(over, bank[0][:, 16:24], 128.5, None, ALU.is_gt))
                dv(dve.tensor_tensor_scan(out=place, data0=over, data1=over, initial=0.0, op0=ALU.add, op1=ALU.bypass))
                for i in range(3):
                    sel = rt[:, 128:136]
                    dv(ts(sel, place, float(i + 1), None, ALU.is_equal))
                    dv(tt(sel, sel, over, ALU.mult))
                    dv(tt(rt[:, 136:144], sel, iota[:, 0:8], ALU.mult))
                    dv(dve.tensor_reduce(rt[:, 144 + i:145 + i], rt[:, 136:144], AX.X, ALU.add))
                    for tb in range(2):
                        dv(stt(rt[:, 136:144], keys[:, tb, 0:8], -128.0, sel, ALU.add, ALU.mult))
                        dv(dve.tensor_reduce(keys[:, tb, 8 + i:9 + i], rt[:, 136:144], AX.X, ALU.add))
                        dv(tt(rt[:, 136:144], w8[:, tb, :], sel, ALU.mult))
                        dv(dve.tensor_reduce(wts[:, tb, 8 + i:9 + i], rt[:, 136:144], AX.X, ALU.add))
                dv(dve.memset(ctrl[0:1, :], 0))
                dv(dve.tensor_copy(ctrl[0:1, 8:11], rt[0:1, 144:147]))
                dv(dve.tensor_copy(ctrl[0:1, NJ:NJ + 1], place[0:1, 7:8]))
                dv(ts(rt[0:1, 150:151], place[0:1, 7:8], float(NE), None, ALU.add))
                dv(dve.tensor_copy(ctrl[0:1, NJ + 1:NJ + 2], rt[0:1, 150:151]), "ctrl")
                dv(dve.memset(m_GwT, 0.0), "gwt0")
                jobs_here = dve.value_load(ctrl[0:1, NJ + 1:NJ + 2], min_val=NE, max_val=NJ)

                def one_hot(j):
                    for tb in range(2):
                        dve.tensor_scalar(m_G[:, tb, :], iota, keys[:, tb, bass.ds(j, 1)], None, ALU.is_equal).then_inc(X["key2"], 1)
                    dve.wait_ge(X["key2"], j * 2 + 2)
                    for tb in range(2):
                        ins = dve.tensor_scalar(m_Gw[:, tb, :], m_G[:, tb, :], wts[:, tb, bass.ds(j, 1)], None, ALU.mult)
                    ins.then_inc(X["key"], 1)

                def gathered(j, g):
                    dve.wait_ge(X["xg"], j * 2 + (g + 1))
                    dve.tensor_tensor(xg_lo[:, 4 * g:4 * g + 4, :], bank[6][:, :].rearrange("p (a b) -> p a b", a=4),
                                      xg_hi[:, 4 * g:4 * g + 4, :].bitcast(f32), ALU.subtract).then_inc(X["xl"], 1)

                def scattered(j, units_done):
                    for g in range(4):
                        dve.wait_ge(X["sc"], j * 4 + (g + 1))
                        if g == 0:
                            dve.wait_ge(X["lo"], j * NU + units_done)
                        for k in range(2):
                            kk_ = 2 * g + k
                            ins = dve.scalar_tensor_tensor(x3[:, kk_, CTX:T], bank[4 + g][:, 256 * k:256 * k + 256], modv[:, 40 + kk_, 0:1],
                                                           x3[:, kk_, CTX:T], ALU.mult, ALU.add)
                        ins.then_inc(X["add"], 1)

                one_hot(0)
                for g in range(2):
                    gathered(0, g)
                with dve.Fori(0, jobs_here) as j:
                    def hidden(c):
                        dve.wait_ge(X["silu"], j * EC + (c + 1))
                        dve.wait_ge(X["wused"], j * NU + (WB + unit("u", c, 1) + 1))
                        if c >= 2:
                            dve.wait_ge(X["tr"], j * EC + (c - 1))
                        dve.tensor_tensor(m_hid[:, c % 2, :], bank[2 * (c % 2) + 1][:, :], m_sil[:, c % 2, :], ALU.mult).then_inc(X["act"], 1)

                    def tr(c):
                        dve.wait_ge(X["trc"], j * EC + (c + 1))
                        dve.tensor_tensor(hT_lo[:, c % 2, :, :], bank[4][:, :].rearrange("p (a b) -> p a b", a=4),
                                          hT_hi[:, c % 2, :, :].bitcast(f32), ALU.subtract).then_inc(X["trl"], 1)

                    for m, (kind, c) in enumerate(order):
                        for half in range(2):
                            u = unit(kind, c, half)
                            dve.wait_ge(X["hi"], count(j, u))
                            dve.tensor_tensor(w_lo[:, u % WB, :], slot(N_STATIC + m)[:, UNIT * half:UNIT * half + UNIT],
                                              w_hi[:, u % WB, :].bitcast(f32), ALU.subtract).then_inc(X["lo"], 1)
                        if kind == "g" and c >= 1:
                            hidden(c - 1)
                        if kind == "u" and c >= 1:
                            tr(c - 1)
                        if (kind, c) == ("g", 1):
                            scattered(j, unit("g", 1, 1) + 1)
                        if (kind, c) == ("u", 3):
                            dve.wait_ge(X["gt"], j + 1)
                            one_hot(j + 1)
                        if (kind, c) == ("d", EC - 2):
                            gathered(j + 1, 0)
                            hidden(EC - 1)
                    tr(EC - 1)
                    gathered(j + 1, 1)
                scattered(jobs_here, 0)
                dve.wait_ge(X["add"], jobs_here * 4 + 4)
                dv(dve.tensor_copy(small[:, 200:201], small[:, 34:35]), "final")

        @block.gpsimd
        def _(pool):
            seen = {}

            def need(sig, *key):
                n = sig.count(*key)
                if seen.get(sig.name, 0) < n:
                    seen[sig.name] = n
                    pool.wait_ge(sig.sem, n)

            for l in range(L):
                for i in range(20):
                    need(act_done, "whi", "in", l, i)
                    hi, lo = block_parts("in", i)
                    pool_done.done(pool.tensor_tensor(lo, raw_block("in", l, i), hi.bitcast(f32), ALU.subtract), "wlo", "in", l, i)
                if l == 0:
                    need(dve_done, "shift", 0, 13)
                    for b in range(NB):
                        pool.dma_start(vf_mid[:, b, :], pr[:, 4 + 3 * b, :]).then_inc(vf_stored, 16)
                    pool.wait_ge(vf_stored, 16 * NB)
                    need(act_done, "yatt", 0, NB - 1)
                else:
                    need(act_done, "yatt", 1, NB - 1)
                    pool.dma_start(wk(2048, 2048, NB), vf_mid).then_inc(vf_loaded, 16)
                    need(dve_done, "vres", NB - 1)
                pool.wait_ge(h_free, l + 1)
                for v_ in (wk(*J["kapbd"]), hb(1024, 1024), wk(*J["Kbd"]), wk(*J["Bbd"]), wk(*J["vbd"])):
                    pool_done.done(pool.memset(v_, 0.0), "zeroed", l)
                pool.wait_ge(pool_done.sem, pool_done.n)

                def spread(jn):
                    need(dve_done, "bb", *jn)
                    need(act_done, "decay", *jn)
                    for h in range(2):
                        hs = slice(64 * h, 64 * h + 64)
                        s8 = lambda ap: ap.rearrange("p d (c t) -> p (d c) t", c=4)
                        pool_done.done(pool.tensor_tensor(j_B[hs, :, hs], s8(j_bb[hs, :, :]), s8(j_Q[hs, :, :]), ALU.mult), "bd", *jn)

                spread(layer_jobs(l)[0][0])
                for jn, prev, nxt in layer_jobs(l):
                    for lv in range(6):
                        for d in range(2):
                            if lv == 0:
                                need(dve_done, "gram", *jn, 1, 2 * d + 1)
                            else:
                                need(pe_done, "x", *jn, lv - 1, d)
                                if lv == 1:
                                    need(dve_done, "n", *jn, d)
                            pool_done.done(pool.tensor_tensor(j_Um[:, 4 * d:4 * d + 4, :], j_U[:, 4 * d:4 * d + 4, :],
                                                              level[:, 2 * lv + d, :].unsqueeze(1).to_broadcast([P, 4, 128]), ALU.mult),
                                           "um", *jn, lv, d)
                    if nxt is not None:
                        need(pe_done, "mn", *jn, 5, 1)
                        spread(nxt)
    return book


_OUT = (P, KT, LAT)


def kernel(**inputs):
    import numpy as _np
    import concourse.bacc as _bacc
    from concourse import mybir as _mybir
    from concourse.bass_utils import run_bass_kernel_spmd as _run

    arrays = lay_out({k: _np.asarray(v) for k, v in inputs.items()})
    book = {}
    for _ in range(2):
        nc = _bacc.Bacc("TRN2", target_bir_lowering=False, num_devices=1)
        f32 = _mybir.dt.float32
        aps = {n: nc.dram_tensor("in_" + n, v.shape, f32, kind="ExternalInput").ap() for n, v in arrays.items()}
        out = nc.dram_tensor("out_0", _OUT, f32, kind="ExternalOutput").ap()
        x_mid = nc.dram_tensor("x_mid", (P, KT, T), f32, kind="Internal").ap()
        vf_mid = nc.dram_tensor("vf_mid", (P, NB, T), f32, kind="Internal").ap()
        h_mid = nc.dram_tensor("h_mid", (P, KT * T), f32, kind="Internal").ap()
        build(nc, aps, out, x_mid, vf_mid, h_mid, book)
    r = _run(nc, [{"in_" + n: v for n, v in arrays.items()}], core_ids=[0])
    y = r.results[0]["out_0"]
    return _np.ascontiguousarray(y.transpose(2, 1, 0).reshape(1, LAT, D))


def lay_out(i):
    c32 = np.ascontiguousarray

    def kp(w):
        s = w.shape
        w = w.reshape(s[:-2] + (s[-2] // P, P, s[-1]))
        return np.swapaxes(w, -3, -2)

    def blocks(w, n):
        w = kp(w)
        return w.reshape(P, w.shape[1], n, P).transpose(0, 2, 1, 3)

    o = {}
    x = np.concatenate([i["ctx"][0], i["x"][0]], 0)
    o["x"] = c32(x.T.reshape(KT, P, T).transpose(1, 0, 2))
    c = np.stack([i["c"][0], i["c_ctx"]], -1)
    o["c"] = c32(c.reshape(KT, P, 2).transpose(1, 0, 2).reshape(P, 16))
    o["consts"] = constants()
    o["w_mod"] = c32(kp(i["w_mod"]).reshape(L, P, KT, 12, 512).transpose(0, 3, 1, 2, 4).reshape(L, 12, P, 4096))
    rw, at = 3 * RW + 256, 768
    hp = np.concatenate([np.r_[64 * h:64 * h + 64, 64 * (h + 4):64 * (h + 4) + 64] for h in range(4)])
    blk = np.arange(P)
    colsets = [3 * RW + blk, 3 * RW + 128 + blk, rw + 512 + blk, rw + 640 + blk] + [rw + hp[P * b:P * b + P] for b in range(4)]
    rwcols = [3 * RW + blk, 3 * RW + 128 + blk]
    for b in range(NB):
        for part in range(3):
            colsets.append(part * RW + P * b + blk)
            rwcols.append(part * RW + P * b + blk)
    win, wmrg, wout, pvs, mws = [], [], [], [], []
    for l in range(L):
        w = i["w_in"][l]
        bl = blocks(w[:, np.concatenate(colsets)], 20)
        win.append(bl.reshape(P, 5, 4096).transpose(1, 0, 2))
        g = w[:, rw + at:]
        g0, g1 = blocks(g[:, :D], KT), blocks(g[:, D:], KT)
        b0, b1 = blocks(i["w_br_rwkv"][l], KT), blocks(i["w_br_attn"][l][hp], KT)
        m = np.concatenate([v.reshape(P, KT, -1) for v in (g0, g1, b0, b1)], -1)
        wmrg.append(m.transpose(1, 0, 2))
        wout.append(blocks(i["w_out"][l], KT).reshape(P, 2, 4096).transpose(1, 0, 2))
        pv = np.zeros((P, NPV), np.float32)

        def put(name, v):
            pv[:, PV[name][0]:PV[name][1]] = v

        put("norm1", i["norm1"][l].reshape(KT, P).T)
        put("norm2", i["norm2"][l].reshape(KT, P).T)
        put("bmod", i["b_mod"][l].reshape(48, P).T)
        for q in range(2):
            put(f"mu{q}", np.stack([i["tshift"][l, q][cs] for cs in rwcols], 1))
        put("w0", i["w0"][l].reshape(8, P).T)
        put("a0", i["a0"][l].reshape(8, P).T)
        for n, s in (("kk", "k_k"), ("ka", "k_a"), ("lg", "lnx_g"), ("lb", "lnx_b")):
            put(n, i[s][l].reshape(NB, P).T)
        put("rk", i["r_k"][l].reshape(NB, P).T)
        if l:
            put("v0", i["v0"][l - 1].reshape(NB, P).T)
        put("qn", np.concatenate([i["q_norm"][l]] * 2)[:, None])
        put("kn", np.concatenate([i["k_norm"][l]] * 2)[:, None])
        put("sink", np.broadcast_to(i["sink"][l][None], (P, 8)))
        pvs.append(pv)
        mw = np.zeros((P, 2304), np.float32)
        mw[0:64, 0:1024] = i["w_decay_up"][l].transpose(1, 0, 2).reshape(64, 1024)
        mw[64:128, 0:1024] = i["w_iclr_up"][l].transpose(1, 0, 2).reshape(64, 1024)
        mw[:, 1024:1536] = i["w_gate_up"][l]
        if l:
            mw[:, 1536:1792] = kp(i["w_vres_down"][l - 1]).reshape(P, 256)
            mw[0:32, 1792:2304] = i["w_vres_up"][l - 1]
        mws.append(mw)
    o["w_in"], o["w_mrg"], o["w_out"] = c32(np.stack(win)), c32(np.stack(wmrg)), c32(np.stack(wout))
    o["pv"], o["mw"] = np.stack(pvs), np.stack(mws)
    g, u = blocks(i["ffn_gate"][0], NFF), blocks(i["ffn_up"][0], NFF)
    gu = np.stack([g, u], 2)
    o["w_gu"] = c32(gu.reshape(P, 11, 4096).transpose(1, 0, 2))
    o["w_dn"] = c32(blocks(i["ffn_down"][0], KT).reshape(P, KT, FF).transpose(1, 0, 2))
    o["router"] = c32(kp(i["router"][0]).reshape(P, 64))
    g = kp(i["moe_gate"][0]).reshape(NE, P, KT, EC, 512)
    u = kp(i["moe_up"][0]).reshape(NE, P, KT, EC, 512)
    d = kp(i["moe_down"][0]).reshape(NE, P, EC, 4, D)
    gu = lambda w, c: w[:, :, :, c, :].reshape(NE, P, 4096)
    parts = [gu(g, 0), gu(u, 0)]
    for c in range(1, EC):
        parts += [gu(g, c), gu(u, c), d[:, :, c - 1].reshape(NE, P, 4096)]
    parts.append(d[:, :, EC - 1].reshape(NE, P, 4096))
    w_exp = np.empty((NE, 3 * EC, P, 4096), np.float32)
    for m, p_ in enumerate(parts):
        w_exp[:, m] = p_
    o["w_exp"] = w_exp
    return o
```
